# Optimizing a Trainium2 kernel written in Bass

```python
import math
import jax, jax.numpy as jnp
from jax import lax
import numpy as np

D_MODEL = 1024
BATCH = 1
SEQ = 256
DEPTH = 2
DEC_BATCH = 8
DEC_SEQ = 1
PAST_LEN = 2048
PAGE_SIZE = 128

EPS = 1e-6
N_EVEN = (DEPTH + 1) // 2
N_ODD = DEPTH // 2
MEM_LEN = 256
X_HEADS = 4
X_HEAD_DIM = D_MODEL // X_HEADS
A_CHUNK = 128
A_HEADS = 8
A_CH = D_MODEL
A_HEAD_DIM = A_CH // A_HEADS
B_INNER = D_MODEL
B_HEAD_DIM = 64
B_HEADS = B_INNER // B_HEAD_DIM
B_GROUPS = 2
B_HPG = B_HEADS // B_GROUPS
B_STATE = 128
B_CONV = 4
B_CONV_DIM = B_INNER + 2 * B_GROUPS * B_STATE
B_CHUNK = 128
IN0 = 2 * A_CH + B_INNER + B_CONV_DIM + B_HEADS
SPLIT0 = [A_CH, 2 * A_CH, 2 * A_CH + B_INNER, 2 * A_CH + B_INNER + B_CONV_DIM]
MIX0 = A_CH + B_INNER
C_KDIM = 128
C_HEADS = D_MODEL // C_KDIM
C_VDIM = D_MODEL // C_HEADS
C_CHUNK = 64
F_DENSE = 2816
N_EXPERTS = 8
TOP_K = 2
F_EXPERT = 3584

kernel_name = 'hybrid_gmlp_ssd_hgrn2_memxattn_step'

def rmsnorm(x, g):
    xf = x.astype(jnp.float32)
    y = xf * lax.rsqrt(jnp.mean(xf * xf, -1, keepdims=True) + EPS)
    return (y * g.astype(jnp.float32)).astype(x.dtype)

def group_rmsnorm(x, g, n_groups):
    shp = x.shape
    xf = x.astype(jnp.float32).reshape(shp[:-1] + (n_groups, shp[-1] // n_groups))
    y = (xf * lax.rsqrt(jnp.mean(xf * xf, -1, keepdims=True) + EPS)).reshape(shp)
    return (y * g.astype(jnp.float32)).astype(x.dtype)

def layernorm(x, g, b):
    xf = x.astype(jnp.float32)
    xc = xf - jnp.mean(xf, -1, keepdims=True)
    y = xc * lax.rsqrt(jnp.mean(xc * xc, -1, keepdims=True) + EPS)
    return (y * g.astype(jnp.float32) + b.astype(jnp.float32)).astype(x.dtype)

def chunk_spatial_gate(u, v, ws, bs):
    b, T = u.shape[:2]
    L = min(A_CHUNK, T)
    n = T // L
    mask = jnp.tril(jnp.ones((L, L), dtype=bool))
    w = jnp.where(mask, ws[:, :L, :L], 0.0).astype(v.dtype)
    vc = v.reshape(b, n, L, A_HEADS, A_HEAD_DIM)
    mix = jnp.einsum('hts,bnshd->bnthd', w, vc) + bs[:, :L].T.astype(v.dtype)[None, None, :, :, None]
    return u * mix.reshape(u.shape)

def causal_dwconv(x, prefix, w, bias):
    xp = jnp.concatenate([prefix.astype(x.dtype), x], axis=1)
    out = lax.conv_general_dilated(xp, w[:, None, :].astype(x.dtype), window_strides=(1,), padding='VALID',
                                   dimension_numbers=('NWC', 'WIO', 'NWC'), feature_group_count=x.shape[-1])
    return out + bias.astype(x.dtype), xp[:, -(B_CONV - 1):]

def ssd_scan(x, dt, a, bmat, cmat, s0):
    f32 = jnp.float32
    b, T = x.shape[:2]
    L = B_CHUNK if T % B_CHUNK == 0 else T
    n = T // L
    xg = x.astype(f32).reshape(b, n, L, B_GROUPS, B_HPG, B_HEAD_DIM)
    dtg = dt.reshape(b, n, L, B_GROUPS, B_HPG)
    xdt = xg * dtg[..., None]
    da = jnp.moveaxis(dtg * a.reshape(B_GROUPS, B_HPG), (3, 4), (1, 2))
    cs = jnp.cumsum(da, axis=-1)
    mask = jnp.tril(jnp.ones((L, L), dtype=bool))
    lmat = jnp.exp(jnp.where(mask, cs[..., :, None] - cs[..., None, :], -jnp.inf))
    Bc = bmat.astype(f32).reshape(b, n, L, B_GROUPS, B_STATE)
    Cc = cmat.astype(f32).reshape(b, n, L, B_GROUPS, B_STATE)
    y_diag = jnp.einsum('bclgn,bcsgn,bghcls,bcsghp->bclghp', Cc, Bc, lmat, xdt)
    decay = jnp.exp(cs[..., -1:] - cs)
    states = jnp.einsum('bclgn,bghcl,bclghp->bcghpn', Bc, decay, xdt)
    chunk_decay = jnp.exp(cs[..., -1])

    def step(s, inp):
        dec, st = inp
        return dec[..., None, None] * s + st, s

    s_final, prev = lax.scan(step, s0.astype(f32), (jnp.moveaxis(chunk_decay, -1, 0), jnp.moveaxis(states, 1, 0)))
    prev = jnp.moveaxis(prev, 0, 1)
    y_off = jnp.einsum('bclgn,bcghpn,bghcl->bclghp', Cc, prev, jnp.exp(cs))
    return (y_diag + y_off).reshape(b, T, B_HEADS, B_HEAD_DIM), s_final

def gla_chunked(q, k, v, logf, s0):
    b, T, H, K = q.shape
    V = v.shape[-1]
    L = C_CHUNK if T % C_CHUNK == 0 else T
    n = T // L
    q, k, v, logf = [t.reshape(b, n, L, H, t.shape[-1]) for t in (q, k, v, logf)]
    bc = jnp.cumsum(logf, axis=2)
    btot = bc[:, :, -1]
    q_in = q * jnp.exp(bc)
    k_in = k * jnp.exp(-bc)
    mask = jnp.tril(jnp.ones((L, L), dtype=bool))
    att = jnp.where(mask, jnp.einsum('bnthk,bnshk->bnhts', q_in, k_in), 0.0)
    o_intra = jnp.einsum('bnhts,bnshv->bnthv', att, v)
    upd = jnp.einsum('bnshk,bnshv->bnhkv', k * jnp.exp(btot[:, :, None] - bc), v)

    def step(s, inp):
        dec, u = inp
        return jnp.exp(dec)[..., None] * s + u, s

    s_final, prev = lax.scan(step, s0, (jnp.moveaxis(btot, 1, 0), jnp.moveaxis(upd, 1, 0)))
    prev = jnp.moveaxis(prev, 0, 1)
    o_inter = jnp.einsum('bnthk,bnhkv->bnthv', q_in, prev)
    return (o_intra + o_inter).reshape(b, T, H, V), s_final

def mixer_even(h, conv0, ssm0, w_in, a_ws, a_bs, a_ln_g, a_ln_b, conv_w, conv_b, dt_bias, a_log, d_skip, b_norm, w_out):
    f32 = jnp.float32
    b, T, _ = h.shape
    u, v, z, xbc, dt = jnp.split(h @ w_in, SPLIT0, axis=-1)
    u = jax.nn.gelu(u)
    v = layernorm(jax.nn.gelu(v), a_ln_g, a_ln_b)
    ya = chunk_spatial_gate(u.reshape(b, T, A_HEADS, A_HEAD_DIM), v.reshape(b, T, A_HEADS, A_HEAD_DIM), a_ws, a_bs)
    ya = ya.reshape(b, T, A_CH)
    xbc, conv_new = causal_dwconv(xbc, conv0, conv_w, conv_b)
    xbc = jax.nn.silu(xbc)
    xs, bm, cm = jnp.split(xbc, [B_INNER, B_INNER + B_GROUPS * B_STATE], axis=-1)
    dtf = jax.nn.softplus(dt.astype(f32) + dt_bias.astype(f32))
    a = -jnp.exp(a_log.astype(f32))
    xs4 = xs.reshape(b, T, B_HEADS, B_HEAD_DIM)
    y, ssm_new = ssd_scan(xs4, dtf, a, bm.reshape(b, T, B_GROUPS, B_STATE), cm.reshape(b, T, B_GROUPS, B_STATE), ssm0)
    y = (y + d_skip.astype(f32)[:, None] * xs4.astype(f32)).reshape(b, T, B_INNER).astype(h.dtype)
    yb = group_rmsnorm(y * jax.nn.silu(z), b_norm, B_GROUPS)
    out = jnp.concatenate([ya, yb], axis=-1) @ w_out
    return out, conv_new, ssm_new, v

def mixer_odd(h, s0, lb, w_in, c_norm, w_out):
    f32 = jnp.float32
    b, T, _ = h.shape
    q, f, i, g = jnp.split(h @ w_in, 4, axis=-1)
    fg = lb + (1.0 - lb) * jax.nn.sigmoid(f.astype(f32))
    qh = jax.nn.silu(q.astype(f32)).reshape(b, T, C_HEADS, C_KDIM)
    kh = (1.0 - fg).reshape(b, T, C_HEADS, C_KDIM)
    lf = jnp.log(fg).reshape(b, T, C_HEADS, C_KDIM)
    vh = i.astype(f32).reshape(b, T, C_HEADS, C_VDIM)
    o, s_new = gla_chunked(qh, kh, vh, lf, s0.astype(f32))
    o = group_rmsnorm(o.reshape(b, T, D_MODEL), c_norm, C_HEADS).astype(h.dtype) * jax.nn.silu(g)
    return o @ w_out, s_new

def mem_kv(mem, g, w):
    b = mem.shape[0]
    return (rmsnorm(mem, g) @ w).reshape(b, MEM_LEN, X_HEADS, X_HEAD_DIM)

def cross_attend(h, k, v, wq, wo):
    b, T, _ = h.shape
    q = (h @ wq).reshape(b, T, X_HEADS, X_HEAD_DIM)
    s = jnp.einsum('bthd,bmhd->bhtm', q, k.astype(q.dtype)).astype(jnp.float32) * (X_HEAD_DIM ** -0.5)
    p = jax.nn.softmax(s, axis=-1).astype(h.dtype)
    o = jnp.einsum('bhtm,bmhd->bthd', p, v.astype(h.dtype)).reshape(b, T, D_MODEL)
    return o @ wo

def swiglu(h, wg, wu, wd):
    return (jax.nn.silu(h @ wg) * (h @ wu)) @ wd

def moe_swiglu(h, router, wg, wu, wd):
    logits = (h @ router).astype(jnp.float32)
    top_v, top_i = lax.top_k(logits, TOP_K)
    w = jax.nn.softmax(top_v, axis=-1)
    gates = jnp.sum(jax.nn.one_hot(top_i, N_EXPERTS, dtype=jnp.float32) * w[..., None], axis=-2).astype(h.dtype)
    out = jnp.zeros_like(h)
    for e in range(N_EXPERTS):
        out = out + gates[..., e:e + 1] * swiglu(h, wg[e], wu[e], wd[e])
    return out

def _trunk(x, mem_k, mem_v, conv0, ssm0, hgrn0, lower_bounds, P):
    convs, ssms, hgrns, avs = [], [], [], []
    for l in range(DEPTH):
        j = l // 2
        h = rmsnorm(x, P['norm_mix_pre'][l])
        if l % 2 == 0:
            m, c_new, s_new, v_rows = mixer_even(
                h, conv0[j], ssm0[j], P['ev_w_in'][j], P['a_ws'][j], P['a_bs'][j], P['a_ln_g'][j], P['a_ln_b'][j],
                P['b_conv_w'][j], P['b_conv_b'][j], P['b_dt_bias'][j], P['b_a_log'][j], P['b_d'][j], P['b_norm'][j],
                P['ev_w_out'][j])
            convs.append(c_new)
            ssms.append(s_new)
            avs.append(v_rows)
        else:
            m, s_new = mixer_odd(h, hgrn0[j], lower_bounds[l], P['od_w_in'][j], P['c_norm'][j], P['od_w_out'][j])
            hgrns.append(s_new)
        x = x + rmsnorm(m, P['norm_mix_post'][l])
        h = rmsnorm(x, P['norm_x_pre'][l])
        x = x + rmsnorm(cross_attend(h, mem_k[l], mem_v[l], P['xa_wq'][l], P['xa_wo'][l]), P['norm_x_post'][l])
        h = rmsnorm(x, P['norm_ffn_pre'][l])
        if l % 2 == 0:
            f = swiglu(h, P['ffn_w_gate'][j], P['ffn_w_up'][j], P['ffn_w_down'][j])
        else:
            f = moe_swiglu(h, P['moe_router'][j], P['moe_w_gate'][j], P['moe_w_up'][j], P['moe_w_down'][j])
        x = x + rmsnorm(f, P['norm_ffn_post'][l])
    dt = x.dtype
    return x, jnp.stack(convs).astype(dt), jnp.stack(ssms).astype(dt), jnp.stack(hgrns).astype(dt), jnp.stack(avs).astype(dt)

def setup_inputs(seed: int = 0) -> dict:
    key = jax.random.key(seed)
    ks = iter(jax.random.split(key, 64))
    f32 = jnp.float32

    def nrm(shape, scale=1.0):
        return scale * jax.random.normal(next(ks), shape, f32)

    def gain(shape):
        return 1.0 + nrm(shape, 0.05)

    d = D_MODEL
    inp = {}
    inp['x_prompt'] = nrm((BATCH, SEQ, d))
    inp['x_sample'] = nrm((DEC_BATCH, DEC_SEQ, d))
    inp['mem_prompt'] = nrm((BATCH, MEM_LEN, d))
    inp['cache_mem_k'] = nrm((DEPTH, DEC_BATCH, MEM_LEN, X_HEADS, X_HEAD_DIM))
    inp['cache_mem_v'] = nrm((DEPTH, DEC_BATCH, MEM_LEN, X_HEADS, X_HEAD_DIM))
    inp['state_conv'] = nrm((N_EVEN, DEC_BATCH, B_CONV - 1, B_CONV_DIM))
    inp['state_ssm'] = nrm((N_EVEN, DEC_BATCH, B_GROUPS, B_HPG, B_HEAD_DIM, B_STATE), 0.3)
    inp['state_hgrn'] = nrm((N_ODD, DEC_BATCH, C_HEADS, C_KDIM, C_VDIM), 0.3)
    inp['norm_mix_pre'] = gain((DEPTH, d))
    inp['norm_mix_post'] = gain((DEPTH, d))
    inp['norm_x_pre'] = gain((DEPTH, d))
    inp['norm_x_post'] = gain((DEPTH, d))
    inp['norm_ffn_pre'] = gain((DEPTH, d))
    inp['norm_ffn_post'] = gain((DEPTH, d))
    inp['norm_mem'] = gain((DEPTH, d))
    inp['xa_wq'] = nrm((DEPTH, d, d), d ** -0.5)
    inp['xa_wk'] = nrm((DEPTH, d, d), d ** -0.5)
    inp['xa_wv'] = nrm((DEPTH, d, d), d ** -0.5)
    inp['xa_wo'] = nrm((DEPTH, d, d), d ** -0.5)
    inp['ev_w_in'] = nrm((N_EVEN, d, IN0), d ** -0.5)
    inp['a_ws'] = nrm((N_EVEN, A_HEADS, A_CHUNK, A_CHUNK), A_CHUNK ** -0.5)
    inp['a_bs'] = 1.0 + nrm((N_EVEN, A_HEADS, A_CHUNK), 0.1)
    inp['a_ln_g'] = gain((N_EVEN, A_CH))
    inp['a_ln_b'] = nrm((N_EVEN, A_CH), 0.02)
    inp['b_conv_w'] = nrm((N_EVEN, B_CONV, B_CONV_DIM), B_CONV ** -0.5)
    inp['b_conv_b'] = nrm((N_EVEN, B_CONV_DIM), 0.02)
    dt0 = jnp.exp(jax.random.uniform(next(ks), (N_EVEN, B_HEADS), f32, math.log(1e-3), math.log(1e-1)))
    inp['b_dt_bias'] = dt0 + jnp.log(-jnp.expm1(-dt0))
    inp['b_a_log'] = jnp.log(jax.random.uniform(next(ks), (N_EVEN, B_HEADS), f32, 1.0, 16.0))
    inp['b_d'] = gain((N_EVEN, B_HEADS))
    inp['b_norm'] = gain((N_EVEN, B_INNER))
    inp['ev_w_out'] = nrm((N_EVEN, MIX0, d), MIX0 ** -0.5)
    inp['ffn_w_gate'] = nrm((N_EVEN, d, F_DENSE), d ** -0.5)
    inp['ffn_w_up'] = nrm((N_EVEN, d, F_DENSE), d ** -0.5)
    inp['ffn_w_down'] = nrm((N_EVEN, F_DENSE, d), F_DENSE ** -0.5)
    inp['od_w_in'] = nrm((N_ODD, d, 4 * d), d ** -0.5)
    inp['hgrn_lb_logits'] = nrm((DEPTH, d), 0.02)
    inp['c_norm'] = gain((N_ODD, d))
    inp['od_w_out'] = nrm((N_ODD, d, d), d ** -0.5)
    inp['moe_router'] = nrm((N_ODD, d, N_EXPERTS), d ** -0.5)
    inp['moe_w_gate'] = nrm((N_ODD, N_EXPERTS, d, F_EXPERT), d ** -0.5)
    inp['moe_w_up'] = nrm((N_ODD, N_EXPERTS, d, F_EXPERT), d ** -0.5)
    inp['moe_w_down'] = nrm((N_ODD, N_EXPERTS, F_EXPERT, d), F_EXPERT ** -0.5)
    return inp

def reference(x_prompt, x_sample, mem_prompt, cache_mem_k, cache_mem_v, state_conv, state_ssm, state_hgrn,
              norm_mix_pre, norm_mix_post, norm_x_pre, norm_x_post, norm_ffn_pre, norm_ffn_post, norm_mem,
              xa_wq, xa_wk, xa_wv, xa_wo,
              ev_w_in, a_ws, a_bs, a_ln_g, a_ln_b, b_conv_w, b_conv_b, b_dt_bias, b_a_log, b_d, b_norm, ev_w_out,
              ffn_w_gate, ffn_w_up, ffn_w_down,
              od_w_in, hgrn_lb_logits, c_norm, od_w_out,
              moe_router, moe_w_gate, moe_w_up, moe_w_down):
    P = dict(norm_mix_pre=norm_mix_pre, norm_mix_post=norm_mix_post, norm_x_pre=norm_x_pre, norm_x_post=norm_x_post,
             norm_ffn_pre=norm_ffn_pre, norm_ffn_post=norm_ffn_post, xa_wq=xa_wq, xa_wo=xa_wo,
             ev_w_in=ev_w_in, a_ws=a_ws, a_bs=a_bs, a_ln_g=a_ln_g, a_ln_b=a_ln_b, b_conv_w=b_conv_w, b_conv_b=b_conv_b,
             b_dt_bias=b_dt_bias, b_a_log=b_a_log, b_d=b_d, b_norm=b_norm, ev_w_out=ev_w_out,
             ffn_w_gate=ffn_w_gate, ffn_w_up=ffn_w_up, ffn_w_down=ffn_w_down,
             od_w_in=od_w_in, c_norm=c_norm, od_w_out=od_w_out,
             moe_router=moe_router, moe_w_gate=moe_w_gate, moe_w_up=moe_w_up, moe_w_down=moe_w_down)
    lbp = jax.nn.softmax(hgrn_lb_logits.astype(jnp.float32), axis=0)
    lower_bounds = jnp.cumsum(lbp, axis=0) - lbp[0]

    bp = x_prompt.shape[0]
    dtp = x_prompt.dtype
    mem_k_prompt = jnp.stack([mem_kv(mem_prompt, norm_mem[l], xa_wk[l]) for l in range(DEPTH)])
    mem_v_prompt = jnp.stack([mem_kv(mem_prompt, norm_mem[l], xa_wv[l]) for l in range(DEPTH)])
    conv0 = jnp.zeros((N_EVEN, bp, B_CONV - 1, B_CONV_DIM), dtp)
    ssm0 = jnp.zeros((N_EVEN, bp, B_GROUPS, B_HPG, B_HEAD_DIM, B_STATE), dtp)
    hgrn0 = jnp.zeros((N_ODD, bp, C_HEADS, C_KDIM, C_VDIM), dtp)
    y_prompt, conv_prompt, ssm_prompt, hgrn_prompt, _ = _trunk(
        x_prompt, mem_k_prompt, mem_v_prompt, conv0, ssm0, hgrn0, lower_bounds, P)

    y_sample, conv_sample, ssm_sample, hgrn_sample, av_sample = _trunk(
        x_sample, cache_mem_k, cache_mem_v, state_conv, state_ssm, state_hgrn, lower_bounds, P)

    return (y_prompt, y_sample, mem_k_prompt, mem_v_prompt, conv_prompt, ssm_prompt, hgrn_prompt,
            conv_sample, ssm_sample, hgrn_sample, av_sample)


_drawn_inputs = setup_inputs


def setup_inputs(seed=0):
    import zlib

    import numpy as np

    out = dict(_drawn_inputs(seed))
    spreads = {}
    factors = {'hgrn_lb_logits': 3.452}
    for name, (base, spread) in spreads.items():
        noise = np.random.default_rng([zlib.crc32(name.encode()), seed]).standard_normal(out[name].shape)
        drawn = base * np.exp(spread * noise) if base else spread * noise
        out[name] = __import__('jax').numpy.asarray(drawn.astype(out[name].dtype))
    for name, factor in factors.items():
        out[name] = (out[name] * factor).astype(out[name].dtype)
    return out
```

```python
from contextlib import ExitStack

import concourse.bass as bass
from concourse import mybir

ALU = mybir.AluOpType
ACT = mybir.ActivationFunctionType
F32 = mybir.dt.float32
F32R = mybir.dt.float32r
U32 = mybir.dt.uint32
I32 = mybir.dt.int32
X = mybir.AxisListType.X

P = 128
D = 1024
DC = D // P
TP = 256
NB = 8
T = TP + NB
GROUPS = [(0, P), (P, P), (TP, NB)]
EPS = 1e-6
ARENA = 40912
MEM = 256
XH = 4
SSM_HEADS = 16
CONV_CH = 1536
CC = CONV_CH // P
FD = 2816
FC = FD // P
FGROUPS = [4, 4, 4, 4, 4, 2]
NE = 8
FE = 3584
SL = 512
NSL = FE // SL
KB = 4
BLK = KB * SL
RING = 2
MRING = 7
QF = BLK // 2
QRING = 4
ORDER = [("gate", 0), ("up", 0)]
for _s in range(1, NSL):
    ORDER += [("gate", _s), ("up", _s), ("down", _s - 1)]
ORDER += [("down", NSL - 1)]
QUARTERS = [(kind, s, i) for kind, s in ORDER for i in range(4)]
NQ = len(QUARTERS)
NBLK = NQ // 2
assert NBLK % MRING == 0 and NQ % QRING == 0
LAST = {(kind, s): q for q, (kind, s, i) in enumerate(QUARTERS) if i == 3}
TURN = {LAST["up", s + 1] - 2 if s + 1 < NSL else LAST["down", NSL - 2]: s for s in range(NSL)}
BIG = 1e30


def program(nc, a, o):
    with ExitStack() as ctx:
        ar = ctx.enter_context(nc.sbuf_tensor("arena", [P, ARENA], F32))
        wr_ = ctx.enter_context(nc.sbuf_tensor("weight_parts", [P, QRING, 2, QF], F32R))
        xr_ = ctx.enter_context(nc.sbuf_tensor("token_parts", [P, 4096], F32R))
        ps = ctx.enter_context(nc.psum_tensor("banks", [P, 8, 512], F32))
        made = {}

        def S(name):
            if name not in made:
                made[name] = ctx.enter_context(nc.semaphore(name))
            return made[name]

        def at(off, n, parts=P):
            return ar[0:parts, off:off + n]

        def split(ap, c):
            return ap.rearrange("p (c t) -> p c t", c=c)

        def slot(s):
            return at(s * BLK, BLK)

        SC = RING * BLK
        PERS = 28812
        pos = [PERS]

        def keep(n, parts=P):
            pos[0] += n
            assert pos[0] <= ARENA
            return at(pos[0] - n, n, parts)

        XT = split(keep(DC * T), DC)
        HT = split(keep(DC * T), DC)
        MT = split(keep(DC * T), DC)
        memh = split(keep(DC * MEM), DC)
        ident, ones, triu, tris, mneg, iota = (keep(P) for _ in range(6))
        onehot = split(keep(NB * P, NB), NB)
        head_of = keep(D, SSM_HEADS)
        bsr = ar[32:33, pos[0] - D:pos[0]]
        par = keep(220)
        rs = keep(T)
        small = keep(400)
        eps_c = small[:, 399:400]

        def gain(kind, layer, c):
            return par[:, kind * 16 + layer * 8 + c:kind * 16 + layer * 8 + c + 1]

        MIX_PRE, MIX_POST, X_PRE, X_POST, F_PRE, F_POST, MEM_G = range(7)
        LNG, LNB, BN, CN, LB, CB, CW = 112, 120, 128, 136, 144, 160, 172

        U = split(at(SC, 2112), DC)
        Z = split(at(SC + 2112, 2112), DC)
        UZ = split(at(SC, 4224), 16)
        V = split(at(SC + 4224, 2112), DC)
        raw = split(at(SC + 6336, CC * 259), CC)
        raws = at(SC + 9444, CC * 32).rearrange("p (c k b) -> p c k b", c=CC, k=4)
        XBC = split(at(SC + 9828, CC * T), CC)
        x_tm = split(at(SC + 12996, 2048), 2)
        b_tm = split(at(SC + 15044, 512), 2)
        bc_s = at(SC + 15556, 512, NB)
        CBT = split(at(SC + 16068, 512), 4)
        Lm = [at(SC + 16580 + 512 * i, 512) for i in range(2)]
        ecs = at(SC + 17604, 512)
        Ce = [at(SC + 18116 + 512 * i, 512) for i in range(2)]
        xw = at(SC + 19140, 1024)
        prev = at(SC + 20164, 1024)
        s0 = [split(at(SC + 21188 + 1024 * i, 1024), DC) for i in range(2)]
        t2 = split(at(SC + 23236, 1024), DC)
        conv_tail = at(SC + 24260, CC * 11)
        conv_o = at(SC + 2112, CONV_CH, 11)
        xin = at(SC, 3072).rearrange("p (g n) -> p g n", g=3)
        av_o = at(SC + 6336, D, NB)
        sfin = at(SC + 7360, 1024)
        ssm_o = split(at(SC + 8384, 1024), DC)
        v_tm = at(PERS + 2 * 2112, 2048).rearrange("p (g n) -> p g n", g=2)
        ws = at(PERS + 3 * 2112, 1024)
        wsT = split(at(PERS + 3 * 2112 + 1024, 1024), DC)
        par_in = [at(SC + 4000, P, 112), at(SC + 4128, P, 108)]
        st_in = at(SC + 4256, CONV_CH, 24)
        dcol = small[:, 0:8]
        dtb, alog = small[0:16, 8:9], small[0:16, 9:10]
        aexp = small[0:16, 10:11]
        mrs = small[:, 16:20]
        lb1, omlb = small[:, 24:32], small[:, 32:40]
        wb = small[:, 40:56]
        dd = small[:, 64:128].rearrange("p (j i h) -> p j i h", j=2, i=2)
        cs = small[:, 128:160].rearrange("p (j h) -> p j h", j=2)
        wdec = small[:, 160:192].rearrange("p (j h) -> p j h", j=2)
        cdec = small[:, 192:224].rearrange("p (j h) -> p j h", j=2)
        exc = small[:, 224:352].rearrange("p (c k) -> p c k", c=DC)
        exd = small[0:16, 352:368]
        rsg = split(at(SC + 16580, 2 * T), 2)
        ysum = split(at(SC + 24392, 64), DC)
        dtr = [at(SC + 18116 + T * i, T, 16) for i in range(7)]

        QT = split(at(SC, 2112), DC)
        OT = split(at(SC + 2112, 2112), DC)
        MG = split(at(SC + 4224, 2048), DC)
        k_tm = at(SC + 6272, 2048).rearrange("p (m n) -> p m n", m=2)
        vm_tm = at(SC + 8320, 2048).rearrange("p (m n) -> p m n", m=2)
        KT = split(at(SC + 10368, 2048), DC)
        PR = at(SC + 12416, 2048).rearrange("p (g h m) -> p g h m", g=2, h=XH)
        PT = at(SC + 14464, 2048).rearrange("p (h m t) -> p h m t", h=XH, m=2)
        kc = [at(SC + 16512 + 2048 * i, 2048).rearrange("p (m n) -> p m n", m=2) for i in range(2)]
        vc = [at(SC + 20608 + 2048 * i, 2048).rearrange("p (m n) -> p m n", m=2) for i in range(2)]
        mem_in = at(SC + 4224, 2048).rearrange("p (m n) -> p m n", m=2)
        q_s = at(SC + 12416, D, NB)
        junk = at(SC + 13440, 256)
        scs = small[:, 64:128].rearrange("p (m k) -> p m k", m=2)
        mx, sm = small[:, 128:136], small[:, 136:144]
        smx, ssm = small[0:32, 144:145], small[0:32, 145:146]
        p_s = at(SC + 13696, 256, 32)
        pts = small[:, 160:224].rearrange("p (m k) -> p m k", m=2)

        hid = split(at(SC, FC * T), FC)
        gtmp = [at(SC + 6000 + T * i, T) for i in range(4)]

        Q, Fg, I, G, K, E, BC = (split(at(SC + 2112 * i, 2112), DC) for i in range(7))
        cmask = MT
        kp_tm = at(PERS + 2 * 2112, 2048).rearrange("p (g n) -> p g n", g=2)
        i_tm = at(SC + 14784, 2048).rearrange("p (g n) -> p g n", g=2)
        att = at(SC + 16832, 2048).rearrange("p (h j t) -> p h j t", h=8, j=2)
        st = [split(at(SC + 18880 + 1024 * i, 1024), DC) for i in range(4)]
        tsc = split(at(SC + 22976, 512), 4)
        i_s = at(SC + 23488, D, NB)
        etot = small[:, 64:96].rearrange("p (c k) -> p c k", c=DC)
        es = small[:, 96:160].rearrange("p (c k) -> p c k", c=DC)

        ME = SC + 12288
        h_tok = at(ME, 3072).rearrange("p (g n) -> p g n", g=3)
        acc = at(ME + 3072, 3072).rearrange("p (g n) -> p g n", g=3)
        xe_hi, xe_lo = (xr_[:, i * 1024:(i + 1) * 1024] for i in range(2))
        hT_hi, hT_lo = ([xr_[:, 2048 + (2 * b + i) * 512:2560 + (2 * b + i) * 512] for b in range(2)] for i in range(2))
        sg = [at(ME + 7168 + 512 * i, 512) for i in range(2)]
        hs = [at(ME + 8192 + 512 * i, 512) for i in range(2)]

        pick = split(at(ME + 10240, 384), 3)
        pickg = split(at(ME + 10624, 384), 3)
        pickT = at(ME + 11008, T)
        oe = at(ME + 11272, D)

        def quarter(q):
            return slot(q // 2 % MRING)[:, (q % 2) * QF:(q % 2 + 1) * QF]

        wr = split(small[:, 0:64], DC)
        x_tok = at(0, 3072).rearrange("p (g n) -> p g n", g=3)
        gb = at(3072, D)
        ysq = at(4096, D)
        rtf = at(PERS + 2112, 2112)
        lg = split(rtf[:, 0:24], 3)
        top = split(rtf[:, 24:48], 3)
        topi = split(rtf[:, 48:72].bitcast(U32), 3)
        topf = split(rtf[:, 72:96], 3)
        tw = split(rtf[:, 96:108], 3)
        oh = split(rtf[:, 108:156], 6)
        msk = split(rtf[:, 156:180], 3)
        gat = split(rtf[:, 180:204], 3)
        posn = split(rtf[:, 204:228], 3)
        table = rtf[:, 228:300].rearrange("p (e k) -> p e k", e=NE)
        cur = rtf[:, 300:309]
        cnt = rtf[:, 309:317]
        cmx = rtf[:, 317:320]
        rounds = rtf[:, 320:321]
        rounds_i = rtf[:, 321:322].bitcast(I32)
        frs = rtf[:, 324:330]

        tiles, first = [], {}

        def plan(name, n, who="a"):
            first[name] = len(tiles)
            tiles.extend(who[i % len(who)] for i in range(n))

        plan("par", 1, "v"), plan("st", 1, "v"), plan("xT", DC)
        plan("xbc", CC), plan("dt", 1, "v"), plan("v", 8), plan("tr0", 9), plan("cb", 1)
        plan("z", 8), plan("vmean", 1, "v")
        plan("csB", 6, "v"), plan("stA", 4, "v"), plan("csC", 2, "v"), plan("sfT", 2)
        plan("u", 8), plan("bcs", 8, "v"), plan("vvar", 1), plan("vtm", 4), plan("avT", 2), plan("wsT", 2, "v")
        plan("mixA", 8, "v"), plan("gate", 2)
        plan("out0", 8)
        for l in range(2):
            if l == 0:
                plan("memT", 8)
            plan(f"k{l}", 4), plan(f"kT{l}", 8), plan(f"q{l}", 8), plan(f"vm{l}", 4)
            plan(f"qs{l}", 2), plan(f"qB{l}", 16, "v"), plan(f"sT{l}", 1), plan(f"pTs{l}", 1, "v")
            plan(f"sc{l}", 4), plan(f"pT{l}", 4), plan(f"pv{l}", 8), plan(f"xo{l}", 8)
            if l == 0:
                for i, n in enumerate(FGROUPS):
                    plan(f"gate{i}", n), plan(f"up{i}", n, "v")
                plan("down", 8)
                plan("f", 8), plan("q", 8), plan("i", 8), plan("g", 8)
                plan("iT", 4), plan("isT", 2), plan("kT", 4), plan("att", 2, "v")
                plan("upd", 8, "v"), plan("ho", 8), plan("vB", 16, "v"), plan("hn", 8)
                plan("out1", 8)
        plan("htok", 6), plan("logit", 1, "v"), plan("posn", 1, "v")

        def n_of(name, i=0):
            return first[name] + i

        def n_csb(i):
            return n_of("csB", i) if i < 6 else n_of("csC", i - 6)

        def bank(n):
            return ps[:, n % 4, :]

        def emptied(n):
            return tiles[n], sum(w == tiles[n] for w in tiles[:n + 1])

        empty = {"a": S("tile_emptied_by_act"), "v": S("tile_emptied_by_dve")}
        tile_done = S("tile_done")
        part_used = S("block_part_used")

        blocks = []
        parts = [0]

        def weights(name, w, tile_w=P, tiles_per=None, koff=0):
            k, n = w.shape
            t = first[name]
            for c0 in range(0, n, SL):
                cols = min(SL, n - c0)
                nt = (cols + P - 1) // P if tiles_per is None else tiles_per
                for k0 in range(0, k, KB * P):
                    rows = min(KB * P, k - k0)
                    src = w[k0:k0 + rows, c0:c0 + cols].rearrange("(k p) n -> p k n", p=P)
                    if k0 + rows == k:
                        t += nt
                        blocks.append((src, rows // P, cols, (tile_done, t)))
                    else:
                        parts[0] += 1
                        blocks.append((src, rows // P, cols, (part_used, parts[0])))

        w0, fg_, fu_ = a["ev_w_in"][0], a["ffn_w_gate"][0], a["ffn_w_up"][0]
        weights("xbc", w0[:, 3072:4608])
        weights("dt", w0[:, 4608:4624])
        weights("v", w0[:, 1024:2048])
        weights("z", w0[:, 2048:3072])
        weights("u", w0[:, 0:1024])
        weights("out0", a["ev_w_out"][0])
        for l in range(2):
            weights(f"k{l}", a["xa_wk"][l], tiles_per=2)
            weights(f"q{l}", a["xa_wq"][l])
            weights(f"vm{l}", a["xa_wv"][l], tiles_per=2)
            weights(f"xo{l}", a["xa_wo"][l])
            if l == 0:
                for i, n in enumerate(FGROUPS):
                    weights(f"gate{i}", fg_[:, i * SL:i * SL + n * P])
                    weights(f"up{i}", fu_[:, i * SL:i * SL + n * P])
                weights("down", a["ffn_w_down"][0])
                wi = a["od_w_in"][0]
                weights("f", wi[:, 1024:2048])
                weights("q", wi[:, 0:1024])
                weights("i", wi[:, 2048:3072])
                weights("g", wi[:, 3072:4096])
                weights("out1", a["od_w_out"][0])
        loaded = [S(f"slot{s}_loaded") for s in range(RING)]
        mloaded = [S(f"expert_slot{s}_loaded") for s in range(MRING)]

        NORMS = [(MIX_PRE, 0, 1), (MIX_POST, 0, 0), (X_PRE, 0, 1), (X_POST, 0, 0), (F_PRE, 0, 1),
                 (F_POST, 0, 0), (MIX_PRE, 1, 1), (MIX_POST, 1, 0), (X_PRE, 1, 1), (X_POST, 1, 0),
                 (F_PRE, 1, 1)]
        posts = [n for n, (_, _, pre) in enumerate(NORMS) if not pre]

        block = ctx.enter_context(nc.Block())

        @block.sync
        def _(sp):
            nc.sync.dma_start(xin[:, 0:2, :], a["x_prompt"][0].rearrange("(g p) n -> p g n", p=P)) \
                .then_inc(S("x_loaded"), 16)
            nc.sync.dma_start(xin[0:NB, 2, :], a["x_sample"][:, 0, :]).then_inc(S("x_loaded"), 16)
            names = ["norm_mix_pre", "norm_mix_post", "norm_x_pre", "norm_x_post", "norm_ffn_pre",
                     "norm_ffn_post", "norm_mem"]
            for i, name in enumerate(names):
                nc.sync.dma_start(par_in[0][i * 16:i * 16 + 16, :], a[name].rearrange("l (c p) -> (l c) p", p=P)) \
                    .then_inc(S("par_loaded"), 16)
            r = 0
            for name in ("a_ln_g", "a_ln_b", "b_norm", "c_norm", "hgrn_lb_logits", "b_conv_b"):
                v = a[name].rearrange("l (c p) -> (l c) p", p=P)
                nc.sync.dma_start(par_in[1][r:r + v.shape[0], :], v).then_inc(S("par_loaded"), 16)
                r += v.shape[0]
            nc.sync.dma_start(par_in[1][r:r + 48, :], a["b_conv_w"][0].rearrange("k (c p) -> (k c) p", p=P)) \
                .then_inc(S("par_loaded"), 16)
            nc.sync.dma_start(st_in, a["state_conv"][0].rearrange("b k n -> (b k) n")).then_inc(S("st_loaded"), 16)
            for b, (src, kc_, cols, _) in enumerate(blocks):
                if b >= RING:
                    sem, value = blocks[b - RING][3]
                    sp.wait_ge(sem, value)
                dst = split(slot(b % RING)[:, 0:kc_ * cols], kc_)
                nc.sync.dma_start(dst, src).then_inc(loaded[b % RING], 16)
                if b == 8:
                    nc.sync.dma_start(bsr, a["a_bs"].rearrange("o h t -> o (h t)")).then_inc(S("bs_loaded"), 16)
                    nc.sync.dma_start(ws.rearrange("p (h s) -> p h s", h=8), a["a_ws"][0].rearrange("h t s -> t h s")) \
                        .then_inc(S("ws_loaded"), 16)
            for b in range(len(blocks) - RING, len(blocks)):
                sem, value = blocks[b][3]
                sp.wait_ge(sem, value)
            sp.wait_ge(S("experts_may_start"), 1)
            sp.wait_ge(S("rounds_ready"), 1)
            rounds_v = nc.values_load(rounds_i[0:1, 0:1], engines=[mybir.EngineType.SP], min_val=1, max_val=3)
            with sp.Fori(0, rounds_v) as r:
                with sp.Fori(0, NE) as e:
                    it = sp.snap(r * NE + e)
                    for j in range(NBLK):
                        kind, s, i = QUARTERS[2 * j]
                        sp.wait_ge(S("lo_made"), it * NQ + 2 * j + 2)
                        if kind == "down":
                            src = a["moe_w_down"][0, bass.ds(e, 1), s * SL + i * P:s * SL + (i + 2) * P, :]
                        else:
                            w = a["moe_w_gate"] if kind == "gate" else a["moe_w_up"]
                            src = w[0, bass.ds(e, 1), 2 * i * P:2 * (i + 2) * P, s * SL:(s + 1) * SL]
                        rows = 2 if kind == "down" else KB
                        nc.sync.dma_start(split(slot(j % MRING), rows), src.rearrange("o (k p) n -> p (o k) n", p=P)) \
                            .then_inc(mloaded[j % MRING], 16)

        @block.gpsimd
        def _(pool):
            g = nc.gpsimd
            made_ = [0]

            def link(ins):
                made_[0] += 1
                ins.then_inc(S("pool_step"), 1)
                pool.wait_ge(S("pool_step"), made_[0])

            for t in (ident, ones, triu, tris, mneg):
                g.memset(t, 1.0 if t is ones or t is triu or t is tris else 0.0)
            g.memset(onehot, 0.0)
            g.memset(head_of, 1.0)
            link(g.memset(raw[:, :, 0:3], 0.0))
            link(g.affine_select(out=ident, in_=ident, compare_op=ALU.not_equal, fill=1.0, base=0,
                                 pattern=[[-1, P]], channel_multiplier=1))
            g.affine_select(out=triu, in_=triu, compare_op=ALU.is_ge, fill=0.0, base=0,
                            pattern=[[1, P]], channel_multiplier=-1)
            g.affine_select(out=tris, in_=tris, compare_op=ALU.is_gt, fill=0.0, base=0,
                            pattern=[[1, P]], channel_multiplier=-1)
            g.affine_select(out=mneg, in_=mneg, compare_op=ALU.is_ge, fill=-BIG, base=0,
                            pattern=[[1, P]], channel_multiplier=-1)
            g.iota(iota, pattern=[[1, P]], base=0, channel_multiplier=0, allow_small_or_imprecise_dtypes=True)
            g.affine_select(out=onehot, in_=onehot, compare_op=ALU.not_equal, fill=1.0, base=0,
                            pattern=[[-1, NB], [0, P]], channel_multiplier=1)
            link(g.affine_select(out=head_of, in_=head_of, compare_op=ALU.is_ge, fill=0.0, base=0,
                                 pattern=[[1, D]], channel_multiplier=-64))
            g.affine_select(out=head_of, in_=head_of, compare_op=ALU.is_ge, fill=0.0, base=63,
                            pattern=[[-1, D]], channel_multiplier=64).then_inc(S("consts_ready"), 1)
            for j in range(2):
                g.dma_start(dcol[64 * j:64 * j + 64, :],
                            a["b_d"][0:1, :].rearrange("o (c j) -> o j c", j=2)[:, j, :].broadcast_to([64, 8]),
                            allow_slow_non_contiguous=True) \
                    .then_inc(S("small_loaded"), 16)
            g.dma_start(dtb, a["b_dt_bias"].rearrange("o h -> h o"), allow_slow_non_contiguous=True).then_inc(S("small_loaded"), 16)
            g.dma_start(alog, a["b_a_log"].rearrange("o h -> h o"), allow_slow_non_contiguous=True).then_inc(S("small_loaded"), 16)
            g.dma_start(o["conv_sample"][0][:, 0:2, :], a["state_conv"][0][:, 1:3, :]).then_inc(S("stored"), 16)

            ssm_in = a["state_ssm"][0].rearrange("b g h p n -> b (g h p) n")
            ssm_out = o["ssm_sample"][0].rearrange("b g h p n -> b (g h p) n")

            def load_s0(b):
                if b >= 2:
                    pool.wait_ge(S("s0_stored"), 16 * (b - 1))
                g.dma_start(s0[b % 2], ssm_in[b].rearrange("(c p) n -> p c n", p=P)).then_inc(S(f"s0_loaded{b % 2}"), 16)

            load_s0(0)
            load_s0(1)
            pool.wait_ge(empty["a"], emptied(n_of("tr0", 2))[1])
            g.dma_start(o["conv_prompt"][0, 0], conv_o[0:3, :]).then_inc(S("conv_stored"), 16)
            g.dma_start(o["conv_sample"][0][:, 2, :], conv_o[3:11, :]).then_inc(S("conv_stored"), 16)
            pool.wait_ge(S("exc_ready"), 1)
            for b in range(NB):
                pool.wait_ge(S(f"s0_loaded{b % 2}"), 16 * (b // 2 + 1))
                g.tensor_tensor(s0[b % 2], s0[b % 2], exc[:, :, b:b + 1].broadcast_to([P, DC, P]), ALU.mult) \
                    .then_inc(S("s0_decayed"), 1)
                pool.wait_ge(S("s0_used"), b + 1)
                g.dma_start(ssm_out[b].rearrange("(c p) n -> p c n", p=P), s0[b % 2]).then_inc(S("s0_stored"), 16)
                if b + 2 < NB:
                    load_s0(b + 2)
            pool.wait_ge(empty["a"], emptied(n_of("sfT", 1))[1])
            g.dma_start(o["ssm_prompt"][0, 0].rearrange("g h p n -> (g h p) n").rearrange("(c p) n -> p c n", p=P),
                        ssm_o).then_inc(S("stored"), 16)
            pool.wait_ge(empty["a"], emptied(n_of("avT", 1))[1])
            g.dma_start(o["av_sample"][0][:, 0, :], av_o).then_inc(S("stored"), 16)

            for l in range(2):
                if l == 0:
                    pool.wait_ge(tile_done, n_of("out0", 7) + 1)
                    g.dma_start(mem_in, a["mem_prompt"][0].rearrange("(m p) n -> p m n", p=P)) \
                        .then_inc(S("mem_loaded"), 16)
                    pool.wait_ge(S("stored"), 48)
                    pool.wait_ge(S("s0_stored"), 128)
                else:
                    pool.wait_ge(tile_done, n_of("out1", 7) + 1)
                    pool.wait_ge(S("hgrn_stored"), 16 * 9)

                def load_k(b):
                    if b >= 2:
                        pool.wait_ge(S("k_cache_used"), NB * l + b - 1)
                    g.dma_start(kc[b % 2], a["cache_mem_k"][l, b].rearrange("(m p) h d -> p m (h d)", p=P)) \
                        .then_inc(S(f"k_cache_loaded{b % 2}"), 16)

                def load_v(b):
                    if b >= 2:
                        pool.wait_ge(S("v_cache_used"), NB * l + b - 1)
                    g.dma_start(vc[b % 2], a["cache_mem_v"][l, b].rearrange("(m p) h d -> p m (h d)", p=P)) \
                        .then_inc(S(f"v_cache_loaded{b % 2}"), 16)

                load_k(0), load_k(1), load_v(0), load_v(1)
                pool.wait_ge(empty["a"], emptied(n_of("memT", 7))[1])
                for c in range(DC):
                    last = g.tensor_scalar(MG[:, c, :], memh[:, c, :], gain(MEM_G, l, c), None, ALU.mult)
                last.then_inc(S("mem_gain_ready"), 1)
                pool.wait_ge(empty["a"], emptied(n_of(f"k{l}", 3))[1])
                g.dma_start(o["mem_k"][l, 0].rearrange("(m p) h d -> p m (h d)", p=P), k_tm).then_inc(S("kv_stored"), 16)
                pool.wait_ge(empty["a"], emptied(n_of(f"vm{l}", 3))[1])
                g.dma_start(o["mem_v"][l, 0].rearrange("(m p) h d -> p m (h d)", p=P), vm_tm).then_inc(S("kv_stored"), 16)
                for b in range(2, NB):
                    load_k(b)
                for b in range(2, NB):
                    load_v(b)
                if l == 0:
                    pool.wait_ge(S("square_sums_done"), 7)
                    g.memset(cmask, 1.0)
                    pool.wait_ge(tile_done, n_of("down", 7) + 1)
                    pool.wait_ge(S("kv_stored"), 32)
                    link(g.memset(att, 0.0))
                    g.memset(cmask[:, :, 0:TP:64], 0.0)
                    g.memset(cmask[:, :, TP:T], 0.0).then_inc(S("hgrn_consts"), 1)
                    pool.wait_ge(S("s4_ready"), 1)
                    g.dma_start(o["hgrn_prompt"][0, 0].rearrange("h k v -> k h v"), st[3]).then_inc(S("hgrn_stored"), 16)
                    pool.wait_ge(tile_done, n_of("ho", 7) + 1)

                    def load_h(b):
                        if b >= 3:
                            pool.wait_ge(S("hgrn_stored"), 16 * (b - 1))
                            pool.wait_ge(S("hgrn_read"), b - 2)
                        g.dma_start(st[b % 3], a["state_hgrn"][0, b].rearrange("h k v -> k h v")) \
                            .then_inc(S(f"h0_loaded{b % 3}"), 16)

                    load_h(0), load_h(1), load_h(2)
                    for b in range(NB):
                        pool.wait_ge(S(f"h0_loaded{b % 3}"), 16 * (b // 3 + 1))
                        g.tensor_tensor(st[b % 3], st[b % 3], es[:, :, b:b + 1].broadcast_to([P, DC, P]), ALU.mult) \
                            .then_inc(S("h0_decayed"), 1)
                        pool.wait_ge(S("h_updated"), b + 1)
                        g.dma_start(o["hgrn_sample"][0, b].rearrange("h k v -> k h v"), st[b % 3]) \
                            .then_inc(S("hgrn_stored"), 16)
                        if b + 3 < NB:
                            load_h(b + 3)
            pool.wait_ge(tile_done, n_of("xo1", 7) + 1)
            pool.wait_ge(S("kv_stored"), 64)
            g.dma_start(wr, a["moe_router"][0].rearrange("(k p) e -> p k e", p=P)).then_inc(S("router_loaded"), 16)
            g.memset(acc, 0.0)
            g.memset(pick, 0.0)
            g.memset(h_tok[:, 2, :], 0.0).then_inc(S("experts_may_start"), 1)
            pool.wait_ge(S("experts_done"), 1)
            g.dma_start(gb, a["norm_ffn_post"][1:2, :].broadcast_to([P, D])).then_inc(S("gb_loaded"), 16)
            pool.wait_ge(S("y_ready"), 3)
            g.dma_start(o["y_prompt"][0].rearrange("(g p) n -> p g n", p=P), acc[:, 0:2, :]).then_inc(S("stored"), 16)
            g.dma_start(o["y_sample"][:, 0, :], acc[0:NB, 2, :]).then_inc(S("stored"), 16)
            pool.wait_ge(S("conv_stored"), 32)
            pool.wait_ge(S("s0_stored"), 128)
            pool.wait_ge(S("kv_stored"), 64)
            pool.wait_ge(S("hgrn_stored"), 16 * 9)
            pool.wait_ge(S("stored"), 16 * 5)

        @block.tensor
        def _(pe):
            mm, tr = nc.tensor.matmul, nc.tensor.transpose
            at_block = [0]

            def take(n):
                if n >= 4:
                    who, count = emptied(n - 4)
                    pe.wait_ge(empty[who], count)
                return bank(n)

            def next_block():
                b = at_block[0]
                at_block[0] += 1
                pe.wait_ge(loaded[b % RING], 16 * (b // RING + 1))
                _, kc_, cols, _ = blocks[b]
                return split(slot(b % RING)[:, 0:kc_ * cols], kc_)

            def project(name, rhs, kchunks, cols):
                n = n_of(name)
                for c0 in range(0, cols, SL):
                    width = min(SL, cols - c0)
                    nt = (width + P - 1) // P
                    for k0 in range(0, kchunks, KB):
                        w = next_block()
                        ks = min(KB, kchunks - k0)
                        for i in range(nt):
                            m = min(P, width - i * P)
                            b = take(n + i) if k0 == 0 else bank(n + i)
                            for k in range(ks):
                                last = mm(b[0:m, 0:T], w[:, k, i * P:i * P + m], rhs[:, k0 + k, :],
                                          start=(k0 + k == 0), stop=(k0 + k == kchunks - 1))
                            if k0 + ks == kchunks:
                                last.then_inc(tile_done, 1)
                        if k0 + ks < kchunks:
                            last.then_inc(part_used, 1)
                    n += nt

            def project_tm(name, lhs):
                n = n_of(name)
                for c0 in range(0, D, SL):
                    for k0 in range(0, DC, KB):
                        w = next_block()
                        for m in range(2):
                            b = take(n + m) if k0 == 0 else bank(n + m)
                            for k in range(KB):
                                last = mm(b, lhs[:, k0 + k, m * P:(m + 1) * P], w[:, k, :], start=(k0 + k == 0),
                                          stop=(k0 + k == DC - 1))
                            if k0 + KB == DC:
                                last.then_inc(tile_done, 1)
                        if k0 + KB < DC:
                            last.then_inc(part_used, 1)
                    n += 2

            def transposes(n, items):
                b = take(n)
                col = 0
                for src, p_, f_ in items:
                    last = tr(b[0:f_, col:col + p_], src, ident[0:p_, 0:p_])
                    col += p_
                last.then_inc(tile_done, 1)

            def square_sums(k):
                for c in range(DC):
                    pe.wait_ge(S("squares_ready"), DC * k + c + 1)
                    sq = MT if NORMS[k][2] else HT
                    last = mm(ps[:, 4, 0:T], ones, sq[:, c, :], start=(c == 0), stop=(c == DC - 1))
                last.then_inc(S("square_sums_done"), 1)

            def wait_norm(k):
                pe.wait_ge(S("normed"), [i for i, x in enumerate(NORMS) if x[2]].index(k) + 1)

            pe.wait_ge(S("consts_ready"), 1)
            pe.wait_ge(S("par_loaded"), 16 * 14)
            transposes(n_of("par"), [(par_in[0], 112, P), (par_in[1], 108, P)])
            pe.wait_ge(S("st_loaded"), 16)
            transposes(n_of("st"), [(st_in[:, c * P:(c + 1) * P], 24, P) for c in range(CC)])
            pe.wait_ge(S("x_loaded"), 32)
            for c in range(DC):
                transposes(n_of("xT", c), [(xin[0:n, g, c * P:(c + 1) * P], n, P)
                                           for g, (_, n) in enumerate(GROUPS)])
            square_sums(0)
            wait_norm(0)
            project("xbc", HT, DC, CONV_CH)
            project("dt", HT, DC, 16)
            project("v", HT, DC, D)
            n = n_of("tr0")
            for i in range(3):
                pe.wait_ge(S("tail_ready"), 1)
                b = take(n + i)
                for c in range(4):
                    last = tr(b[0:11, c * P:(c + 1) * P], conv_tail[:, (4 * i + c) * 11:(4 * i + c + 1) * 11], ident)
                last.then_inc(tile_done, 1)
            n += 3
            pe.wait_ge(S("xbc_ready"), CC)
            for j in range(2):
                for half in range(2):
                    b = take(n)
                    for c in range(4):
                        last = tr(b[:, c * P:(c + 1) * P], XBC[:, 4 * half + c, j * P:(j + 1) * P], ident)
                    last.then_inc(tile_done, 1)
                    n += 1
            b = take(n)
            for j in range(2):
                for g in range(2):
                    last = tr(b[:, (2 * j + g) * P:(2 * j + g + 1) * P], XBC[:, 8 + g, j * P:(j + 1) * P], ident)
            last.then_inc(tile_done, 1)
            n += 1
            b = take(n)
            for c in range(4):
                last = tr(b[0:NB, c * P:(c + 1) * P], XBC[:, 8 + c, TP:T], ident)
            last.then_inc(tile_done, 1)
            b = take(n_of("cb"))
            for j in range(2):
                for g in range(2):
                    last = mm(b[:, (2 * j + g) * P:(2 * j + g + 1) * P], XBC[:, 8 + g, j * P:(j + 1) * P],
                              XBC[:, 10 + g, j * P:(j + 1) * P], start=True, stop=True)
            last.then_inc(tile_done, 1)
            pe.wait_ge(S("dt_ready"), 1)
            for j in range(2):
                for i in range(2):
                    tr(ps[:, 5, (2 * j + i) * 16:(2 * j + i) * 16 + 16], dtr[i][:, j * P:(j + 1) * P], ident[0:16, 0:16])
            for c in range(DC):
                last = mm(ps[:, 5, 128 + 16 * c:144 + 16 * c], head_of[:, c * P:(c + 1) * P], exd, start=True, stop=True)
            last.then_inc(S("dt_tm_done"), 1)
            project("z", HT, DC, D)
            b = take(n_of("vmean"))
            pe.wait_ge(empty["a"], emptied(n_of("v", 7))[1])
            for c in range(DC):
                last = mm(b[:, 0:T], ones, V[:, c, :], start=(c == 0), stop=(c == DC - 1))
            last.then_inc(tile_done, 1)
            pe.wait_ge(S("dt_tm_ready"), 1)
            for j in range(2):
                mm(ps[:, 6, 16 * j:16 * j + 16], triu, dd[:, j, 1, :], start=True, stop=True)
                last = mm(ps[:, 6, 32 + 16 * j:48 + 16 * j], ones, dd[:, j, 1, :], start=True, stop=True)
            last.then_inc(S("cs_done"), 1)

            def csb(i):
                j, hq = i // 4, i % 4
                b = take(n_csb(i))
                for h in range(4):
                    last = mm(b[:, h * P:(h + 1) * P], dd[:, j, 1, 4 * hq + h:4 * hq + h + 1].broadcast_to([P, P]), triu,
                              start=True, stop=True)
                last.then_inc(tile_done, 1)

            def ssd(i):
                j, hq = i // 4, i % 4
                y = ps[:, 5 + 2 * (i % 2), 0:256]
                pe.wait_ge(S("lmat_ready"), i + 1)
                if i >= 2:
                    pe.wait_ge(S("y_ssd_used"), i - 1)
                for h in range(4):
                    r0, c0 = 64 * (h % 2), P * (h // 2)
                    hh = 4 * hq + h
                    last = mm(y[r0:r0 + 64, c0:c0 + P], x_tm[:, j, 64 * hh:64 * hh + 64], Lm[i % 2][:, h * P:(h + 1) * P],
                              start=True, stop=(j == 0))
                    if j:
                        last = mm(y[r0:r0 + 64, c0:c0 + P], prev[:, 64 * hh:64 * hh + 64], Ce[i % 2][:, h * P:(h + 1) * P],
                                  start=False, stop=True)
                last.then_inc(S("y_ssd_done"), 1)

            csb(0), csb(1)
            for i in range(4):
                ssd(i)
                csb(i + 2)
            for j in range(2):
                pe.wait_ge(S("xw_ready"), j + 1)
                for g in range(2):
                    b = take(n_of("stA", 2 * j + g))
                    mm(b, b_tm[:, j, g * P:(g + 1) * P], xw[:, g * 512:(g + 1) * 512], start=True, stop=True) \
                        .then_inc(tile_done, 1)
            pe.wait_ge(empty["v"], emptied(n_of("stA", 1))[1])
            for i in range(4, 8):
                ssd(i)
                if i < 6:
                    csb(i + 2)
            pe.wait_ge(empty["v"], emptied(n_of("stA", 3))[1])
            for half in range(2):
                b = take(n_of("sfT", half))
                for c in range(4):
                    last = tr(b[:, c * P:(c + 1) * P], sfin[:, (4 * half + c) * P:(4 * half + c + 1) * P], ident)
                last.then_inc(tile_done, 1)
            project("u", HT, DC, D)
            for b_ in range(NB):
                b = take(n_of("bcs", b_))
                mm(b, onehot[:, b_, :], bc_s, start=True, stop=True).then_inc(tile_done, 1)
            b = take(n_of("vvar"))
            for c in range(DC):
                pe.wait_ge(S("v_squares"), c + 1)
                last = mm(b[:, 0:T], ones, HT[:, c, :], start=(c == 0), stop=(c == DC - 1))
            last.then_inc(tile_done, 1)
            pe.wait_ge(S("v_normed"), DC)
            for j in range(2):
                for half in range(2):
                    b = take(n_of("vtm", 2 * j + half))
                    for c in range(4):
                        last = tr(b[:, c * P:(c + 1) * P], V[:, 4 * half + c, j * P:(j + 1) * P], ident)
                    last.then_inc(tile_done, 1)
            for half in range(2):
                b = take(n_of("avT", half))
                for c in range(4):
                    last = tr(b[0:NB, c * P:(c + 1) * P], V[:, 4 * half + c, TP:T], ident)
                last.then_inc(tile_done, 1)
            pe.wait_ge(S("ws_loaded"), 16)
            for half in range(2):
                b = take(n_of("wsT", half))
                for c in range(4):
                    last = tr(b[:, c * P:(c + 1) * P], ws[:, (4 * half + c) * P:(4 * half + c + 1) * P], ident)
                last.then_inc(tile_done, 1)
            pe.wait_ge(S("bs_loaded"), 16)
            mm(ps[:, 6, 128:136], ones[0:1, :], ws[0:1, 0:1024:P], start=True, stop=True)
            mm(ps[:, 5, 136:144], ones[32:33, :], bsr[:, 0:1024:P], start=True, stop=True).then_inc(S("wb_done"), 1)
            pe.wait_ge(empty["a"], emptied(n_of("vtm", 3))[1])
            pe.wait_ge(empty["v"], emptied(n_of("wsT", 1))[1])
            for h in range(8):
                b = take(n_of("mixA", h))
                for j in range(2):
                    mm(b[:, j * P:(j + 1) * P], v_tm[:, j, h * P:(h + 1) * P], wsT[:, h, :], start=True, stop=False)
                    last = mm(b[:, j * P:(j + 1) * P], ones[32:33, :], bsr[:, h * P:(h + 1) * P], start=False, stop=True)
                last.then_inc(tile_done, 1)
            for g in range(2):
                b = take(n_of("gate", g))
                for c in range(4):
                    pe.wait_ge(S("yz_squares"), 4 * g + c + 1)
                    last = mm(b[:, 0:T], ones, HT[:, 4 * g + c, :], start=(c == 0), stop=(c == 3))
                last.then_inc(tile_done, 1)
            pe.wait_ge(S("yb_ready"), DC)
            pe.wait_ge(S("ya_ready"), 1)
            project("out0", UZ, 16, D)
            square_sums(1)

            def attention(l, k_post, k_pre):
                if l == 0:
                    pe.wait_ge(S("mem_scaled"), 1)
                    for c in range(DC):
                        b = take(n_of("memT", c))
                        for m in range(2):
                            last = tr(b[:, m * P:(m + 1) * P], mem_in[:, m, c * P:(c + 1) * P], ident)
                        last.then_inc(tile_done, 1)
                pe.wait_ge(S("mem_gain_ready"), l + 1)
                project_tm(f"k{l}", MG)
                square_sums(k_pre)
                pe.wait_ge(empty["a"], emptied(n_of(f"k{l}", 3))[1])
                for c in range(DC):
                    b = take(n_of(f"kT{l}", c))
                    for m in range(2):
                        last = tr(b[:, m * P:(m + 1) * P], k_tm[:, m, c * P:(c + 1) * P], ident)
                    last.then_inc(tile_done, 1)
                wait_norm(k_pre)
                project(f"q{l}", HT, DC, D)
                project_tm(f"vm{l}", MG)
                for half in range(2):
                    b = take(n_of(f"qs{l}", half))
                    for c in range(4):
                        last = tr(b[0:NB, c * P:(c + 1) * P], QT[:, 4 * half + c, TP:T], ident)
                    last.then_inc(tile_done, 1)
                pe.wait_ge(empty["a"], emptied(n_of(f"qs{l}", 1))[1])
                for i in range(16):
                    b = take(n_of(f"qB{l}", i))
                    mm(b, onehot[:, i // 2, :], q_s[:, (i % 2) * 512:(i % 2) * 512 + 512], start=True, stop=True) \
                        .then_inc(tile_done, 1)
                b = take(n_of(f"sT{l}"))
                pe.wait_ge(S("k_cache_used"), NB * (l + 1))
                for m in range(2):
                    last = tr(b[0:32, m * P:(m + 1) * P], scs[:, m, :], ident)
                last.then_inc(tile_done, 1)
                pe.wait_ge(S("sample_probs"), l + 1)
                b = take(n_of(f"pTs{l}"))
                for m in range(2):
                    last = tr(b[:, m * 32:m * 32 + 32], p_s[:, m * P:(m + 1) * P], ident[0:32, 0:32])
                last.then_inc(tile_done, 1)
                for i in range(4):
                    g, hp = i // 2, i % 2
                    b = take(n_of(f"sc{l}", i))
                    for h in range(2):
                        for d in range(2):
                            c = 2 * (2 * hp + h) + d
                            last = mm(b[:, h * 256:(h + 1) * 256], QT[:, c, g * P:(g + 1) * P], KT[:, c, :],
                                      start=(d == 0), stop=(d == 1))
                    last.then_inc(tile_done, 1)
                pe.wait_ge(empty["v"], emptied(n_of(f"pTs{l}"))[1])
                for b_ in range(NB):
                    pe.wait_ge(S(f"v_cache_loaded{b_ % 2}"), 16 * (4 * l + b_ // 2 + 1))
                    for c in range(DC):
                        for m in range(2):
                            k = (c // 2) * NB + b_
                            last = mm(ps[:, 7, c * NB + b_:c * NB + b_ + 1], vc[b_ % 2][:, m, c * P:(c + 1) * P],
                                      pts[:, m, k:k + 1], start=(m == 0), stop=(m == 1))
                    last.then_inc(S("v_cache_used"), 1)
                for h in range(XH):
                    pe.wait_ge(S("probs_ready"), 4 * l + 4)
                    b = take(n_of(f"pT{l}", h))
                    for m in range(2):
                        for g in range(2):
                            last = tr(b[:, m * 256 + g * P:m * 256 + g * P + P], PR[:, g, h, m * P:(m + 1) * P], ident)
                    last.then_inc(tile_done, 1)
                for c in range(DC):
                    pe.wait_ge(empty["a"], emptied(n_of(f"pT{l}", c // 2))[1])
                    b = take(n_of(f"pv{l}", c))
                    for m in range(2):
                        last = mm(b[:, 0:256], vm_tm[:, m, c * P:(c + 1) * P], PT[:, c // 2, m, :],
                                  start=(m == 0), stop=(m == 1))
                    last.then_inc(tile_done, 1)
                pe.wait_ge(empty["a"], emptied(n_of(f"pv{l}", 7))[1])
                pe.wait_ge(S("o_samples"), l + 1)
                project(f"xo{l}", OT, DC, D)
                square_sums(k_pre + 1)
                square_sums(k_pre + 2)
                wait_norm(k_pre + 2)

            attention(0, 1, 2)
            for i, n in enumerate(FGROUPS):
                project(f"gate{i}", HT, DC, n * P)
                project(f"up{i}", HT, DC, n * P)
            pe.wait_ge(empty["v"], emptied(n_of("up5", 1))[1])
            project("down", hid, FC, D)
            square_sums(5)
            square_sums(6)
            wait_norm(6)
            project("f", HT, DC, D)
            project("q", HT, DC, D)
            project("i", HT, DC, D)
            project("g", HT, DC, D)
            for j in range(2):
                for half in range(2):
                    b = take(n_of("iT", 2 * j + half))
                    for c in range(4):
                        last = tr(b[:, c * P:(c + 1) * P], I[:, 4 * half + c, j * P:(j + 1) * P], ident)
                    last.then_inc(tile_done, 1)
            for half in range(2):
                b = take(n_of("isT", half))
                for c in range(4):
                    last = tr(b[0:NB, c * P:(c + 1) * P], I[:, 4 * half + c, TP:T], ident)
                last.then_inc(tile_done, 1)
            pe.wait_ge(S("k_decayed"), 1)
            for j in range(2):
                for half in range(2):
                    b = take(n_of("kT", 2 * j + half))
                    for c in range(4):
                        last = tr(b[:, c * P:(c + 1) * P], K[:, 4 * half + c, j * P:(j + 1) * P], ident)
                    last.then_inc(tile_done, 1)
            for hq in range(2):
                b = take(n_of("att", hq)).rearrange("p (h j t) -> p h j t", h=4, j=2)
                for h in range(4):
                    for ch in range(4):
                        r0, hh = 64 * (ch % 2), 4 * hq + h
                        last = mm(b[r0:r0 + 64, h, ch // 2, :], Fg[:, hh, ch * 64:ch * 64 + 64],
                                  Q[:, hh, ch * 64:ch * 64 + 64], start=True, stop=True)
                last.then_inc(tile_done, 1)
            pe.wait_ge(empty["a"], emptied(n_of("kT", 3))[1])
            for ch in range(4):
                r0, j = 64 * (ch % 2), ch // 2
                for half in range(2):
                    b = take(n_of("upd", 2 * ch + half))
                    for c in range(4):
                        hh = 4 * half + c
                        last = mm(b[:, c * P:(c + 1) * P], kp_tm[r0:r0 + 64, j, hh * P:(hh + 1) * P],
                                  i_tm[r0:r0 + 64, j, hh * P:(hh + 1) * P], start=True, stop=True)
                    last.then_inc(tile_done, 1)
            for h in range(8):
                b = take(n_of("ho", h))
                if h == 0:
                    pe.wait_ge(empty["v"], emptied(n_of("upd", 7))[1])
                for j in range(2):
                    mm(b[:, j * P:(j + 1) * P], i_tm[:, j, h * P:(h + 1) * P], att[:, h, j, :], start=True, stop=False,
                       skip_group_check=True)
                    for ch in range(2 * j, 2 * j + 2):
                        if ch:
                            last = mm(b[:, ch * 64:ch * 64 + 64], st[ch - 1][:, h, :], Q[:, h, ch * 64:ch * 64 + 64],
                                      start=False, stop=(ch % 2 == 1), skip_group_check=True)
                last.then_inc(tile_done, 1)
            pe.wait_ge(empty["a"], emptied(n_of("isT", 1))[1])

            def hgrn_read(b_):
                pe.wait_ge(S("h_updated"), b_ + 1)
                for h in range(8):
                    last = mm(ps[:, 7, 64 + 8 * h + b_:64 + 8 * h + b_ + 1], st[b_ % 3][:, h, :], Q[:, h, TP + b_:TP + b_ + 1],
                              start=True, stop=True)
                last.then_inc(S("hgrn_read"), 1)

            for b_ in range(NB):
                for half in range(2):
                    b = take(n_of("vB", 2 * b_ + half))
                    mm(b, onehot[:, b_, :], i_s[:, half * 512:(half + 1) * 512], start=True, stop=True).then_inc(tile_done, 1)
                if b_:
                    hgrn_read(b_ - 1)
            hgrn_read(NB - 1)
            for h in range(8):
                b = take(n_of("hn", h))
                pe.wait_ge(S("ho_squares"), h + 1)
                mm(b[:, 0:T], ones, HT[:, h, :], start=True, stop=True).then_inc(tile_done, 1)
            pe.wait_ge(S("ho_ready"), 1)
            project("out1", E, DC, D)
            square_sums(7)
            attention(1, 7, 8)
            pe.wait_ge(S("experts_may_start"), 1)
            for g, (t0, nt) in enumerate(GROUPS):
                for half in range(2):
                    b = take(n_of("htok", 2 * g + half))
                    for c in range(4):
                        last = tr(b[0:nt, c * P:(c + 1) * P], HT[:, 4 * half + c, t0:t0 + nt], ident)
                    last.then_inc(tile_done, 1)
            pe.wait_ge(S("router_loaded"), 16)
            b = take(n_of("logit"))
            for g, (t0, nt) in enumerate(GROUPS):
                for k in range(DC):
                    last = mm(b[0:nt, 8 * g:8 * g + 8], HT[:, k, t0:t0 + nt], wr[:, k, :], start=(k == 0), stop=(k == DC - 1))
            last.then_inc(tile_done, 1)
            pe.wait_ge(S("mask_ready"), 1)
            b = take(n_of("posn"))
            for g, (t0, nt) in enumerate(GROUPS):
                for g2 in range(g + 1):
                    w = tris if g2 == g else ones
                    k = GROUPS[g2][1]
                    last = mm(b[:, 8 * g:8 * g + 8], w[0:k, :], msk[0:k, g2, :], start=(g2 == 0), stop=(g2 == g))
            for g, (t0, nt) in enumerate(GROUPS):
                last = mm(b[:, 24:32], ones[0:nt, :], msk[0:nt, g, :], start=(g == 0), stop=(g == 2))
            last.then_inc(tile_done, 1)
            pe.sem_inc(S("quarter_used"), QRING)
            pe.wait_ge(S("rounds_ready"), 1)
            rounds_v = nc.values_load(rounds_i[0:1, 0:1], engines=[mybir.EngineType.PE], min_val=1, max_val=3)
            with pe.Fori(0, rounds_v) as r:
                with pe.Fori(0, NE) as e:
                    it = pe.snap(r * NE + e)
                    pe.wait_ge(S("pick_ready"), it + 1)
                    pe.wait_ge(S("acc_added"), it * 6 + 1)
                    for c in range(DC):
                        for g, (t0, nt) in enumerate(GROUPS):
                            last = mm(ps[:, 6 + c // 4, (c % 4) * P:(c % 4 + 1) * P], h_tok[0:nt, g, c * P:(c + 1) * P],
                                      pick[0:nt, g, :], start=(g == 0), stop=(g == 2))
                    last.then_inc(S("gather_done"), 1)
                    pe.wait_ge(S("xe_ready"), it + 1)
                    for q, (kind, s, i) in enumerate(QUARTERS):
                        hi, lo = wr_[:, q % QRING, 0, :], wr_[:, q % QRING, 1, :]
                        if kind == "gate" and i == 0:
                            pe.wait_ge(S("hs_ready"), it * NSL + NSL + max(s - 1, 0))
                        if kind == "down" and i == 0:
                            pe.wait_ge(S("hT_ready"), it * NSL + s + 1)
                        pe.wait_ge(S("lo_made"), it * NQ + 2 * MRING + q + 1)
                        if kind == "down":
                            for half in range(2):
                                cols = slice(half * 512, (half + 1) * 512)
                                xh, xl = (x[s % 2][:, i * P:(i + 1) * P] for x in (hT_hi, hT_lo))
                                out = ps[:, 4 + half, :]
                                mm(out, xh, hi[:, cols], start=(s == 0 and i == 0), stop=False)
                                mm(out, xh, lo[:, cols], start=False, stop=False)
                                last = mm(out, xl, hi[:, cols], start=False, stop=(s == NSL - 1 and i == 3))
                        else:
                            out = ps[:, 2 * (s % 2) + (kind == "up"), :]
                            for k in range(2):
                                cols = slice(k * SL, (k + 1) * SL)
                                c = 2 * i + k
                                xh, xl = (x[:, c * P:(c + 1) * P] for x in (xe_hi, xe_lo))
                                mm(out, xh, hi[:, cols], start=(c == 0), stop=False)
                                mm(out, xh, lo[:, cols], start=False, stop=False)
                                last = mm(out, xl, hi[:, cols], start=False, stop=(c == DC - 1))
                        last.then_inc(S("quarter_used"), 1)
                        if q in TURN:
                            s = TURN[q]
                            pe.wait_ge(S("hs_ready"), it * NSL + NSL + s + 1)
                            if s:
                                pe.wait_ge(S("hT_ready"), it * NSL + s)
                            for k in range(4):
                                last = tr(ps[:, 6, k * P:(k + 1) * P], hs[s % 2][:, k * P:(k + 1) * P], ident)
                            last.then_inc(S("h_transposed"), 1)
                    for g, (t0, nt) in enumerate(GROUPS):
                        last = tr(ps[:, 6, t0:t0 + nt], pickg[0:nt, g, :], ident[0:nt, 0:nt])
                    last.then_inc(S("pickT_done"), 1)
                    pe.wait_ge(S("oe_ready"), it + 1)
                    for i in range(6):
                        g, half = i // 2, i % 2
                        t0, nt = GROUPS[g]
                        if i >= 2:
                            pe.wait_ge(S("acc_added"), it * 6 + i)
                        mm(ps[0:nt, 7 - i % 2, :], pickT[:, t0:t0 + nt], oe[:, half * 512:(half + 1) * 512],
                           start=True, stop=True).then_inc(S("scatter_done"), 1)
            pe.wait_ge(S("experts_done"), 1)
            for g, (t0, nt) in enumerate(GROUPS):
                for half in range(2):
                    for c in range(4):
                        last = tr(ps[0:nt, 2 * g + half, c * P:(c + 1) * P], XT[:, 4 * half + c, t0:t0 + nt], ident)
            last.then_inc(S("x_tok_done"), 1)

        @block.scalar
        def _(act):
            f = nc.scalar.activation

            def tile(n):
                act.wait_ge(tile_done, n + 1)
                return bank(n)

            def copies(name, dsts, view=lambda b: b):
                for i, dst in enumerate(dsts):
                    b = tile(n_of(name, i))
                    f(dst, view(b), ACT.Copy).then_inc(empty["a"], 1)

            def block_out(name):
                for c in range(DC):
                    b = tile(n_of(name, c))
                    f(HT[:, c, :], b[:, 0:T], ACT.Square).then_inc(S("squares_ready"), 1)
                    f(MT[:, c, :], b[:, 0:T], ACT.Copy).then_inc(empty["a"], 1)

            def root(k):
                act.wait_ge(S("square_sums_done"), k + 1)
                f(rs, ps[:, 4, 0:T], ACT.Sqrt, bias=eps_c, scale=1.0 / D).then_inc(S("root_ready"), 1)

            def squares_of_x(k):
                for c in range(DC):
                    act.wait_ge(S("x_updated"), DC * posts.index(k - 1) + c + 1)
                    f(MT[:, c, :], XT[:, c, :], ACT.Square).then_inc(S("squares_ready"), 1)

            act.wait_ge(S("small_loaded"), 64)
            f(aexp, alog, ACT.Exp).then_inc(S("aexp_ready"), 1)
            for c in range(DC):
                b = tile(n_of("xT", c))
                f(MT[:, c, :], b[:, 0:T], ACT.Square).then_inc(S("squares_ready"), 1)
                f(XT[:, c, :], b[:, 0:T], ACT.Copy).then_inc(empty["a"], 1)
            act.wait_ge(S("lb_diff"), 1)
            f(lb1, omlb, ACT.Sigmoid).then_inc(S("lb_ready"), 1)
            act.wait_ge(S("eps_ready"), 1)
            root(0)
            for c in range(CC):
                b = tile(n_of("xbc", c))
                f(raw[:, c, 3:259], b[:, 0:TP], ACT.Copy)
                f(raws[:, c, 3, :], b[:, TP:T], ACT.Copy).then_inc(empty["a"], 1)
            act.wait_ge(S("dt_abs_ready"), 1)
            f(dtr[3], dtr[3], ACT.Exp, scale=-1.0).then_inc(S("dt_exp_ready"), 1)
            act.wait_ge(S("dt_done"), 1)
            f(exd[:, 0:8], dtr[1][:, TP:T], ACT.Exp)
            f(exd[:, 8:16], dtr[0][:, TP:T], ACT.Copy).then_inc(S("dt_ready"), 1)
            for c in range(DC):
                b = tile(n_of("v", c))
                f(V[:, c, :], b[:, 0:T], ACT.Gelu_apprx_tanh).then_inc(empty["a"], 1)
            for c in range(CC):
                act.wait_ge(S("conv_ready"), 1 + c // 4)
                f(XBC[:, c, :], XBC[:, c, :], ACT.Silu, bias=par[:, CB + c:CB + c + 1]).then_inc(S("xbc_ready"), 1)
            copies("tr0", [conv_o[:, i * 512:(i + 1) * 512] for i in range(3)], lambda b: b[0:11, :])
            for i in range(4):
                b = tile(n_of("tr0", 3 + i))
                f(x_tm[:, i // 2, (i % 2) * 512:(i % 2 + 1) * 512], b, ACT.Copy).then_inc(empty["a"], 1)
            b = tile(n_of("tr0", 7))
            f(b_tm.rearrange("p j n -> p (j n)"), b, ACT.Copy).then_inc(empty["a"], 1)
            b = tile(n_of("tr0", 8))
            f(bc_s, b[0:NB, :], ACT.Copy).then_inc(empty["a"], 1)
            copies("cb", [CBT.rearrange("p k n -> p (k n)")])
            act.wait_ge(S("conv_stored"), 32)
            for c in range(DC):
                b = tile(n_of("z", c))
                f(Z[:, c, :], b[:, 0:T], ACT.Silu).then_inc(empty["a"], 1)
            act.wait_ge(S("dec_in"), 1)
            f(small[:, 160:224], small[:, 160:224], ACT.Exp).then_inc(S("dec_ready"), 1)

            def lmat(i):
                if i >= 4:
                    b = tile(n_csb(i))
                    if i >= 5:
                        act.wait_ge(S("ce_ready"), i - 4)
                    f(ecs, b, ACT.Exp).then_inc(S("ecs_ready"), 1)
                act.wait_ge(S("ldiff_ready"), i + 1)
                f(Lm[i % 2], Lm[i % 2], ACT.Exp).then_inc(S("lexp_ready"), 1)

            for i in range(8):
                lmat(i)
            copies("sfT", [ssm_o[:, 4 * i:4 * i + 4, :].rearrange("p c n -> p (c n)") for i in range(2)])
            for c in range(DC):
                b = tile(n_of("u", c))
                f(U[:, c, :], b[:, 0:T], ACT.Gelu_apprx_tanh).then_inc(empty["a"], 1)
            for c in range(DC):
                f(HT[:, c, :], V[:, c, :], ACT.Square).then_inc(S("v_squares"), 1)
            b = tile(n_of("vvar"))
            f(rs, b[:, 0:T], ACT.Sqrt, bias=eps_c, scale=1.0 / D).then_inc(empty["a"], 1)
            for c in range(DC):
                act.wait_ge(S("v_scaled"), c + 1)
                f(V[:, c, :], V[:, c, :], ACT.Identity, bias=par[:, LNB + c:LNB + c + 1]).then_inc(S("v_normed"), 1)
            for i in range(4):
                b = tile(n_of("vtm", i))
                f(v_tm[:, i // 2, (i % 2) * 512:(i % 2 + 1) * 512], b, ACT.Copy).then_inc(empty["a"], 1)
            copies("avT", [av_o[:, i * 512:(i + 1) * 512] for i in range(2)], lambda b: b[0:NB, :])
            for c in range(DC):
                act.wait_ge(S("yz_ready"), 1)
                f(HT[:, c, :], Z[:, c, :], ACT.Square).then_inc(S("yz_squares"), 1)
            for g in range(2):
                b = tile(n_of("gate", g))
                f(rsg[:, g, :], b[:, 0:T], ACT.Sqrt, bias=eps_c, scale=2.0 / D).then_inc(empty["a"], 1)
            block_out("out0")

            def attention(l, k_post, k_pre):
                if l == 0:
                    act.wait_ge(S("mem_loaded"), 16)
                    for m in range(2):
                        f(KT.rearrange("p c t -> p (c t)")[:, m * D:(m + 1) * D], mem_in[:, m, :], ACT.Square,
                          accum_out=mrs[:, m:m + 1]).then_inc(S("mem_step"), 1)
                    act.wait_ge(S("mem_step"), 2)
                    f(mrs[:, 2:4], mrs[:, 0:2], ACT.Sqrt, bias=eps_c, scale=1.0 / D).then_inc(S("mem_root"), 1)
                root(k_post)
                if l == 0:
                    act.wait_ge(S("mem_rs_ready"), 1)
                    for m in range(2):
                        last = f(mem_in[:, m, :], mem_in[:, m, :], ACT.Copy, scale=mrs[:, m:m + 1])
                    last.then_inc(S("mem_scaled"), 1)
                    copies("memT", [memh[:, c, :] for c in range(DC)], lambda b: b[:, 0:MEM])
                squares_of_x(k_pre)
                for i in range(4):
                    b = tile(n_of(f"k{l}", i))
                    f(k_tm[:, i % 2, (i // 2) * 512:(i // 2 + 1) * 512], b, ACT.Copy).then_inc(empty["a"], 1)
                root(k_pre)
                copies(f"kT{l}", [KT[:, c, :] for c in range(DC)], lambda b: b[:, 0:MEM])
                for c in range(DC):
                    b = tile(n_of(f"q{l}", c))
                    f(QT[:, c, :], b[:, 0:T], ACT.Copy, scale=(D // XH) ** -0.5).then_inc(empty["a"], 1)
                for i in range(4):
                    b = tile(n_of(f"vm{l}", i))
                    f(vm_tm[:, i % 2, (i // 2) * 512:(i // 2 + 1) * 512], b, ACT.Copy).then_inc(empty["a"], 1)
                copies(f"qs{l}", [q_s[:, i * 512:(i + 1) * 512] for i in range(2)], lambda b: b[0:NB, :])
                b = tile(n_of(f"sT{l}"))
                act.wait_ge(S("sample_max"), l + 1)
                f(p_s, b[0:32, 0:256], ACT.Exp, bias=smx, accum_out=ssm).then_inc(empty["a"], 1)
                for i in range(4):
                    b = tile(n_of(f"sc{l}", i))
                    act.wait_ge(S("max_ready"), 4 * l + i + 1)
                    g, hp = i // 2, i % 2
                    for h in range(2):
                        last = f(PR[:, g, 2 * hp + h, :], b[:, h * 256:(h + 1) * 256], ACT.Exp,
                                 bias=mx[:, 2 * i + h:2 * i + h + 1], accum_out=sm[:, 2 * i + h:2 * i + h + 1])
                    last.then_inc(empty["a"], 1)
                copies(f"pT{l}", [PT[:, h].rearrange("p m t -> p (m t)") for h in range(XH)])
                copies(f"pv{l}", [OT[:, c, 0:TP] for c in range(DC)], lambda b: b[:, 0:TP])
                block_out(f"xo{l}")
                root(k_pre + 1)
                squares_of_x(k_pre + 2)
                root(k_pre + 2)

            attention(0, 1, 2)
            for i in range(FC):
                b = tile(n_of(f"gate{i // 4}", i % 4))
                if i >= 4:
                    act.wait_ge(empty["v"], emptied(n_of(f"up{i // 4 - 1}", i % 4))[1])
                f(gtmp[i % 4], b[:, 0:T], ACT.Silu).then_inc(empty["a"], 1)
            block_out("down")
            root(5)
            squares_of_x(6)
            root(6)
            for name, dst, fn in (("f", Fg, ACT.Sigmoid), ("q", Q, ACT.Silu)):
                for c in range(DC):
                    b = tile(n_of(name, c))
                    f(dst[:, c, :], b[:, 0:T], fn).then_inc(empty["a"], 1)
            act.wait_ge(S("fg_ready"), 1)
            f(Fg, Fg, ACT.Ln).then_inc(S("logf_ready"), 1)
            for c in range(DC):
                b = tile(n_of("i", c))
                f(I[:, c, :], b[:, 0:T], ACT.Copy).then_inc(empty["a"], 1)
            act.wait_ge(S("bc_ready"), 1)
            f(etot[:, :, 0:4], BC[:, :, 63:TP:64], ACT.Exp)
            f(es, BC[:, :, TP:T], ACT.Exp).then_inc(S("es_ready"), 1)
            f(E[:, :, 0:TP], BC[:, :, 0:TP], ACT.Exp).then_inc(S("e_ready"), 1)
            act.wait_ge(S("e_used"), 1)
            f(E[:, :, 0:TP], BC[:, :, 0:TP], ACT.Exp, scale=-1.0).then_inc(S("e_ready"), 1)
            act.wait_ge(S("e_used"), 2)
            f(E[:, :, 0:TP], E[:, :, 0:TP], ACT.Exp).then_inc(S("e_ready"), 1)
            for c in range(DC):
                b = tile(n_of("g", c))
                f(G[:, c, :], b[:, 0:T], ACT.Silu).then_inc(empty["a"], 1)
            for i in range(4):
                b = tile(n_of("iT", i))
                f(i_tm[:, i // 2, (i % 2) * 512:(i % 2 + 1) * 512], b, ACT.Copy).then_inc(empty["a"], 1)
            copies("isT", [i_s[:, i * 512:(i + 1) * 512] for i in range(2)], lambda b: b[0:NB, :])
            for i in range(4):
                b = tile(n_of("kT", i))
                f(kp_tm[:, i // 2, (i % 2) * 512:(i % 2 + 1) * 512], b, ACT.Copy).then_inc(empty["a"], 1)
            copies("ho", [E[:, h, 0:TP] for h in range(8)], lambda b: b[:, 0:TP])
            act.wait_ge(S("ho_samples"), 1)
            act.wait_ge(empty["a"], emptied(n_of("ho", 7))[1])
            for h in range(8):
                f(HT[:, h, :], E[:, h, :], ACT.Square).then_inc(S("ho_squares"), 1)
            for h in range(8):
                b = tile(n_of("hn", h))
                f(BC[:, h, :], b[:, 0:T], ACT.Sqrt, bias=eps_c, scale=1.0 / P).then_inc(empty["a"], 1)
            block_out("out1")
            attention(1, 7, 8)
            act.wait_ge(S("experts_may_start"), 1)
            for i in range(6):
                g, half = i // 2, i % 2
                nt = GROUPS[g][1]
                b = tile(n_of("htok", i))
                f(h_tok[0:nt, g, half * 512:(half + 1) * 512], b[0:nt, :], ACT.Copy).then_inc(empty["a"], 1)
            act.wait_ge(S("top_diff"), 1)
            f(tw[:, :, 1], tw[:, :, 0], ACT.Exp).then_inc(S("top_exp"), 1)
            act.wait_ge(S("rounds_ready"), 1)
            rounds_v = nc.values_load(rounds_i[0:1, 0:1], engines=[mybir.EngineType.Activation], min_val=1, max_val=3)
            with act.Fori(0, rounds_v) as r:
                with act.Fori(0, NE) as e:
                    it = act.snap(r * NE + e)
                    def make_hi(q):
                        if q % 2 == 0:
                            act.wait_ge(mloaded[q // 2 % MRING], it * (16 * NBLK // MRING) + 16 * (q // 2 // MRING + 1))
                        act.wait_ge(S("quarter_used"), it * NQ + q + 1)
                        f(wr_[:, q % QRING, 0, :], quarter(q), ACT.Copy).then_inc(S("hi_made"), 1)

                    for q in range(NQ):
                        make_hi(q)
                        if q == QRING - 1:
                            act.wait_ge(S("gather_done"), it + 1)
                            for half in range(2):
                                f(xe_hi[:, half * 512:(half + 1) * 512], ps[:, 6 + half, :], ACT.Copy).then_inc(S("xe_hi_made"), 1)
                        kind, s, i = QUARTERS[q - QRING] if q >= QRING else ("", 0, 0)
                        if kind == "gate" and i == 3:
                            act.wait_ge(S("quarter_used"), it * NQ + q + 1)
                            f(sg[s % 2], ps[:, 2 * (s % 2), :], ACT.Silu).then_inc(S("silu_done"), 1)
                        if q - QRING in TURN:
                            s = TURN[q - QRING]
                            act.wait_ge(S("h_transposed"), it * NSL + s + 1)
                            f(hT_hi[s % 2], ps[:, 6, :], ACT.Copy).then_inc(S("hT_hi_made"), 1)
                    act.wait_ge(S("pickT_done"), it + 1)
                    f(pickT, ps[:, 6, 0:T], ACT.Copy)
                    act.wait_ge(S("quarter_used"), it * NQ + NQ + QRING)
                    f(oe[:, 0:512], ps[:, 4, :], ACT.Copy)
                    f(oe[:, 512:D], ps[:, 5, :], ACT.Copy).then_inc(S("oe_ready"), 1)
            act.wait_ge(S("experts_done"), 1)
            act.wait_ge(S("x_tok_done"), 1)
            for g, (t0, nt) in enumerate(GROUPS):
                f(x_tok[0:nt, g, 0:512], ps[0:nt, 2 * g, :], ACT.Copy)
                f(x_tok[0:nt, g, 512:D], ps[0:nt, 2 * g + 1, :], ACT.Copy).then_inc(S("x_tok_ready"), 1)
                f(ysq[0:nt, :], acc[0:nt, g, :], ACT.Square, accum_out=frs[0:nt, g:g + 1]).then_inc(S("y_squares"), 1)
                act.wait_ge(S("y_squares"), g + 1)
                f(frs[0:nt, 3 + g:4 + g], frs[0:nt, g:g + 1], ACT.Sqrt, bias=eps_c[0:nt], scale=1.0 / D) \
                    .then_inc(S("y_root"), 1)

        @block.vector
        def _(dve):
            v = nc.vector
            TT, TS, STT = v.tensor_tensor, v.tensor_scalar, v.scalar_tensor_tensor
            steps = [0]

            def link(ins):
                steps[0] += 1
                ins.then_inc(S("dve_step"), 1)
                dve.wait_ge(S("dve_step"), steps[0])

            def tile(n):
                dve.wait_ge(tile_done, n + 1)
                return bank(n)

            def finish_norm(k):
                kind, layer, pre = NORMS[k]
                dve.wait_ge(S("root_ready"), k + 1)
                link(v.reciprocal(rs, rs))
                if pre:
                    for c in range(DC):
                        last = STT(out=HT[:, c, :], in0=XT[:, c, :], scalar=gain(kind, layer, c), in1=rs,
                                   op0=ALU.mult, op1=ALU.mult)
                    last.then_inc(S("normed"), 1)
                else:
                    for c in range(DC):
                        last = STT(out=MT[:, c, :], in0=MT[:, c, :], scalar=gain(kind, layer, c), in1=rs,
                                   op0=ALU.mult, op1=ALU.mult)
                    link(last)
                    for c in range(DC):
                        TT(XT[:, c, :], XT[:, c, :], MT[:, c, :], ALU.add).then_inc(S("x_updated"), 1)

            v.memset(eps_c, EPS).then_inc(S("eps_ready"), 1)
            b = tile(n_of("par"))
            v.tensor_copy(par, b[:, 0:220]).then_inc(empty["v"], 1)
            dve.wait_ge(empty["v"], 1)
            TT(omlb, par[:, LB + 8:LB + 16], par[:, LB:LB + 8], ALU.subtract).then_inc(S("lb_diff"), 1)
            b = tile(n_of("st"))
            v.tensor_copy(raws[:, :, 0:3, :], b[:, 0:288].rearrange("p (c b k) -> p c k b", c=CC, b=NB)) \
                .then_inc(empty["v"], 1)
            dve.wait_ge(S("lb_ready"), 1)
            link(TS(omlb, lb1, -1.0, 1.0, ALU.mult, ALU.add))
            finish_norm(0)
            for c4 in range(3):
                dve.wait_ge(empty["a"], emptied(n_of("xbc", 4 * c4 + 3))[1])
                cc = range(4 * c4, 4 * c4 + 4)
                for c in cc:
                    last = TS(XBC[:, c, 0:TP], raw[:, c, 3:259], par[:, CW + 36 + c:CW + 37 + c], None, ALU.mult)
                link(last)
                for k in range(3):
                    for c in cc:
                        last = STT(out=XBC[:, c, 0:TP], in0=raw[:, c, k:k + TP], scalar=par[:, CW + 12 * k + c:CW + 12 * k + c + 1],
                                   in1=XBC[:, c, 0:TP], op0=ALU.mult, op1=ALU.add)
                    link(last)
                xs = XBC[:, 4 * c4:4 * c4 + 4, TP:T]
                tmp = t2[:, 0, 0:32].rearrange("p (c b) -> p c b", c=4)
                for k in range(4):
                    w = par[:, CW + 12 * k + 4 * c4:CW + 12 * k + 4 * c4 + 4].unsqueeze(2).broadcast_to([P, 4, NB])
                    link(TT(tmp if k else xs, raws[:, 4 * c4:4 * c4 + 4, k, :], w, ALU.mult))
                    if k:
                        ins = TT(xs, xs, tmp, ALU.add)
                        if k < 3:
                            link(ins)
                        else:
                            ins.then_inc(S("conv_ready"), 1)
            tail = conv_tail.rearrange("p (c t) -> p c t", c=CC)
            v.tensor_copy(tail[:, :, 0:3], raw[:, :, TP:TP + 3])
            v.tensor_copy(tail[:, :, 3:11], raws[:, :, 3, :]).then_inc(S("tail_ready"), 1)
            b = tile(n_of("dt"))
            x_, p_, e_, z_, z2_ = dtr[2], dtr[4], dtr[3], dtr[5], dtr[6]
            v.tensor_scalar(x_, b[0:16, 0:T], dtb, None, ALU.add).then_inc(empty["v"], 1)
            dve.wait_ge(empty["v"], emptied(n_of("dt"))[1])
            link(TS(e_, x_, -1.0, None, ALU.mult))
            TT(e_, e_, x_, ALU.max).then_inc(S("dt_abs_ready"), 1)
            dve.wait_ge(S("dt_exp_ready"), 1)
            link(TS(z_, e_, 2.0, None, ALU.add))
            link(v.reciprocal(z_, z_))
            link(TT(z_, z_, e_, ALU.mult))
            link(TT(z2_, z_, z_, ALU.mult))
            link(TS(p_, z2_, 1.0 / 17, None, ALU.mult))
            for k in range(7, 0, -1):
                link(STT(out=p_, in0=p_, scalar=1.0 / (2 * k + 1), in1=z2_, op0=ALU.add, op1=ALU.mult))
            link(STT(out=p_, in0=p_, scalar=1.0, in1=z_, op0=ALU.add, op1=ALU.mult))
            link(TS(x_, x_, 0.0, None, ALU.max))
            link(STT(out=dtr[0], in0=p_, scalar=2.0, in1=x_, op0=ALU.mult, op1=ALU.add))
            dve.wait_ge(S("aexp_ready"), 1)
            TS(dtr[1], dtr[0], aexp, -1.0, ALU.mult, ALU.mult).then_inc(S("dt_done"), 1)
            dve.wait_ge(S("dt_tm_done"), 1)
            v.tensor_copy(small[:, 64:128], ps[:, 5, 0:64]).then_inc(S("dt_tm_ready"), 1)
            link(v.tensor_copy(exc.rearrange("p c k -> p (c k)"), ps[:, 5, 128:256]))
            dve.wait_ge(S("xbc_ready"), CC)
            TT(exc[:, :, 8:16], exc[:, :, 8:16], XBC[:, 0:DC, TP:T], ALU.mult).then_inc(S("exc_ready"), 1)
            b = tile(n_of("vmean"))
            for c in range(DC):
                last = STT(out=V[:, c, :], in0=b[:, 0:T], scalar=-1.0 / D, in1=V[:, c, :], op0=ALU.mult, op1=ALU.add)
            last.then_inc(empty["v"], 1)
            dve.wait_ge(S("cs_done"), 1)
            v.tensor_copy(small[:, 128:160], ps[:, 6, 0:32])
            link(v.tensor_copy(small[:, 192:224], ps[:, 6, 32:64]))
            TT(small[:, 160:192], small[:, 192:224], small[:, 128:160], ALU.subtract).then_inc(S("dec_in"), 1)
            dve.wait_ge(S("dec_ready"), 1)
            link(TT(wdec, wdec, dd[:, :, 0, :], ALU.mult))

            def weigh(j):
                TT(xw.rearrange("p (h n) -> p h n", h=16), x_tm[:, j, :].rearrange("p (h n) -> p h n", h=16),
                   wdec[:, j, :].unsqueeze(2).broadcast_to([P, 16, 64]), ALU.mult).then_inc(S("xw_ready"), 1)

            def lmat(i):
                j, hq = i // 4, i % 4
                b = tile(n_csb(i))
                if i >= 2:
                    dve.wait_ge(S("y_ssd_done"), i - 1)
                if i >= 4:
                    dve.wait_ge(S("ecs_ready"), i - 3)
                for h in range(4):
                    last = STT(out=Lm[i % 2][:, h * P:(h + 1) * P], in0=b[:, h * P:(h + 1) * P],
                               scalar=cs[:, j, 4 * hq + h:4 * hq + h + 1], in1=mneg, op0=ALU.subtract, op1=ALU.add)
                last.then_inc(empty["v"], 1)
                dve.wait_ge(empty["v"], emptied(n_csb(i))[1])
                v.sem_inc(S("ldiff_ready"), 1)
                if i >= 4:
                    TT(split(Ce[i % 2], 4), split(ecs, 4), XBC[:, 10 + hq // 2, j * P:(j + 1) * P].unsqueeze(1).broadcast_to([P, 4, P]),
                       ALU.mult).then_inc(S("ce_ready"), 1)
                dve.wait_ge(S("lexp_ready"), i + 1)
                for h in range(4):
                    last = STT(out=Lm[i % 2][:, h * P:(h + 1) * P], in0=Lm[i % 2][:, h * P:(h + 1) * P],
                               scalar=dd[:, j, 0, 4 * hq + h:4 * hq + h + 1], in1=CBT[:, 2 * j + hq // 2, :],
                               op0=ALU.mult, op1=ALU.mult)
                last.then_inc(S("lmat_ready"), 1)

            def y_out(i):
                j, hq = i // 4, i % 4
                dve.wait_ge(S("y_ssd_done"), i + 1)
                for c2 in range(2):
                    c = 2 * hq + c2
                    last = STT(out=XBC[:, c, j * P:(j + 1) * P], in0=XBC[:, c, j * P:(j + 1) * P], scalar=dcol[:, c:c + 1],
                               in1=ps[:, 5 + 2 * (i % 2), c2 * P:(c2 + 1) * P], op0=ALU.mult, op1=ALU.add)
                last.then_inc(S("y_ssd_used"), 1)

            dve.wait_ge(empty["a"], emptied(n_of("cb"))[1])
            weigh(0)
            lmat(0), lmat(1)
            for i in range(4):
                y_out(i)
                lmat(i + 2)
            for g in range(2):
                b = tile(n_of("stA", g))
                v.tensor_copy(prev[:, g * 512:(g + 1) * 512], b).then_inc(empty["v"], 1)
            weigh(1)
            dve.wait_ge(empty["v"], emptied(n_of("stA", 1))[1])
            link(TT(sfin.rearrange("p (h n) -> p h n", h=16), prev.rearrange("p (h n) -> p h n", h=16),
                    cdec[:, 1, :].unsqueeze(2).broadcast_to([P, 16, 64]), ALU.mult))
            for g in range(2):
                b = tile(n_of("stA", 2 + g))
                TT(sfin[:, g * 512:(g + 1) * 512], sfin[:, g * 512:(g + 1) * 512], b, ALU.add).then_inc(empty["v"], 1)
            for i in range(4, 8):
                y_out(i)
                if i < 6:
                    lmat(i + 2)
            ys = exc[:, :, 0:8]
            for b_ in range(NB):
                b = tile(n_of("bcs", b_))
                if b_:
                    dve.wait_ge(S("s0_used"), b_)
                for g in range(2):
                    last = TT(t2[:, 4 * g:4 * g + 4, :], b[:, g * P:(g + 1) * P].unsqueeze(1).broadcast_to([P, 4, P]),
                              exc[:, 4 * g:4 * g + 4, 8 + b_:9 + b_].broadcast_to([P, 4, P]), ALU.mult)
                link(last)
                dve.wait_ge(S("s0_decayed"), b_ + 1)
                TT(s0[b_ % 2], s0[b_ % 2], t2, ALU.add).then_inc(S("s0_summed"), 1)
                dve.wait_ge(S("s0_summed"), b_ + 1)
                for g in range(2):
                    last = TT(t2[:, 4 * g:4 * g + 4, :], s0[b_ % 2][:, 4 * g:4 * g + 4, :],
                              b[:, 256 + g * P:256 + (g + 1) * P].unsqueeze(1).broadcast_to([P, 4, P]), ALU.mult)
                last.then_inc(empty["v"], 1)
                dve.wait_ge(empty["v"], emptied(n_of("bcs", b_))[1])
                v.tensor_reduce(ysum[:, :, b_], t2, X, ALU.add).then_inc(S("s0_used"), 1)
            dve.wait_ge(S("s0_used"), NB)
            xs = XBC[:, 0:DC, TP:T]
            link(TT(xs, xs, dcol.unsqueeze(2).broadcast_to([P, DC, NB]), ALU.mult))
            link(TT(xs, xs, ysum, ALU.add))
            TT(Z, Z, XBC[:, 0:DC, :], ALU.mult).then_inc(S("yz_ready"), 1)
            dve.wait_ge(empty["a"], emptied(n_of("vvar"))[1])
            link(v.reciprocal(rs, rs))
            for c in range(DC):
                STT(out=V[:, c, :], in0=V[:, c, :], scalar=par[:, LNG + c:LNG + c + 1], in1=rs, op0=ALU.mult, op1=ALU.mult) \
                    .then_inc(S("v_scaled"), 1)
            for i in range(2):
                b = tile(n_of("wsT", i))
                TT(wsT[:, 4 * i:4 * i + 4, :], split(b, 4), triu.unsqueeze(1).broadcast_to([P, 4, P]), ALU.mult) \
                    .then_inc(empty["v"], 1)
            dve.wait_ge(S("wb_done"), 1)
            v.tensor_copy(wb[:, 0:8], ps[:, 6, 128:136])
            link(v.tensor_copy(wb[:, 8:16], ps[:, 5, 136:144]))
            dve.wait_ge(S("v_normed"), DC)
            tmp = t2[:, 0, 0:64].rearrange("p (c b) -> p c b", c=DC)
            link(TT(tmp, V[:, :, TP:T], wb[:, 0:8].unsqueeze(2).broadcast_to([P, DC, NB]), ALU.mult))
            link(TT(tmp, tmp, wb[:, 8:16].unsqueeze(2).broadcast_to([P, DC, NB]), ALU.add))
            dve.wait_ge(empty["a"], emptied(n_of("u", 7))[1])
            TT(U[:, :, TP:T], U[:, :, TP:T], tmp, ALU.mult)
            for h in range(8):
                b = tile(n_of("mixA", h))
                TT(U[:, h, 0:TP], U[:, h, 0:TP], b[:, 0:TP], ALU.mult).then_inc(empty["v"], 1)
            dve.wait_ge(empty["v"], emptied(n_of("mixA", 7))[1])
            v.sem_inc(S("ya_ready"), 1)
            dve.wait_ge(empty["a"], emptied(n_of("gate", 1))[1])
            link(v.reciprocal(rsg, rsg))
            for c in range(DC):
                STT(out=Z[:, c, :], in0=Z[:, c, :], scalar=par[:, BN + c:BN + c + 1], in1=rsg[:, c // 4, :],
                    op0=ALU.mult, op1=ALU.mult).then_inc(S("yb_ready"), 1)

            def attention(l, k_post, k_pre):
                if l == 0:
                    dve.wait_ge(S("mem_root"), 1)
                    v.reciprocal(mrs[:, 0:2], mrs[:, 2:4]).then_inc(S("mem_rs_ready"), 1)
                finish_norm(k_post)
                finish_norm(k_pre)
                for i in range(16):
                    b_, half = i // 2, i % 2
                    b = tile(n_of(f"qB{l}", i))
                    if half == 0:
                        dve.wait_ge(S(f"k_cache_loaded{b_ % 2}"), 16 * (4 * l + b_ // 2 + 1))
                    for m in range(2):
                        for h in range(2):
                            col = (2 * half + h) * NB + b_
                            ins = v.tensor_tensor_reduce(out=junk, in0=kc[b_ % 2][:, m, (2 * half + h) * 256:(2 * half + h + 1) * 256],
                                                         in1=b[:, h * 256:(h + 1) * 256], scale=1.0, scalar=0.0, op0=ALU.mult,
                                                         op1=ALU.add, accum_out=scs[:, m, col:col + 1])
                            link(ins) if not (m and h) else None
                    ins.then_inc(empty["v"], 1)
                    dve.wait_ge(empty["v"], emptied(n_of(f"qB{l}", i))[1])
                    if half:
                        v.sem_inc(S("k_cache_used"), 1)
                b = tile(n_of(f"sT{l}"))
                link(v.tensor_reduce(smx, b[0:32, 0:256], X, ALU.max))
                TS(smx, smx, -1.0, None, ALU.mult).then_inc(S("sample_max"), 1)
                dve.wait_ge(empty["a"], emptied(n_of(f"sT{l}"))[1])
                link(v.reciprocal(ssm, ssm))
                TS(p_s, p_s, ssm, None, ALU.mult).then_inc(S("sample_probs"), 1)
                b = tile(n_of(f"pTs{l}"))
                v.tensor_copy(pts.rearrange("p m k -> p (m k)"), b[:, 0:64]).then_inc(empty["v"], 1)
                for i in range(5):
                    if i < 4:
                        b = tile(n_of(f"sc{l}", i))
                        link(v.tensor_reduce(mx[:, 2 * i:2 * i + 2], b.rearrange("p (h m) -> p h m", h=2), X, ALU.max))
                        TS(mx[:, 2 * i:2 * i + 2], mx[:, 2 * i:2 * i + 2], -1.0, None, ALU.mult).then_inc(S("max_ready"), 1)
                    if i:
                        g, hp = (i - 1) // 2, (i - 1) % 2
                        dve.wait_ge(empty["a"], emptied(n_of(f"sc{l}", i - 1))[1])
                        link(v.reciprocal(sm[:, 2 * i - 2:2 * i], sm[:, 2 * i - 2:2 * i]))
                        TT(PR[:, g, 2 * hp:2 * hp + 2, :], PR[:, g, 2 * hp:2 * hp + 2, :],
                           sm[:, 2 * i - 2:2 * i].unsqueeze(2).broadcast_to([P, 2, MEM]), ALU.mult).then_inc(S("probs_ready"), 1)
                dve.wait_ge(S("v_cache_used"), NB * (l + 1))
                v.tensor_copy(OT[:, :, TP:T], split(ps[:, 7, 0:64], DC)).then_inc(S("o_samples"), 1)
                finish_norm(k_pre + 1)
                finish_norm(k_pre + 2)

            attention(0, 1, 2)
            for i in range(FC):
                dve.wait_ge(empty["a"], emptied(n_of(f"gate{i // 4}", i % 4))[1])
                b = tile(n_of(f"up{i // 4}", i % 4))
                TT(hid[:, i, :], b[:, 0:T], gtmp[i % 4], ALU.mult).then_inc(empty["v"], 1)
            finish_norm(5)
            finish_norm(6)
            dve.wait_ge(empty["a"], emptied(n_of("f", 7))[1])
            for c in range(DC):
                last = TS(Fg[:, c, :], Fg[:, c, :], omlb[:, c:c + 1], lb1[:, c:c + 1], ALU.mult, ALU.add)
            link(last)
            TS(K, Fg, -1.0, 1.0, ALU.mult, ALU.add).then_inc(S("fg_ready"), 1)
            dve.wait_ge(S("logf_ready"), 1)
            dve.wait_ge(S("hgrn_consts"), 1)
            flat = "p c t -> p (c t)"
            v.tensor_tensor_scan(BC.rearrange(flat), cmask.rearrange(flat), Fg.rearrange(flat), 0.0, ALU.mult, ALU.add) \
                .then_inc(S("bc_ready"), 1)
            pr = (slice(None), slice(None), slice(0, TP))
            dve.wait_ge(S("e_ready"), 1)
            TT(Q[pr], Q[pr], E[pr], ALU.mult).then_inc(S("e_used"), 1)
            dve.wait_ge(S("e_ready"), 2)
            link(TT(Fg[pr], K[pr], E[pr], ALU.mult))
            for c in range(DC):
                last = TT(E[:, c, 0:TP].rearrange("p (k t) -> p k t", k=4),
                          BC[:, c, 63:TP:64].unsqueeze(2).broadcast_to([P, 4, 64]),
                          BC[:, c, 0:TP].rearrange("p (k t) -> p k t", k=4), ALU.subtract)
            last.then_inc(S("e_used"), 1)
            dve.wait_ge(S("e_ready"), 3)
            TT(K[pr], K[pr], E[pr], ALU.mult).then_inc(S("k_decayed"), 1)
            for hq in range(2):
                b = tile(n_of("att", hq)).rearrange("p (h j t) -> p h j t", h=4, j=2)
                for q in range(2):
                    rows = slice(64 * q, 64 * q + 64)
                    last = v.copy_predicated(att[rows, 4 * hq:4 * hq + 4, :, 64 * q:64 * q + 64],
                                             triu[rows, 64 * q:64 * q + 64].bitcast(U32).unsqueeze(1).unsqueeze(1)
                                             .broadcast_to([64, 4, 2, 64]), b[rows, :, :, :])
                last.then_inc(empty["v"], 1)
            for ch in range(4):
                for half in range(2):
                    b = tile(n_of("upd", 2 * ch + half))
                    if ch:
                        dve.wait_ge(empty["v"], emptied(n_of("upd", 2 * ch - 2 + half))[1])
                    for c in range(4):
                        h = 4 * half + c
                        if ch:
                            last = STT(out=st[ch][:, h, :], in0=st[ch - 1][:, h, :], scalar=etot[:, h, ch:ch + 1],
                                       in1=b[:, c * P:(c + 1) * P], op0=ALU.mult, op1=ALU.add)
                        else:
                            last = v.tensor_copy(st[0][:, h, :], b[:, c * P:(c + 1) * P])
                    last.then_inc(empty["v"], 1)
            dve.wait_ge(empty["v"], emptied(n_of("upd", 7))[1])
            v.sem_inc(S("s4_ready"), 1)
            for b_ in range(NB):
                for half in range(2):
                    b = tile(n_of("vB", 2 * b_ + half))
                    if b_ and half == 0:
                        dve.wait_ge(S("h_updated"), b_)
                    TT(tsc, split(b, 4), K[:, 4 * half:4 * half + 4, TP + b_:TP + b_ + 1].broadcast_to([P, 4, P]), ALU.mult) \
                        .then_inc(empty["v"], 1)
                    dve.wait_ge(empty["v"], emptied(n_of("vB", 2 * b_ + half))[1])
                    dve.wait_ge(S("h0_decayed"), b_ + 1)
                    sl = st[b_ % 3][:, 4 * half:4 * half + 4, :]
                    ins = TT(sl, sl, tsc, ALU.add)
                    link(ins) if half == 0 else ins.then_inc(S("h_updated"), 1)
            dve.wait_ge(S("hgrn_read"), NB)
            dve.wait_ge(S("h_updated"), NB)
            v.tensor_copy(E[:, :, TP:T], split(ps[:, 7, 64:128], DC)).then_inc(S("ho_samples"), 1)
            dve.wait_ge(empty["a"], emptied(n_of("hn", 7))[1])
            link(v.reciprocal(BC, BC))
            for c in range(DC):
                last = STT(out=E[:, c, :], in0=E[:, c, :], scalar=par[:, CN + c:CN + c + 1], in1=BC[:, c, :],
                           op0=ALU.mult, op1=ALU.mult)
            link(last)
            TT(E, E, G, ALU.mult).then_inc(S("ho_ready"), 1)
            attention(1, 7, 8)
            b = tile(n_of("logit"))
            dve.wait_ge(empty["a"], emptied(n_of("htok", 5))[1])
            link(v.memset(rtf[:, 0:330], 0.0))
            for g, (t0, nt) in enumerate(GROUPS):
                last = v.tensor_copy(lg[0:nt, g, :], b[0:nt, 8 * g:8 * g + 8])
            last.then_inc(empty["v"], 1)
            dve.wait_ge(empty["v"], emptied(n_of("logit"))[1])
            for g in range(3):
                last = v.max(top[:, g, :], lg[:, g, :])
            link(last)
            for g in range(3):
                v.max_index(topi[:, g, :], top[:, g, :], lg[:, g, :])
            link(TT(tw[:, :, 0], top[:, :, 1], top[:, :, 0], ALU.subtract))
            v.tensor_copy(topf, topi).then_inc(S("top_diff"), 1)
            dve.wait_ge(S("top_diff"), 1)
            for g in range(3):
                for q in range(2):
                    last = TS(oh[:, 2 * g + q, :], iota[:, 0:8], topf[:, g, q:q + 1], None, ALU.is_equal)
            link(last)
            TT(msk, oh[:, 0:6:2, :], oh[:, 1:6:2, :], ALU.add).then_inc(S("mask_ready"), 1)
            dve.wait_ge(S("top_exp"), 1)
            link(TS(tw[:, :, 2], tw[:, :, 1], 1.0, None, ALU.add))
            link(v.reciprocal(tw[:, :, 3], tw[:, :, 2]))
            link(TT(tw[:, :, 0], tw[:, :, 3], tw[:, :, 1], ALU.mult))
            for g in range(3):
                last = TS(gat[:, g, :], oh[:, 2 * g, :], tw[:, g, 3:4], None, ALU.mult)
            link(last)
            for g in range(3):
                last = STT(out=gat[:, g, :], in0=oh[:, 2 * g + 1, :], scalar=tw[:, g, 0:1], in1=gat[:, g, :],
                           op0=ALU.mult, op1=ALU.add)
            link(last)
            b = tile(n_of("posn"))
            v.tensor_copy(table[:, :, 0:3], split(b[:, 0:24], 3).rearrange("p g e -> p e g"))
            v.tensor_copy(table[:, :, 3:6], msk.rearrange("p g e -> p e g"))
            v.tensor_copy(table[:, :, 6:9], gat.rearrange("p g e -> p e g"))
            v.tensor_reduce(cmx[:, 0:1], b[:, 24:32], X, ALU.max).then_inc(empty["v"], 1)
            dve.wait_ge(empty["v"], emptied(n_of("posn"))[1])
            link(TS(cmx[:, 1:2], cmx[:, 0:1], float(P), 1.0, ALU.is_gt, ALU.add))
            link(TS(cmx[:, 2:3], cmx[:, 0:1], float(2 * P), None, ALU.is_gt))
            link(TT(rounds, cmx[:, 1:2], cmx[:, 2:3], ALU.add))
            v.tensor_copy(rounds_i, rounds).then_inc(S("rounds_ready"), 1)
            v.sem_inc(S("hs_ready"), NSL)
            v.sem_inc(S("lo_made"), 2 * MRING)
            v.sem_inc(S("acc_added"), 1)
            dve.wait_ge(S("rounds_ready"), 1)
            dve.wait_ge(S("experts_may_start"), 1)
            rounds_v = nc.values_load(rounds_i[0:1, 0:1], engines=[mybir.EngineType.DVE], min_val=1, max_val=3)
            with dve.Fori(0, rounds_v) as r:
                with dve.Fori(0, NE) as e:
                    it = dve.snap(r * NE + e)
                    v.tensor_copy(cur.unsqueeze(1), table[:, bass.ds(e, 1), :]).then_inc(S("cur_ready"), 1)
                    dve.wait_ge(S("cur_ready"), it + 1)
                    for g in range(3):
                        TS(pickg[:, g, :], iota, cur[:, g:g + 1], cur[:, 6 + g:7 + g], ALU.is_equal, ALU.mult)
                        last = TS(pick[:, g, :], iota, cur[:, g:g + 1], cur[:, 3 + g:4 + g], ALU.is_equal, ALU.mult)
                    last.then_inc(S("pick_ready"), 1)
                    for q in range(NQ):
                        dve.wait_ge(S("hi_made"), it * NQ + q + 1)
                        TT(wr_[:, q % QRING, 1, :], quarter(q), wr_[:, q % QRING, 0, :].bitcast(F32), ALU.subtract) \
                            .then_inc(S("lo_made"), 1)
                        if q == QRING - 1:
                            for half in range(2):
                                cols = slice(half * 512, (half + 1) * 512)
                                dve.wait_ge(S("xe_hi_made"), it * 2 + half + 1)
                                last = TT(xe_lo[:, cols], ps[:, 6 + half, :], xe_hi[:, cols].bitcast(F32), ALU.subtract)
                            last.then_inc(S("xe_ready"), 1)
                        kind, s, i = QUARTERS[q - QRING] if q >= QRING else ("", 0, 0)
                        if kind == "up" and i == 3:
                            dve.wait_ge(S("quarter_used"), it * NQ + q + 1)
                            dve.wait_ge(S("silu_done"), it * NSL + s + 1)
                            TT(hs[s % 2], sg[s % 2], ps[:, 2 * (s % 2) + 1, :], ALU.mult).then_inc(S("hs_ready"), 1)
                        if q - QRING in TURN:
                            s = TURN[q - QRING]
                            dve.wait_ge(S("hT_hi_made"), it * NSL + s + 1)
                            TT(hT_lo[s % 2], ps[:, 6, :], hT_hi[s % 2].bitcast(F32), ALU.subtract).then_inc(S("hT_ready"), 1)
                    for i in range(6):
                        g, half = i // 2, i % 2
                        nt = GROUPS[g][1]
                        dve.wait_ge(S("scatter_done"), it * 6 + i + 1)
                        sl = acc[0:nt, g, half * 512:(half + 1) * 512]
                        TT(sl, sl, ps[0:nt, 7 - i % 2, :], ALU.add).then_inc(S("acc_added"), 1)
                TS(table[:, :, 0:3], table[:, :, 0:3], -float(P), None, ALU.add).then_inc(S("table_moved"), 1)
                dve.wait_ge(S("table_moved"), r + 1)
            v.sem_inc(S("experts_done"), 1)
            dve.wait_ge(S("gb_loaded"), 16)
            for g, (t0, nt) in enumerate(GROUPS):
                dve.wait_ge(S("y_root"), g + 1)
                link(v.reciprocal(frs[0:nt, g:g + 1], frs[0:nt, 3 + g:4 + g]))
                link(STT(out=acc[0:nt, g, :], in0=acc[0:nt, g, :], scalar=frs[0:nt, g:g + 1], in1=gb[0:nt, :],
                         op0=ALU.mult, op1=ALU.mult))
                dve.wait_ge(S("x_tok_ready"), g + 1)
                TT(acc[0:nt, g, :], acc[0:nt, g, :], x_tok[0:nt, g, :], ALU.add).then_inc(S("y_ready"), 1)


INPUTS = ["x_prompt", "x_sample", "mem_prompt", "cache_mem_k", "cache_mem_v", "state_conv", "state_ssm", "state_hgrn",
          "norm_mix_pre", "norm_mix_post", "norm_x_pre", "norm_x_post", "norm_ffn_pre", "norm_ffn_post", "norm_mem",
          "xa_wq", "xa_wk", "xa_wv", "xa_wo", "ev_w_in", "a_ws", "a_bs", "a_ln_g", "a_ln_b", "b_conv_w", "b_conv_b",
          "b_dt_bias", "b_a_log", "b_d", "b_norm", "ev_w_out", "ffn_w_gate", "ffn_w_up", "ffn_w_down", "od_w_in",
          "hgrn_lb_logits", "c_norm", "od_w_out", "moe_router", "moe_w_gate", "moe_w_up", "moe_w_down"]
OUTPUTS = [("y_prompt", (1, 256, 1024)), ("y_sample", (8, 1, 1024)), ("mem_k", (2, 1, 256, 4, 256)),
           ("mem_v", (2, 1, 256, 4, 256)), ("conv_prompt", (1, 1, 3, 1536)), ("ssm_prompt", (1, 1, 2, 8, 64, 128)),
           ("hgrn_prompt", (1, 1, 8, 128, 128)), ("conv_sample", (1, 8, 3, 1536)),
           ("ssm_sample", (1, 8, 2, 8, 64, 128)), ("hgrn_sample", (1, 8, 8, 128, 128)), ("av_sample", (1, 8, 1, 1024))]


def kernel(**inputs):
    import numpy as np
    import concourse.bacc as bacc
    from concourse.bass_utils import run_bass_kernel_spmd

    nc = bacc.Bacc("TRN2", target_bir_lowering=False, num_devices=1)
    arrays, a, o = {}, {}, {}
    for name in INPUTS:
        x = np.ascontiguousarray(inputs[name])
        arrays[f"in_{name}"] = x
        a[name] = nc.dram_tensor(f"in_{name}", x.shape, mybir.dt.from_np(x.dtype), kind="ExternalInput").ap()
    for name, shape in OUTPUTS:
        o[name] = nc.dram_tensor(f"out_{name}", shape, F32, kind="ExternalOutput").ap()
    program(nc, a, o)
    r = run_bass_kernel_spmd(nc, [arrays], core_ids=[0])
    return tuple(r.results[0][f"out_{name}"] for name, _ in OUTPUTS)
```

```python
from contextlib import ExitStack

import concourse.bass as bass
from concourse import mybir

ALU = mybir.AluOpType
ACT = mybir.ActivationFunctionType
F32 = mybir.dt.float32
F32R = mybir.dt.float32r
U32 = mybir.dt.uint32
I32 = mybir.dt.int32
X = mybir.AxisListType.X

P = 128
D = 1024
DC = D // P
TP = 256
NB = 8
T = TP + NB
GROUPS = [(0, P), (P, P), (TP, NB)]
EPS = 1e-6
ARENA = 40784
MEM = 256
XH = 4
SSM_HEADS = 16
CONV_CH = 1536
CC = CONV_CH // P
FD = 2816
FC = FD // P
FGROUPS = [4, 4, 4, 4, 4, 2]
NE = 8
FE = 3584
SL = 512
NSL = FE // SL
KB = 4
BLK = KB * SL
RING = 2
MRING = 7
QF = BLK // 2
QRING = 4
ORDER = [("gate", 0), ("up", 0)]
for _s in range(1, NSL):
    ORDER += [("gate", _s), ("up", _s), ("down", _s - 1)]
ORDER += [("down", NSL - 1)]
QUARTERS = [(kind, s, i) for kind, s in ORDER for i in range(4)]
NQ = len(QUARTERS)
NBLK = NQ // 2
assert NBLK % MRING == 0 and NQ % QRING == 0
LAST = {(kind, s): q for q, (kind, s, i) in enumerate(QUARTERS) if i == 3}
TURN = {LAST["up", s + 1] - 2 if s + 1 < NSL else LAST["down", NSL - 2]: s for s in range(NSL)}
SCATTER, TURN_PLACES, GATHER = list(range(2, 8)), 10, LAST["up", NSL - 1]
SPLIT = {"q0", "q1", "f", "q", "i", "g"} | {f"{kind}{i}" for kind in ("gate", "up") for i in range(6)}
SPLIT_NORMS = (2, 4, 6, 8)
BIG = 1e30


def program(nc, a, o):
    with ExitStack() as ctx:
        ar = ctx.enter_context(nc.sbuf_tensor("arena", [P, ARENA], F32))
        wr_ = ctx.enter_context(nc.sbuf_tensor("weight_parts", [P, QRING, 2, QF], F32R))
        xr_ = ctx.enter_context(nc.sbuf_tensor("token_parts", [P, 4224], F32R))
        ps = ctx.enter_context(nc.psum_tensor("banks", [P, 8, 512], F32))
        made = {}

        def S(name):
            if name not in made:
                made[name] = ctx.enter_context(nc.semaphore(name))
            return made[name]

        def at(off, n, parts=P):
            return ar[0:parts, off:off + n]

        def split(ap, c):
            return ap.rearrange("p (c t) -> p c t", c=c)

        def slot(s):
            return at(s * BLK, BLK)

        SC = RING * BLK
        PERS = 28684
        pos = [PERS]

        def keep(n, parts=P):
            pos[0] += n
            assert pos[0] <= ARENA
            return at(pos[0] - n, n, parts)

        XT = split(keep(DC * T), DC)
        HT = split(keep(DC * T), DC)
        MT = split(keep(DC * T), DC)
        memh = split(keep(DC * MEM), DC)
        ident, ones, triu, tris, mneg, iota = (keep(P) for _ in range(6))
        onehot = split(keep(NB * P, NB), NB)
        head_of = keep(D, SSM_HEADS)
        bsr = ar[32:33, pos[0] - D:pos[0]]
        par = keep(220)
        rs = keep(T)
        small = keep(400)
        eps_c = small[:, 399:400]

        def gain(kind, layer, c):
            return par[:, kind * 16 + layer * 8 + c:kind * 16 + layer * 8 + c + 1]

        MIX_PRE, MIX_POST, X_PRE, X_POST, F_PRE, F_POST, MEM_G = range(7)
        LNG, LNB, BN, CN, LB, CB, CW = 112, 120, 128, 136, 144, 160, 172

        U = split(at(SC, 2112), DC)
        Z = split(at(SC + 2112, 2112), DC)
        UZ = split(at(SC, 4224), 16)
        V = split(at(SC + 4224, 2112), DC)
        raw = split(at(SC + 6336, CC * 259), CC)
        raws = at(SC + 9444, CC * 32).rearrange("p (c k b) -> p c k b", c=CC, k=4)
        XBC = split(at(SC + 9828, CC * T), CC)
        x_tm = split(at(SC + 12996, 2048), 2)
        b_tm = split(at(SC + 15044, 512), 2)
        bc_s = at(SC + 15556, 512, NB)
        CBT = split(at(SC + 16068, 512), 4)
        Lm = [at(SC + 16580 + 512 * i, 512) for i in range(2)]
        ecs = at(SC + 17604, 512)
        Ce = [at(SC + 18116 + 512 * i, 512) for i in range(2)]
        xw = at(SC + 19140, 1024)
        prev = at(SC + 20164, 1024)
        s0 = [split(at(SC + o_, 1024), DC) for o_ in (21188, 22212, 20164, 19140)]
        t2 = split(at(SC + 23236, 1024), DC)
        conv_tail = at(SC + 24260, CC * 11)
        conv_o = at(SC + 2112, CONV_CH, 11)
        xin = at(SC, 3072).rearrange("p (g n) -> p g n", g=3)
        av_o = at(SC + 6336, D, NB)
        sfin = at(SC + 7360, 1024)
        ssm_o = split(at(SC + 8384, 1024), DC)
        v_tm = at(PERS + 2 * 2112, 2048).rearrange("p (g n) -> p g n", g=2)
        ws = at(PERS + 3 * 2112, 1024)
        wsT = split(at(PERS + 3 * 2112 + 1024, 1024), DC)
        par_in = [at(SC + 4000, P, 112), at(SC + 4128, P, 108)]
        st_in = at(SC + 4256, CONV_CH, 24)
        dcol = small[:, 0:8]
        dtb, alog = small[0:16, 8:9], small[0:16, 9:10]
        aexp = small[0:16, 10:11]
        mrs = small[:, 16:20]
        lb1, omlb = small[:, 24:32], small[:, 32:40]
        wb = small[:, 40:56]
        dd = small[:, 64:128].rearrange("p (j i h) -> p j i h", j=2, i=2)
        cs = small[:, 128:160].rearrange("p (j h) -> p j h", j=2)
        wdec = small[:, 160:192].rearrange("p (j h) -> p j h", j=2)
        cdec = small[:, 192:224].rearrange("p (j h) -> p j h", j=2)
        exc = small[:, 224:352].rearrange("p (c k) -> p c k", c=DC)
        exd = small[0:16, 352:368]
        rsg = split(at(SC + 16580, 2 * T), 2)
        v_sq = split(at(SC + 12996, 2112), DC)
        ysum = split(at(SC + 24392, 64), DC)
        dtr = [at(SC + 18116 + T * i, T, 16) for i in range(7)]

        QT = split(at(SC, 2112), DC)
        OT = split(at(SC + 2112, 2112), DC)
        MG = split(at(SC + 4224, 2048), DC)
        k_tm = at(SC + 6272, 2048).rearrange("p (m n) -> p m n", m=2)
        vm_tm = at(SC + 8320, 2048).rearrange("p (m n) -> p m n", m=2)
        KT = split(at(SC + 10368, 2048), DC)
        PR = at(SC + 12416, 2048).rearrange("p (g h m) -> p g h m", g=2, h=XH)
        PT = at(SC + 10368, 2048).rearrange("p (h m t) -> p h m t", h=XH, m=2)
        kc = [at(SC + 14464 + 2048 * i, 2048).rearrange("p (m n) -> p m n", m=2) for i in range(2)]
        vc = [at(SC + 18560 + 2048 * i, 2048).rearrange("p (m n) -> p m n", m=2) for i in range(2)]
        vc += kc
        mem_in = at(PERS + 2112, 2048).rearrange("p (m n) -> p m n", m=2)
        q_s = at(SC + 12416, D, NB)
        junk = at(SC + 13440, 256)
        scs = small[:, 64:128].rearrange("p (m k) -> p m k", m=2)
        mx, sm = small[:, 128:136], small[:, 136:144]
        smx, ssm = small[0:32, 144:145], small[0:32, 145:146]
        p_s = at(SC + 2112, 256, 32)
        pts = at(SC + 4224, 512).rearrange("p (k b n) -> p k b n", k=2 * XH, b=NB)
        o_tm = at(SC + 4736, D, NB).rearrange("p (h n) -> p h n", h=XH)

        hid = split(at(SC, FC * T), FC)
        gtmp = [at(SC + 6000 + T * i, T) for i in range(4)]

        Q, Fg, I, G, K, E, BC = (split(at(SC + 2112 * i, 2112), DC) for i in range(7))
        cmask = MT
        kp_tm = at(PERS + 2 * 2112, 2048).rearrange("p (g n) -> p g n", g=2)
        i_tm = at(SC + 14784, 2048).rearrange("p (g n) -> p g n", g=2)
        att = at(SC + 16832, 2048).rearrange("p (h j t) -> p h j t", h=8, j=2)
        st = [split(at(SC + 18880 + 1024 * i, 1024), DC) for i in range(4)]
        q_one = at(SC + 22976, 512).rearrange("p (h b n) -> p h b n", h=8, b=NB)
        i_s = at(SC + 23488, D, NB)
        etot = small[:, 64:96].rearrange("p (c k) -> p c k", c=DC)
        es = small[:, 96:160].rearrange("p (c k) -> p c k", c=DC)

        ME = SC + 12288
        h_tok = at(ME, 3072).rearrange("p (g n) -> p g n", g=3)
        acc = at(ME + 3072, 3072).rearrange("p (g n) -> p g n", g=3)
        x_hi, x_lo = (split(xr_[:, i * 2112:(i + 1) * 2112], DC) for i in range(2))
        xe_hi, xe_lo = (xr_[:, i * 1024:(i + 1) * 1024] for i in range(2))
        hT_hi, hT_lo = ([xr_[:, 2048 + (2 * b + i) * 512:2560 + (2 * b + i) * 512] for b in range(2)] for i in range(2))
        sg = [at(ME + 7168 + 512 * i, 512) for i in range(2)]
        hs = [at(ME + 8192 + 512 * i, 512) for i in range(2)]

        pick = split(at(ME + 10240, 384), 3)
        pickg = split(at(ME + 10624, 384), 3)
        pickT = at(ME + 11008, T)
        oe = at(ME + 11272, D)

        def quarter(q):
            return slot(q // 2 % MRING)[:, (q % 2) * QF:(q % 2 + 1) * QF]

        wr = split(small[:, 0:64], DC)
        x_tok = at(0, 3072).rearrange("p (g n) -> p g n", g=3)
        gb = at(3072, D)
        ysq = at(4096, D)
        rtf = at(PERS + 2112, 2112)
        lg = split(rtf[:, 0:24], 3)
        top = split(rtf[:, 24:48], 3)
        topi = split(rtf[:, 48:72].bitcast(U32), 3)
        topf = split(rtf[:, 72:96], 3)
        tw = split(rtf[:, 96:108], 3)
        oh = split(rtf[:, 108:156], 6)
        msk = split(rtf[:, 156:180], 3)
        gat = split(rtf[:, 180:204], 3)
        posn = split(rtf[:, 204:228], 3)
        table = rtf[:, 400:400 + 9 * (3 * NE + 1)].rearrange("p (e k) -> p e k", e=3 * NE + 1)
        cur = rtf[:, 300:309]
        cmx = rtf[:, 317:320]
        rounds = rtf[:, 320:321]
        rounds_i = rtf[:, 321:322].bitcast(I32)
        steps_i = rtf[:, 322:323].bitcast(I32)
        frs = rtf[:, 324:330]

        tiles, first = [], {}

        def plan(name, n, who="a"):
            first[name] = len(tiles)
            tiles.extend(who[i % len(who)] for i in range(n))

        plan("xT", DC), plan("par", 1, "v"), plan("st", 1, "v")
        plan("xbc", CC), plan("dt", 1, "v"), plan("v", 8), plan("tr0", 9), plan("cb", 1)
        plan("z", 8), plan("vmean", 1, "v")
        plan("csB", 6, "v"), plan("stA", 4, "v"), plan("csC", 2, "v"), plan("sfT", 2)
        plan("u", 8), plan("wsT", 2, "v"), plan("vtm", 4), plan("avT", 2)
        plan("mixA", 8, "v")
        plan("out0", 8)
        for l in range(2):
            plan(f"k{l}", 4), plan(f"q{l}", 8), plan(f"qs{l}", 2), plan(f"kT{l}", 8), plan(f"vm{l}", 4)
            plan(f"sT{l}", 1), plan(f"scA{l}", 2), plan(f"pTs{l}", 1, "v"), plan(f"scB{l}", 2)
            plan(f"pT{l}", 4), plan(f"pv{l}", 8), plan(f"xo{l}", 8)
            if l == 0:
                for i, n in enumerate(FGROUPS):
                    plan(f"gate{i}", n), plan(f"up{i}", n, "v")
                plan("down", 8)
                plan("f", 8), plan("q", 8), plan("i", 8), plan("g", 8)
                plan("iT", 4), plan("isT", 2), plan("kT", 4), plan("att", 2, "v")
                plan("upd", 8, "v"), plan("ho", 8), plan("hn", 8), plan("vB", 16, "v"), plan("hns", 1)
                plan("out1", 8)
        plan("htok", 6), plan("logit", 1, "v"), plan("posn", 1, "v")

        def n_of(name, i=0):
            return first[name] + i

        def n_sc(l, i):
            return n_of(f"scA{l}", i) if i < 2 else n_of(f"scB{l}", i - 2)

        def n_csb(i):
            return n_of("csB", i) if i < 6 else n_of("csC", i - 6)

        def bank(n):
            return ps[:, n % 4, :]

        def emptied(n):
            return tiles[n], sum(w == tiles[n] for w in tiles[:n + 1])

        empty = {"a": S("tile_emptied_by_act"), "v": S("tile_emptied_by_dve")}
        tile_done = S("tile_done")
        part_used = S("block_part_used")

        blocks = []
        parts = [0]
        quarters = []
        lo_made = S("dense_lo_made")

        def weights(name, w, tiles_per=None):
            k, n = w.shape
            t = first[name]
            for c0 in range(0, n, SL):
                cols = min(SL, n - c0)
                nt = (cols + P - 1) // P if tiles_per is None else tiles_per
                for k0 in range(0, k, KB * P):
                    rows = min(KB * P, k - k0)
                    src = w[k0:k0 + rows, c0:c0 + cols].rearrange("(k p) n -> p k n", p=P)
                    if name in SPLIT:
                        for half in range(2):
                            if k0 + rows == k and half:
                                free = (tile_done, t + nt)
                            else:
                                parts[0] += 1
                                free = (part_used, parts[0])
                            quarters.append((len(blocks), half, cols, free, t))
                        blocks.append((src, rows // P, cols, (lo_made, len(quarters)), None))
                    elif k0 + rows == k:
                        blocks.append((src, rows // P, cols, (tile_done, t + nt), t + nt))
                    else:
                        parts[0] += 1
                        blocks.append((src, rows // P, cols, (part_used, parts[0]), t + nt))
                t += nt

        w0, fg_, fu_ = a["ev_w_in"][0], a["ffn_w_gate"][0], a["ffn_w_up"][0]
        weights("xbc", w0[:, 3072:4608])
        weights("dt", w0[:, 4608:4624])
        weights("v", w0[:, 1024:2048])
        weights("z", w0[:, 2048:3072])
        weights("u", w0[:, 0:1024])
        weights("out0", a["ev_w_out"][0])
        for l in range(2):
            weights(f"k{l}", a["xa_wk"][l], tiles_per=2)
            weights(f"q{l}", a["xa_wq"][l])
            weights(f"vm{l}", a["xa_wv"][l], tiles_per=2)
            weights(f"xo{l}", a["xa_wo"][l])
            if l == 0:
                for i, n in enumerate(FGROUPS):
                    weights(f"gate{i}", fg_[:, i * SL:i * SL + n * P])
                    weights(f"up{i}", fu_[:, i * SL:i * SL + n * P])
                weights("down", a["ffn_w_down"][0])
                wi = a["od_w_in"][0]
                weights("f", wi[:, 1024:2048])
                weights("q", wi[:, 0:1024])
                weights("i", wi[:, 2048:3072])
                weights("g", wi[:, 3072:4096])
                weights("out1", a["od_w_out"][0])

        def needed(n):
            return sum(q[4] <= n for q in quarters)

        def ahead_of(n, made, lead):
            goal = needed(n)
            while goal < min(needed(n) + lead, len(quarters)):
                old = quarters[goal][0] - RING
                if old >= 0 and blocks[old][4] is not None and blocks[old][4] > n:
                    break
                goal += 1
            return range(made, max(made, goal))

        def quarter_of(q):
            b, half, cols, _, _ = quarters[q]
            raw_q = slot(b % RING)[:, half * 2 * cols:(half + 1) * 2 * cols]
            return raw_q, wr_[:, q % QRING, 0, 0:2 * cols], wr_[:, q % QRING, 1, 0:2 * cols]

        loaded = [S(f"slot{s}_loaded") for s in range(RING)]
        mloaded = loaded + [S(f"expert_slot{s}_loaded") for s in range(RING, MRING)]
        mloaded_before = [16 * sum(b % RING == s for b in range(len(blocks))) for s in range(RING)] + [0] * (MRING - RING)

        NORMS = [(MIX_PRE, 0, 1), (MIX_POST, 0, 0), (X_PRE, 0, 1), (X_POST, 0, 0), (F_PRE, 0, 1),
                 (F_POST, 0, 0), (MIX_PRE, 1, 1), (MIX_POST, 1, 0), (X_PRE, 1, 1), (X_POST, 1, 0),
                 (F_PRE, 1, 1)]
        posts = [n for n, (_, _, pre) in enumerate(NORMS) if not pre]
        PRES = [n for n, (_, _, pre) in enumerate(NORMS) if pre]

        block = ctx.enter_context(nc.Block())

        @block.sync
        def _(sp):
            nc.sync.dma_start(xin[:, 0:2, :], a["x_prompt"][0].rearrange("(g p) n -> p g n", p=P)) \
                .then_inc(S("x_loaded"), 16)
            nc.sync.dma_start(xin[0:NB, 2, :], a["x_sample"][:, 0, :]).then_inc(S("x_loaded"), 16)
            names = ["norm_mix_pre", "norm_mix_post", "norm_x_pre", "norm_x_post", "norm_ffn_pre",
                     "norm_ffn_post", "norm_mem"]
            for i, name in enumerate(names):
                nc.sync.dma_start(par_in[0][i * 16:i * 16 + 16, :], a[name].rearrange("l (c p) -> (l c) p", p=P)) \
                    .then_inc(S("par_loaded"), 16)
            r = 0
            for name in ("a_ln_g", "a_ln_b", "b_norm", "c_norm", "hgrn_lb_logits", "b_conv_b"):
                v = a[name].rearrange("l (c p) -> (l c) p", p=P)
                nc.sync.dma_start(par_in[1][r:r + v.shape[0], :], v).then_inc(S("par_loaded"), 16)
                r += v.shape[0]
            nc.sync.dma_start(par_in[1][r:r + 48, :], a["b_conv_w"][0].rearrange("k (c p) -> (k c) p", p=P)) \
                .then_inc(S("par_loaded"), 16)
            nc.sync.dma_start(st_in, a["state_conv"][0].rearrange("b k n -> (b k) n")).then_inc(S("st_loaded"), 16)
            for b, (src, kc_, cols, _, _) in enumerate(blocks):
                if b >= RING:
                    sem, value = blocks[b - RING][3]
                    sp.wait_ge(sem, value)
                dst = split(slot(b % RING)[:, 0:kc_ * cols], kc_)
                nc.sync.dma_start(dst, src).then_inc(loaded[b % RING], 16)
                if b == 8:
                    nc.sync.dma_start(bsr, a["a_bs"].rearrange("o h t -> o (h t)")).then_inc(S("bs_loaded"), 16)
                    nc.sync.dma_start(ws.rearrange("p (h s) -> p h s", h=8), a["a_ws"][0].rearrange("h t s -> t h s")) \
                        .then_inc(S("ws_loaded"), 16)
            for b in range(len(blocks) - RING, len(blocks)):
                sem, value = blocks[b][3]
                sp.wait_ge(sem, value)
            sp.wait_ge(S("experts_may_start"), 1)
            sp.wait_ge(S("rounds_ready"), 1)
            rounds_v = nc.values_load(rounds_i[0:1, 0:1], engines=[mybir.EngineType.SP], min_val=1, max_val=3)
            with sp.Fori(0, rounds_v) as r:
                with sp.Fori(0, NE) as e:
                    it = sp.snap(r * NE + e)
                    for j in range(NBLK):
                        kind, s, i = QUARTERS[2 * j]
                        sp.wait_ge(S("lo_made"), it * NQ + 2 * j + 2)
                        if kind == "down":
                            src = a["moe_w_down"][0, bass.ds(e, 1), s * SL + i * P:s * SL + (i + 2) * P, :]
                        else:
                            w = a["moe_w_gate"] if kind == "gate" else a["moe_w_up"]
                            src = w[0, bass.ds(e, 1), 2 * i * P:2 * (i + 2) * P, s * SL:(s + 1) * SL]
                        rows = 2 if kind == "down" else KB
                        nc.sync.dma_start(split(slot(j % MRING), rows), src.rearrange("o (k p) n -> p (o k) n", p=P)) \
                            .then_inc(mloaded[j % MRING], 16)

        @block.gpsimd
        def _(pool):
            g = nc.gpsimd
            made_ = [0]

            def link(ins):
                made_[0] += 1
                ins.then_inc(S("pool_step"), 1)
                pool.wait_ge(S("pool_step"), made_[0])

            for t in (ident, ones, triu, tris, mneg):
                g.memset(t, 1.0 if t is ones or t is triu or t is tris else 0.0)
            g.memset(onehot, 0.0)
            g.memset(head_of, 1.0)
            link(g.memset(raw[:, :, 0:3], 0.0))
            link(g.affine_select(out=ident, in_=ident, compare_op=ALU.not_equal, fill=1.0, base=0,
                                 pattern=[[-1, P]], channel_multiplier=1))
            g.affine_select(out=triu, in_=triu, compare_op=ALU.is_ge, fill=0.0, base=0,
                            pattern=[[1, P]], channel_multiplier=-1)
            g.affine_select(out=tris, in_=tris, compare_op=ALU.is_gt, fill=0.0, base=0,
                            pattern=[[1, P]], channel_multiplier=-1)
            g.affine_select(out=mneg, in_=mneg, compare_op=ALU.is_ge, fill=-BIG, base=0,
                            pattern=[[1, P]], channel_multiplier=-1)
            g.iota(iota, pattern=[[1, P]], base=0, channel_multiplier=0, allow_small_or_imprecise_dtypes=True)
            g.affine_select(out=onehot, in_=onehot, compare_op=ALU.not_equal, fill=1.0, base=0,
                            pattern=[[-1, NB], [0, P]], channel_multiplier=1)
            link(g.affine_select(out=head_of, in_=head_of, compare_op=ALU.is_ge, fill=0.0, base=0,
                                 pattern=[[1, D]], channel_multiplier=-64))
            g.affine_select(out=head_of, in_=head_of, compare_op=ALU.is_ge, fill=0.0, base=63,
                            pattern=[[-1, D]], channel_multiplier=64).then_inc(S("consts_ready"), 1)
            for j in range(2):
                g.dma_start(dcol[64 * j:64 * j + 64, :],
                            a["b_d"][0:1, :].rearrange("o (c j) -> o j c", j=2)[:, j, :].broadcast_to([64, 8]),
                            allow_slow_non_contiguous=True) \
                    .then_inc(S("small_loaded"), 16)
            g.dma_start(dtb, a["b_dt_bias"].rearrange("o h -> h o"), allow_slow_non_contiguous=True).then_inc(S("small_loaded"), 16)
            g.dma_start(alog, a["b_a_log"].rearrange("o h -> h o"), allow_slow_non_contiguous=True).then_inc(S("small_loaded"), 16)
            g.dma_start(o["conv_sample"][0][:, 0:2, :], a["state_conv"][0][:, 1:3, :]).then_inc(S("stored"), 16)

            ssm_in = a["state_ssm"][0].rearrange("b g h p n -> b (g h p) n")
            ssm_out = o["ssm_sample"][0].rearrange("b g h p n -> b (g h p) n")

            def load_s0(b):
                if b >= 4:
                    pool.wait_ge(S(f"state_stored{b % 2}"), 16 * ((b - 4) // 2 + 1))
                g.dma_start(s0[b % 4], ssm_in[b].rearrange("(c p) n -> p c n", p=P)).then_inc(S(f"state_loaded{b % 4}"), 16)

            load_s0(0)
            load_s0(1)
            pool.wait_ge(empty["a"], emptied(n_of("tr0", 2))[1])
            g.dma_start(o["conv_prompt"][0, 0], conv_o[0:3, :]).then_inc(S("conv_stored"), 16)
            g.dma_start(o["conv_sample"][0][:, 2, :], conv_o[3:11, :]).then_inc(S("conv_stored"), 16)
            pool.wait_ge(S("exc_ready"), 1)
            for b in range(NB + 1):
                if b < NB:
                    pool.wait_ge(S(f"state_loaded{b % 4}"), 16 * (b // 4 + 1))
                    g.tensor_tensor(s0[b % 4], s0[b % 4], exc[:, :, b:b + 1].broadcast_to([P, DC, P]), ALU.mult) \
                        .then_inc(S("s0_decayed"), 1)
                if b == 0:
                    pool.wait_ge(tile_done, n_of("sfT") + 1)
                    load_s0(2), load_s0(3)
                else:
                    pool.wait_ge(S("s0_used"), b)
                    g.dma_start(ssm_out[b - 1].rearrange("(c p) n -> p c n", p=P), s0[(b - 1) % 4]) \
                        .then_inc(S(f"state_stored{(b - 1) % 2}"), 16)
                    if 4 <= b + 2 < NB:
                        load_s0(b + 2)
            pool.wait_ge(empty["a"], emptied(n_of("sfT", 1))[1])
            g.dma_start(o["ssm_prompt"][0, 0].rearrange("g h p n -> (g h p) n").rearrange("(c p) n -> p c n", p=P),
                        ssm_o).then_inc(S("stored"), 16)
            pool.wait_ge(empty["a"], emptied(n_of("avT", 1))[1])
            g.dma_start(o["av_sample"][0][:, 0, :], av_o).then_inc(S("stored"), 16)

            pool.wait_ge(S("gate_done"), 1)
            g.dma_start(mem_in, a["mem_prompt"][0].rearrange("(m p) n -> p m n", p=P)).then_inc(S("mem_loaded"), 16)
            for l in range(2):
                if l == 0:
                    pool.wait_ge(S("memh_ready"), 1)
                    pool.wait_ge(S("stored"), 48)
                    for j in range(2):
                        pool.wait_ge(S(f"state_stored{j}"), 64)

                for c in range(DC):
                    last = g.tensor_scalar(MG[:, c, :], memh[:, c, :], gain(MEM_G, l, c), None, ALU.mult)
                last.then_inc(S("mem_gain_ready"), 1)
                if l == 1:
                    pool.wait_ge(tile_done, n_of("out1", 7) + 1)
                    pool.wait_ge(S("hgrn_stored"), 16)
                    for j in range(2):
                        pool.wait_ge(S(f"state_stored{j}"), 128)

                def load_k(b):
                    if b >= 2:
                        pool.wait_ge(S("k_cache_used"), NB * l + b - 1)
                    g.dma_start(kc[b % 2], a["cache_mem_k"][l, b].rearrange("(m p) h d -> p m (h d)", p=P)) \
                        .then_inc(S(f"k_cache_loaded{b % 2}"), 16)

                def load_v(b):
                    if 2 <= b < 4:
                        pool.wait_ge(S("k_cache_used"), NB * l + b + 5)
                    elif b >= 4:
                        pool.wait_ge(S("v_cache_used"), NB * l + b - 3)
                    g.dma_start(vc[b % 4], a["cache_mem_v"][l, b].rearrange("(m p) h d -> p m (h d)", p=P)) \
                        .then_inc(S(f"v_cache_loaded{b % 4}"), 16)

                load_k(0), load_k(1), load_v(0), load_v(1)
                pool.wait_ge(empty["a"], emptied(n_of(f"k{l}", 3))[1])
                g.dma_start(o["mem_k"][l, 0].rearrange("(m p) h d -> p m (h d)", p=P), k_tm).then_inc(S("kv_stored"), 16)
                for b in range(2, NB):
                    load_k(b)
                pool.wait_ge(empty["a"], emptied(n_of(f"vm{l}", 3))[1])
                g.dma_start(o["mem_v"][l, 0].rearrange("(m p) h d -> p m (h d)", p=P), vm_tm).then_inc(S("kv_stored"), 16)
                g.memset(pts, 0.0).then_inc(S("pts_zeroed"), 1)
                for b in range(2, NB):
                    load_v(b)
                if l == 0:
                    pool.wait_ge(S("square_sums_done"), 7)
                    g.memset(cmask, 1.0)
                    pool.wait_ge(tile_done, n_of("down", 7) + 1)
                    pool.wait_ge(S("kv_stored"), 32)
                    g.memset(q_one, 0.0)
                    link(g.memset(att, 0.0))
                    g.memset(cmask[:, :, 0:TP:64], 0.0)
                    g.memset(cmask[:, :, TP:T], 0.0).then_inc(S("hgrn_consts"), 1)
                    pool.wait_ge(S("s4_ready"), 1)
                    g.dma_start(o["hgrn_prompt"][0, 0].rearrange("h k v -> k h v"), st[3]).then_inc(S("hgrn_stored"), 16)
                    pool.wait_ge(tile_done, n_of("ho", 7) + 1)

                    def load_h(b):
                        if b == 3:
                            pool.wait_ge(S("hgrn_stored"), 16)
                        if b >= 4:
                            pool.wait_ge(S(f"state_stored{b % 2}"), 64 + 16 * ((b - 4) // 2 + 1))
                            pool.wait_ge(S("hgrn_read"), b - 3)
                        g.dma_start(st[b % 4], a["state_hgrn"][0, b].rearrange("h k v -> k h v")) \
                            .then_inc(S(f"state_loaded{b % 4}"), 16)

                    load_h(0), load_h(1), load_h(2), load_h(3)
                    for b in range(NB + 1):
                        if b < NB:
                            pool.wait_ge(S(f"state_loaded{b % 4}"), 32 + 16 * (b // 4 + 1))
                            g.tensor_tensor(st[b % 4], st[b % 4], es[:, :, b:b + 1].broadcast_to([P, DC, P]), ALU.mult) \
                                .then_inc(S("h0_decayed"), 1)
                        if b:
                            pool.wait_ge(S("h_updated"), b)
                            g.dma_start(o["hgrn_sample"][0, b - 1].rearrange("h k v -> k h v"), st[(b - 1) % 4]) \
                                .then_inc(S(f"state_stored{(b - 1) % 2}"), 16)
                        if 4 <= b + 2 < NB:
                            load_h(b + 2)
            pool.wait_ge(tile_done, n_of("xo1", 7) + 1)
            pool.wait_ge(S("kv_stored"), 64)
            g.dma_start(wr, a["moe_router"][0].rearrange("(k p) e -> p k e", p=P)).then_inc(S("router_loaded"), 16)
            g.memset(acc, 0.0)
            g.memset(pick, 0.0)
            g.memset(pickT, 0.0)
            g.memset(h_tok[:, 2, :], 0.0).then_inc(S("experts_may_start"), 1)
            pool.wait_ge(S("experts_done"), 1)
            g.dma_start(gb, a["norm_ffn_post"][1:2, :].broadcast_to([P, D])).then_inc(S("gb_loaded"), 16)
            pool.wait_ge(S("y_ready"), 3)
            g.dma_start(o["y_prompt"][0].rearrange("(g p) n -> p g n", p=P), acc[:, 0:2, :]).then_inc(S("stored"), 16)
            g.dma_start(o["y_sample"][:, 0, :], acc[0:NB, 2, :]).then_inc(S("stored"), 16)
            pool.wait_ge(S("conv_stored"), 32)
            for j in range(2):
                pool.wait_ge(S(f"state_stored{j}"), 128)
            pool.wait_ge(S("kv_stored"), 64)
            pool.wait_ge(S("hgrn_stored"), 16)
            pool.wait_ge(S("stored"), 16 * 5)

        @block.tensor
        def _(pe):
            mm, tr = nc.tensor.matmul, nc.tensor.transpose
            at_block = [0]

            def take(n):
                if n >= 4:
                    who, count = emptied(n - 4)
                    pe.wait_ge(empty[who], count)
                return bank(n)

            def next_block():
                b = at_block[0]
                at_block[0] += 1
                pe.wait_ge(loaded[b % RING], 16 * (b // RING + 1))
                _, kc_, cols, _, _ = blocks[b]
                return split(slot(b % RING)[:, 0:kc_ * cols], kc_)

            def project(name, rhs, kchunks, cols, between=None, norm=None):
                n = n_of(name)
                for c0 in range(0, cols, SL):
                    width = min(SL, cols - c0)
                    nt = (width + P - 1) // P
                    for k0 in range(0, kchunks, KB):
                        w = next_block()
                        ks = min(KB, kchunks - k0)
                        for i in range(nt):
                            m = min(P, width - i * P)
                            b = take(n + i) if k0 == 0 else bank(n + i)
                            for k in range(ks):
                                if norm is not None and c0 == 0 and i == 0:
                                    wait_norm(norm, k0 + k + 1)
                                last = mm(b[0:m, 0:T], w[:, k, i * P:i * P + m], rhs[:, k0 + k, :],
                                          start=(k0 + k == 0), stop=(k0 + k == kchunks - 1))
                            if k0 + ks == kchunks:
                                last.then_inc(tile_done, 1)
                            elif i == nt - 1:
                                last.then_inc(part_used, 1)
                            if between is not None:
                                between()
                    n += nt

            at_quarter = [0]

            def project_split(name, cols, norm=None):
                n = n_of(name)
                for c0 in range(0, cols, SL):
                    width = min(SL, cols - c0)
                    nt = width // P
                    for k0 in range(0, DC, 2):
                        q = at_quarter[0]
                        at_quarter[0] += 1
                        pe.wait_ge(lo_made, q + 1)
                        _, hi, lo = quarter_of(q)
                        for i in range(nt):
                            b = take(n + i) if k0 == 0 else bank(n + i)
                            for k in range(2):
                                c = k0 + k
                                if norm is not None and c0 == 0 and i == 0:
                                    pe.wait_ge(S("x_lo_made"), DC * SPLIT_NORMS.index(norm) + c + 1)
                                part = slice(k * width + i * P, k * width + (i + 1) * P)
                                mm(b[:, 0:T], hi[:, part], x_hi[:, c, :], start=(c == 0), stop=False)
                                mm(b[:, 0:T], hi[:, part], x_lo[:, c, :], start=False, stop=False)
                                last = mm(b[:, 0:T], lo[:, part], x_hi[:, c, :], start=False, stop=(c == DC - 1))
                            if k0 + 2 == DC:
                                last.then_inc(tile_done, 1)
                            elif i == nt - 1:
                                last.then_inc(part_used, 1)
                        if k0 % KB == 2:
                            at_block[0] += 1
                    n += nt

            def project_tm(name, lhs, between=None):
                n = n_of(name)
                for c0 in range(0, D, SL):
                    for k0 in range(0, DC, KB):
                        w = next_block()
                        for m in range(2):
                            b = take(n + m) if k0 == 0 else bank(n + m)
                            for k in range(KB):
                                last = mm(b, lhs[:, k0 + k, m * P:(m + 1) * P], w[:, k, :], start=(k0 + k == 0),
                                          stop=(k0 + k == DC - 1))
                            if k0 + KB == DC:
                                last.then_inc(tile_done, 1)
                            elif m:
                                last.then_inc(part_used, 1)
                            if between is not None:
                                between()
                    n += 2

            def transposes(n, items):
                b = take(n)
                col = 0
                for src, p_, f_ in items:
                    last = tr(b[0:f_, col:col + p_], src, ident[0:p_, 0:p_])
                    col += p_
                last.then_inc(tile_done, 1)

            def square_sums(k):
                for c in range(DC):
                    pe.wait_ge(S("squares_ready"), DC * k + c + 1)
                    sq = MT if NORMS[k][2] else HT
                    last = mm(ps[:, 4, 0:T], ones, sq[:, c, :], start=(c == 0), stop=(c == DC - 1))
                last.then_inc(S("square_sums_done"), 1)

            def wait_norm(k, chunks=DC):
                pe.wait_ge(S("normed"), DC * PRES.index(k) + chunks)

            pe.wait_ge(S("consts_ready"), 1)
            pe.wait_ge(S("x_loaded"), 32)
            for c in range(DC):
                transposes(n_of("xT", c), [(xin[0:n, g, c * P:(c + 1) * P], n, P)
                                           for g, (_, n) in enumerate(GROUPS)])
            pe.wait_ge(S("par_loaded"), 16 * 14)
            transposes(n_of("par"), [(par_in[0], 112, P), (par_in[1], 108, P)])
            pe.wait_ge(S("st_loaded"), 16)
            transposes(n_of("st"), [(st_in[:, c * P:(c + 1) * P], 24, P) for c in range(CC)])
            square_sums(0)
            project("xbc", HT, DC, CONV_CH, norm=0)
            project("dt", HT, DC, 16)
            project("v", HT, DC, D)
            n = n_of("tr0")
            for i in range(3):
                pe.wait_ge(S("tail_ready"), 1)
                b = take(n + i)
                for c in range(4):
                    last = tr(b[0:11, c * P:(c + 1) * P], conv_tail[:, (4 * i + c) * 11:(4 * i + c + 1) * 11], ident)
                last.then_inc(tile_done, 1)
            n += 3
            pe.wait_ge(S("xbc_ready"), CC)
            for j in range(2):
                for half in range(2):
                    b = take(n)
                    for c in range(4):
                        last = tr(b[:, c * P:(c + 1) * P], XBC[:, 4 * half + c, j * P:(j + 1) * P], ident)
                    last.then_inc(tile_done, 1)
                    n += 1
            b = take(n)
            for j in range(2):
                for g in range(2):
                    last = tr(b[:, (2 * j + g) * P:(2 * j + g + 1) * P], XBC[:, 8 + g, j * P:(j + 1) * P], ident)
            last.then_inc(tile_done, 1)
            n += 1
            b = take(n)
            for c in range(4):
                last = tr(b[0:NB, c * P:(c + 1) * P], XBC[:, 8 + c, TP:T], ident)
            last.then_inc(tile_done, 1)
            b = take(n_of("cb"))
            for j in range(2):
                for g in range(2):
                    last = mm(b[:, (2 * j + g) * P:(2 * j + g + 1) * P], XBC[:, 8 + g, j * P:(j + 1) * P],
                              XBC[:, 10 + g, j * P:(j + 1) * P], start=True, stop=True)
            last.then_inc(tile_done, 1)
            pe.wait_ge(S("dt_ready"), 1)
            for j in range(2):
                for i in range(2):
                    tr(ps[:, 5, (2 * j + i) * 16:(2 * j + i) * 16 + 16], dtr[i][:, j * P:(j + 1) * P], ident[0:16, 0:16])
            for c in range(DC):
                last = mm(ps[:, 5, 128 + 16 * c:144 + 16 * c], head_of[:, c * P:(c + 1) * P], exd, start=True, stop=True)
            last.then_inc(S("dt_tm_done"), 1)
            project("z", HT, DC, D)
            b = take(n_of("vmean"))
            pe.wait_ge(empty["a"], emptied(n_of("v", 7))[1])
            for c in range(DC):
                last = mm(b[:, 0:T], ones, V[:, c, :], start=(c == 0), stop=(c == DC - 1))
            last.then_inc(tile_done, 1)
            pe.wait_ge(S("dt_tm_ready"), 1)
            for j in range(2):
                mm(ps[:, 6, 16 * j:16 * j + 16], triu, dd[:, j, 1, :], start=True, stop=True)
                last = mm(ps[:, 6, 32 + 16 * j:48 + 16 * j], ones, dd[:, j, 1, :], start=True, stop=True)
            last.then_inc(S("cs_done"), 1)

            def csb(i):
                j, hq = i // 4, i % 4
                b = take(n_csb(i))
                for h in range(4):
                    last = mm(b[:, h * P:(h + 1) * P], dd[:, j, 1, 4 * hq + h:4 * hq + h + 1].broadcast_to([P, P]), triu,
                              start=True, stop=True)
                last.then_inc(tile_done, 1)

            def ssd(i):
                j, hq = i // 4, i % 4
                y = ps[:, 5 + 2 * (i % 2), 0:256]
                pe.wait_ge(S("lmat_ready"), i + 1)
                if i >= 2:
                    pe.wait_ge(S("y_ssd_used"), i - 1)
                for h in range(4):
                    r0, c0 = 64 * (h % 2), P * (h // 2)
                    hh = 4 * hq + h
                    last = mm(y[r0:r0 + 64, c0:c0 + P], x_tm[:, j, 64 * hh:64 * hh + 64], Lm[i % 2][:, h * P:(h + 1) * P],
                              start=True, stop=(j == 0))
                    if j:
                        last = mm(y[r0:r0 + 64, c0:c0 + P], prev[:, 64 * hh:64 * hh + 64], Ce[i % 2][:, h * P:(h + 1) * P],
                                  start=False, stop=True)
                last.then_inc(S("y_ssd_done"), 1)

            csb(0), csb(1)
            for i in range(4):
                ssd(i)
                csb(i + 2)
            for j in range(2):
                pe.wait_ge(S("xw_ready"), j + 1)
                for g in range(2):
                    b = take(n_of("stA", 2 * j + g))
                    mm(b, b_tm[:, j, g * P:(g + 1) * P], xw[:, g * 512:(g + 1) * 512], start=True, stop=True) \
                        .then_inc(tile_done, 1)
            pe.wait_ge(empty["v"], emptied(n_of("stA", 1))[1])
            for i in range(4, 8):
                ssd(i)
                if i < 6:
                    csb(i + 2)
            pe.wait_ge(empty["v"], emptied(n_of("stA", 3))[1])
            for half in range(2):
                b = take(n_of("sfT", half))
                for c in range(4):
                    last = tr(b[:, c * P:(c + 1) * P], sfin[:, (4 * half + c) * P:(4 * half + c + 1) * P], ident)
                last.then_inc(tile_done, 1)

            def spread_bc(b_):
                if b_ >= 2:
                    pe.wait_ge(S("bc_used"), b_ - 1)
                mm(ps[:, 4 + 2 * (b_ % 2), :], onehot[:, b_, :], bc_s, start=True, stop=True).then_inc(S("bc_spread"), 1)

            u_steps = [0]

            def beside_u():
                i = u_steps[0]
                u_steps[0] += 1
                if i % 2 == 0 and i // 2 < 6:
                    spread_bc(i // 2)
                if i == 8:
                    pe.wait_ge(S("y_ssd_used"), 8)
                    pe.wait_ge(S("v_squares"), DC)
                    for c in range(DC):
                        last = mm(ps[:, 5, 0:T], ones, v_sq[:, c, :], start=(c == 0), stop=(c == DC - 1))
                    last.then_inc(S("variance_done"), 1)

            project("u", HT, DC, D, beside_u)
            pe.wait_ge(S("ws_loaded"), 16)
            for half in range(2):
                b = take(n_of("wsT", half))
                for c in range(4):
                    last = tr(b[:, c * P:(c + 1) * P], ws[:, (4 * half + c) * P:(4 * half + c + 1) * P], ident)
                last.then_inc(tile_done, 1)
            pe.wait_ge(S("v_normed"), DC)
            for j in range(2):
                for half in range(2):
                    b = take(n_of("vtm", 2 * j + half))
                    for c in range(4):
                        last = tr(b[:, c * P:(c + 1) * P], V[:, 4 * half + c, j * P:(j + 1) * P], ident)
                    last.then_inc(tile_done, 1)
            for half in range(2):
                b = take(n_of("avT", half))
                for c in range(4):
                    last = tr(b[0:NB, c * P:(c + 1) * P], V[:, 4 * half + c, TP:T], ident)
                last.then_inc(tile_done, 1)
            spread_bc(6), spread_bc(7)
            pe.wait_ge(S("bs_loaded"), 16)
            mm(ps[:, 7, 128:136], ones[0:1, :], ws[0:1, 0:1024:P], start=True, stop=True)
            mm(ps[:, 5, 136:144], ones[32:33, :], bsr[:, 0:1024:P], start=True, stop=True).then_inc(S("wb_done"), 1)
            pe.wait_ge(empty["a"], emptied(n_of("vtm", 3))[1])
            pe.wait_ge(empty["v"], emptied(n_of("wsT", 1))[1])
            for h in range(8):
                b = take(n_of("mixA", h))
                for j in range(2):
                    mm(b[:, j * P:(j + 1) * P], v_tm[:, j, h * P:(h + 1) * P], wsT[:, h, :], start=True, stop=False)
                    last = mm(b[:, j * P:(j + 1) * P], ones[32:33, :], bsr[:, h * P:(h + 1) * P], start=False, stop=True)
                last.then_inc(tile_done, 1)
            pe.wait_ge(S("ya_ready"), 1)
            out_steps = [0]

            def beside_out():
                out_steps[0] += 1
                if out_steps[0] == 5:
                    for g in range(2):
                        for c in range(4):
                            pe.wait_ge(S("yz_squares"), 4 * g + c + 1)
                            last = mm(ps[:, 4 + 2 * g, 0:T], ones, HT[:, 4 * g + c, :], start=(c == 0), stop=(c == 3))
                    last.then_inc(S("gate_done"), 1)
                if out_steps[0] == 8:
                    pe.wait_ge(S("yb_ready"), DC)
                if out_steps[0] == 14:
                    pe.wait_ge(S("mem_scaled"), 1)
                    for c in range(DC):
                        for m in range(2):
                            last = tr(ps[:, 4 + c // 2, (2 * (c % 2) + m) * P:(2 * (c % 2) + m + 1) * P],
                                      mem_in[:, m, c * P:(c + 1) * P], ident)
                    last.then_inc(S("mem_turned"), 1)

            project("out0", UZ, 16, D, beside_out)
            pe.wait_ge(S("memh_ready"), 1)
            square_sums(1)

            def attention(l, k_post, k_pre):
                pe.wait_ge(S("mem_gain_ready"), l + 1)
                project_tm(f"k{l}", MG)
                square_sums(k_pre)
                project_split(f"q{l}", D, norm=k_pre)
                pe.wait_ge(empty["a"], emptied(n_of(f"q{l}", 7))[1])
                for half in range(2):
                    b = take(n_of(f"qs{l}", half))
                    for c in range(4):
                        last = tr(b[0:NB, c * P:(c + 1) * P], QT[:, 4 * half + c, TP:T], ident)
                    last.then_inc(tile_done, 1)
                for c in range(DC):
                    b = take(n_of(f"kT{l}", c))
                    for m in range(2):
                        last = tr(b[:, m * P:(m + 1) * P], k_tm[:, m, c * P:(c + 1) * P], ident)
                    last.then_inc(tile_done, 1)
                pe.wait_ge(empty["a"], emptied(n_of(f"qs{l}", 1))[1])
                made = [0]

                def spread_q():
                    for i in range(made[0], made[0] + 2):
                        if 16 * l + i >= 2:
                            pe.wait_ge(S("q_spread_used"), 16 * l + i - 1)
                        mm(ps[:, 5 + i % 2, :], onehot[:, i // 2, :], q_s[:, (i % 2) * 512:(i % 2) * 512 + 512],
                           start=True, stop=True).then_inc(S("q_spread"), 1)
                    made[0] += 2

                project_tm(f"vm{l}", MG, spread_q)
                b = take(n_of(f"sT{l}"))
                pe.wait_ge(S("k_cache_used"), NB * (l + 1))
                for m in range(2):
                    last = tr(b[0:32, m * P:(m + 1) * P], scs[:, m, :], ident)
                last.then_inc(tile_done, 1)
                for i in range(4):
                    if i == 2:
                        pe.wait_ge(S("sample_probs"), l + 1)
                        b = take(n_of(f"pTs{l}"))
                        for m in range(2):
                            last = tr(b[:, m * 32:m * 32 + 32], p_s[:, m * P:(m + 1) * P], ident[0:32, 0:32])
                        last.then_inc(tile_done, 1)
                    g, hp = i // 2, i % 2
                    b = take(n_sc(l, i))
                    for h in range(2):
                        for d in range(2):
                            c = 2 * (2 * hp + h) + d
                            last = mm(b[:, h * 256:(h + 1) * 256], QT[:, c, g * P:(g + 1) * P], KT[:, c, :],
                                      start=(d == 0), stop=(d == 1))
                    last.then_inc(tile_done, 1)

                def sample_values(b_):
                    pe.wait_ge(S(f"v_cache_loaded{b_ % 4}"), 16 * (2 * l + b_ // 4 + 1))
                    for h in range(XH):
                        for m in range(2):
                            last = mm(ps[0:NB, 4 + h, 0:256], pts[:, m * XH + h, b_, :],
                                      vc[b_ % 4][:, m, h * 256:(h + 1) * 256],
                                      start=(b_ == 0 and m == 0), stop=(b_ == NB - 1 and m == 1))
                    last.then_inc(S("v_cache_used"), 1)

                pe.wait_ge(empty["v"], emptied(n_of(f"pTs{l}"))[1])
                for b_ in range(4):
                    sample_values(b_)
                for h in range(XH):
                    pe.wait_ge(S("probs_ready"), 4 * l + 4)
                    b = take(n_of(f"pT{l}", h))
                    for m in range(2):
                        for g in range(2):
                            last = tr(b[:, m * 256 + g * P:m * 256 + g * P + P], PR[:, g, h, m * P:(m + 1) * P], ident)
                    last.then_inc(tile_done, 1)
                for c in range(DC):
                    pe.wait_ge(empty["a"], emptied(n_of(f"pT{l}", c // 2))[1])
                    b = take(n_of(f"pv{l}", c))
                    for m in range(2):
                        last = mm(b[:, 0:256], vm_tm[:, m, c * P:(c + 1) * P], PT[:, c // 2, m, :],
                                  start=(m == 0), stop=(m == 1))
                    last.then_inc(tile_done, 1)
                for b_ in range(4, NB):
                    sample_values(b_)
                pe.wait_ge(S("o_rows"), 2 * l + 1)
                for c in range(DC):
                    last = tr(ps[:, 7, c * NB:(c + 1) * NB], o_tm[:, c // 2, (c % 2) * P:(c % 2 + 1) * P],
                              ident[0:NB, 0:NB])
                last.then_inc(S("o_turned"), 1)
                pe.wait_ge(empty["a"], emptied(n_of(f"pv{l}", 7))[1])
                pe.wait_ge(S("o_samples"), l + 1)
                project(f"xo{l}", OT, DC, D)
                square_sums(k_pre + 1)
                square_sums(k_pre + 2)

            attention(0, 1, 2)
            for i, n in enumerate(FGROUPS):
                project_split(f"gate{i}", n * P, norm=4 if i == 0 else None)
                project_split(f"up{i}", n * P)
            pe.wait_ge(empty["v"], emptied(n_of("up5", 1))[1])
            project("down", hid, FC, D)
            square_sums(5)
            square_sums(6)
            project_split("f", D, norm=6)
            project_split("q", D)
            project_split("i", D)
            project_split("g", D)
            for j in range(2):
                for half in range(2):
                    b = take(n_of("iT", 2 * j + half))
                    for c in range(4):
                        last = tr(b[:, c * P:(c + 1) * P], I[:, 4 * half + c, j * P:(j + 1) * P], ident)
                    last.then_inc(tile_done, 1)
            for half in range(2):
                b = take(n_of("isT", half))
                for c in range(4):
                    last = tr(b[0:NB, c * P:(c + 1) * P], I[:, 4 * half + c, TP:T], ident)
                last.then_inc(tile_done, 1)
            pe.wait_ge(S("k_decayed"), 1)
            for j in range(2):
                for half in range(2):
                    b = take(n_of("kT", 2 * j + half))
                    for c in range(4):
                        last = tr(b[:, c * P:(c + 1) * P], K[:, 4 * half + c, j * P:(j + 1) * P], ident)
                    last.then_inc(tile_done, 1)
            for hq in range(2):
                b = take(n_of("att", hq)).rearrange("p (h j t) -> p h j t", h=4, j=2)
                for h in range(4):
                    for ch in range(4):
                        r0, hh = 64 * (ch % 2), 4 * hq + h
                        last = mm(b[r0:r0 + 64, h, ch // 2, :], Fg[:, hh, ch * 64:ch * 64 + 64],
                                  Q[:, hh, ch * 64:ch * 64 + 64], start=True, stop=True)
                last.then_inc(tile_done, 1)
            pe.wait_ge(empty["a"], emptied(n_of("kT", 3))[1])
            for ch in range(4):
                r0, j = 64 * (ch % 2), ch // 2
                for half in range(2):
                    b = take(n_of("upd", 2 * ch + half))
                    for c in range(4):
                        hh = 4 * half + c
                        last = mm(b[:, c * P:(c + 1) * P], kp_tm[r0:r0 + 64, j, hh * P:(hh + 1) * P],
                                  i_tm[r0:r0 + 64, j, hh * P:(hh + 1) * P], start=True, stop=True)
                    last.then_inc(tile_done, 1)
            for h in range(8):
                b = take(n_of("ho", h))
                if h == 0:
                    pe.wait_ge(empty["v"], emptied(n_of("upd", 7))[1])
                for j in range(2):
                    mm(b[:, j * P:(j + 1) * P], i_tm[:, j, h * P:(h + 1) * P], att[:, h, j, :], start=True, stop=False,
                       skip_group_check=True)
                    for ch in range(2 * j, 2 * j + 2):
                        if ch:
                            last = mm(b[:, ch * 64:ch * 64 + 64], st[ch - 1][:, h, :], Q[:, h, ch * 64:ch * 64 + 64],
                                      start=False, stop=(ch % 2 == 1), skip_group_check=True)
                last.then_inc(tile_done, 1)
            pe.wait_ge(empty["a"], emptied(n_of("isT", 1))[1])

            for h in range(8):
                b = take(n_of("hn", h))
                pe.wait_ge(S("ho_squares"), h + 1)
                mm(b[:, 0:TP], ones, HT[:, h, 0:TP], start=True, stop=True).then_inc(tile_done, 1)

            def hgrn_read(b_):
                pe.wait_ge(S("h_updated"), b_ + 1)
                for h in range(8):
                    last = mm(ps[0:NB, 5 + h // 4, (h % 4) * P:(h % 4 + 1) * P], q_one[:, h, b_, :], st[b_ % 4][:, h, :],
                              start=(b_ == 0 and h % 4 == 0),
                              stop=(b_ == NB - 1), skip_group_check=True)
                last.then_inc(S("hgrn_read"), 1)

            for b_ in range(NB):
                for half in range(2):
                    b = take(n_of("vB", 2 * b_ + half))
                    mm(b, onehot[:, b_, :], i_s[:, half * 512:(half + 1) * 512], start=True, stop=True).then_inc(tile_done, 1)
                if b_:
                    hgrn_read(b_ - 1)
            hgrn_read(NB - 1)
            pe.wait_ge(S("o_rows"), 2)
            for h in range(8):
                last = tr(ps[:, 7, 64 + 8 * h:72 + 8 * h], i_s[:, h * P:(h + 1) * P], ident[0:NB, 0:NB])
            last.then_inc(S("o_turned"), 1)
            b = take(n_of("hns"))
            pe.wait_ge(S("ho_squares"), DC + 1)
            mm(split(b[:, 0:64], DC), ones, HT[:, :, TP:T], start=True, stop=True).then_inc(tile_done, 1)
            pe.wait_ge(S("ho_ready"), 1)
            project("out1", E, DC, D)
            square_sums(7)
            attention(1, 7, 8)
            wait_norm(10)
            pe.wait_ge(S("experts_may_start"), 1)
            for g, (t0, nt) in enumerate(GROUPS):
                for half in range(2):
                    b = take(n_of("htok", 2 * g + half))
                    for c in range(4):
                        last = tr(b[0:nt, c * P:(c + 1) * P], HT[:, 4 * half + c, t0:t0 + nt], ident)
                    last.then_inc(tile_done, 1)
            pe.wait_ge(S("router_loaded"), 16)
            b = take(n_of("logit"))
            for g, (t0, nt) in enumerate(GROUPS):
                for k in range(DC):
                    last = mm(b[0:nt, 8 * g:8 * g + 8], HT[:, k, t0:t0 + nt], wr[:, k, :], start=(k == 0), stop=(k == DC - 1))
            last.then_inc(tile_done, 1)
            for half in range(2):
                last = mm(ps[:, 4 + half, :], acc[:, 0, 0:P], acc[:, 0, 0:512], start=True, stop=True)
            last.then_inc(S("quarter_used"), QRING)
            pe.wait_ge(S("mask_ready"), 1)
            b = take(n_of("posn"))
            for g, (t0, nt) in enumerate(GROUPS):
                for g2 in range(g + 1):
                    w = tris if g2 == g else ones
                    k = GROUPS[g2][1]
                    last = mm(b[:, 8 * g:8 * g + 8], w[0:k, :], msk[0:k, g2, :], start=(g2 == 0), stop=(g2 == g))
            for g, (t0, nt) in enumerate(GROUPS):
                last = mm(b[:, 24:32], ones[0:nt, :], msk[0:nt, g, :], start=(g == 0), stop=(g == 2))
            last.then_inc(tile_done, 1)

            def gather():
                for c in range(DC):
                    for g, (t0, nt) in enumerate(GROUPS):
                        last = mm(ps[:, 2 + c // 4, (c % 4) * P:(c % 4 + 1) * P], h_tok[0:nt, g, c * P:(c + 1) * P],
                                  pick[0:nt, g, :], start=(g == 0), stop=(g == 2))
                last.then_inc(S("gather_done"), 1)

            def scatter(i):
                g, half = i // 2, i % 2
                t0, nt = GROUPS[g]
                mm(ps[0:nt, 7 - i % 2, :], pickT[:, t0:t0 + nt], oe[:, half * 512:(half + 1) * 512],
                   start=True, stop=True).then_inc(S("scatter_done"), 1)

            pe.wait_ge(S("rounds_ready"), 1)
            pe.wait_ge(S("pick_ready"), 1)
            gather()
            steps_v = nc.values_load(steps_i[0:1, 0:1], engines=[mybir.EngineType.PE], min_val=NE, max_val=3 * NE)
            with pe.Fori(0, steps_v) as it_:
                it = pe.snap(it_)
                pe.wait_ge(S("xe_ready"), it + 1)
                for q, (kind, s, i) in enumerate(QUARTERS):
                    hi, lo = wr_[:, q % QRING, 0, :], wr_[:, q % QRING, 1, :]
                    if kind == "gate" and i == 0:
                        pe.wait_ge(S("hs_ready"), it * NSL + NSL + max(s - 1, 0))
                    if kind == "down" and i == 0:
                        pe.wait_ge(S("hT_ready"), it * NSL + s + 1)
                    pe.wait_ge(S("lo_made"), it * NQ + 2 * MRING + q + 1)
                    if kind == "down":
                        for half in range(2):
                            cols = slice(half * 512, (half + 1) * 512)
                            xh, xl = (x[s % 2][:, i * P:(i + 1) * P] for x in (hT_hi, hT_lo))
                            out = ps[:, 4 + half, :]
                            mm(out, xh, hi[:, cols], start=(s == 0 and i == 0), stop=False)
                            mm(out, xh, lo[:, cols], start=False, stop=False)
                            last = mm(out, xl, hi[:, cols], start=False, stop=(s == NSL - 1 and i == 3))
                    else:
                        out = ps[:, 2 * (s % 2) + (kind == "up"), :]
                        for k in range(2):
                            cols = slice(k * SL, (k + 1) * SL)
                            c = 2 * i + k
                            xh, xl = (x[:, c * P:(c + 1) * P] for x in (xe_hi, xe_lo))
                            mm(out, xh, hi[:, cols], start=(c == 0), stop=False)
                            mm(out, xh, lo[:, cols], start=False, stop=False)
                            last = mm(out, xl, hi[:, cols], start=False, stop=(c == DC - 1))
                    last.then_inc(S("quarter_used"), 1)
                    if q in TURN:
                        s = TURN[q]
                        pe.wait_ge(S("hs_ready"), it * NSL + NSL + s + 1)
                        if s:
                            pe.wait_ge(S("hT_ready"), it * NSL + s)
                        for k in range(4):
                            last = tr(ps[:, 6, k * P:(k + 1) * P], hs[s % 2][:, k * P:(k + 1) * P], ident)
                        last.then_inc(S("h_transposed"), 1)
                    if q in SCATTER:
                        if q == SCATTER[0]:
                            pe.wait_ge(S("oe_ready"), it + 1)
                        i = SCATTER.index(q)
                        if i >= 2:
                            pe.wait_ge(S("acc_added"), it * 6 + i - 1)
                        scatter(i)
                    if q == TURN_PLACES:
                        pe.wait_ge(S("acc_added"), it * 6 + 6)
                        for g, (t0, nt) in enumerate(GROUPS):
                            last = tr(ps[:, 7, t0:t0 + nt], pickg[0:nt, g, :], ident[0:nt, 0:nt])
                        last.then_inc(S("pickT_done"), 1)
                    if q == GATHER:
                        pe.wait_ge(S("pick_ready"), it + 2)
                        pe.wait_ge(S("hs_ready"), it * NSL + NSL + NSL - 1)
                        gather()
            pe.wait_ge(S("oe_ready"), steps_v + 1)
            for i in range(6):
                if i >= 2:
                    pe.wait_ge(S("acc_added"), steps_v * 6 + i - 1)
                scatter(i)
            pe.wait_ge(S("experts_done"), 1)
            for g, (t0, nt) in enumerate(GROUPS):
                for half in range(2):
                    for c in range(4):
                        last = tr(ps[0:nt, 2 * g + half, c * P:(c + 1) * P], XT[:, 4 * half + c, t0:t0 + nt], ident)
            last.then_inc(S("x_tok_done"), 1)

        @block.scalar
        def _(act):
            f = nc.scalar.activation
            hi_count = [0]

            def make_hi(qs):
                for q in qs:
                    b = quarters[q][0]
                    act.wait_ge(loaded[b % RING], 16 * (b // RING + 1))
                    if q >= QRING:
                        sem, value = quarters[q - QRING][3]
                        act.wait_ge(sem, value)
                    raw_q, hi, _ = quarter_of(q)
                    f(hi, raw_q, ACT.Copy).then_inc(S("dense_hi_made"), 1)
                    hi_count[0] = q + 1

            def first_hi(name):
                make_hi(range(hi_count[0], needed(n_of(name) - 1) + 2))

            def tile(n):
                make_hi(ahead_of(n, hi_count[0], 3))
                act.wait_ge(tile_done, n + 1)
                return bank(n)

            def input_hi(k):
                for c in range(DC):
                    act.wait_ge(S("normed"), DC * PRES.index(k) + c + 1)
                    f(x_hi[:, c, :], HT[:, c, :], ACT.Copy).then_inc(S("x_hi_made"), 1)

            def copies(name, dsts, view=lambda b: b):
                for i, dst in enumerate(dsts):
                    b = tile(n_of(name, i))
                    f(dst, view(b), ACT.Copy).then_inc(empty["a"], 1)

            def block_out(name):
                for c in range(DC):
                    b = tile(n_of(name, c))
                    f(HT[:, c, :], b[:, 0:T], ACT.Square).then_inc(S("squares_ready"), 1)
                    f(MT[:, c, :], b[:, 0:T], ACT.Copy).then_inc(empty["a"], 1)

            def root(k):
                act.wait_ge(S("square_sums_done"), k + 1)
                f(rs, ps[:, 4, 0:T], ACT.Sqrt, bias=eps_c, scale=1.0 / D).then_inc(S("root_ready"), 1)

            def squares_of_x(k):
                for c in range(DC):
                    act.wait_ge(S("x_updated"), DC * posts.index(k - 1) + c + 1)
                    f(MT[:, c, :], XT[:, c, :], ACT.Square).then_inc(S("squares_ready"), 1)

            for c in range(DC):
                b = tile(n_of("xT", c))
                f(MT[:, c, :], b[:, 0:T], ACT.Square).then_inc(S("squares_ready"), 1)
                f(XT[:, c, :], b[:, 0:T], ACT.Copy).then_inc(empty["a"], 1)
            act.wait_ge(S("eps_ready"), 1)
            root(0)
            act.wait_ge(S("lb_diff"), 1)
            f(lb1, omlb, ACT.Sigmoid).then_inc(S("lb_ready"), 1)
            act.wait_ge(S("small_loaded"), 64)
            f(aexp, alog, ACT.Exp).then_inc(S("aexp_ready"), 1)
            for c in range(CC):
                b = tile(n_of("xbc", c))
                f(raw[:, c, 3:259], b[:, 0:TP], ACT.Copy)
                f(raws[:, c, 3, :], b[:, TP:T], ACT.Copy).then_inc(empty["a"], 1)
            act.wait_ge(S("dt_abs_ready"), 1)
            f(dtr[3], dtr[3], ACT.Exp, scale=-1.0).then_inc(S("dt_exp_ready"), 1)
            act.wait_ge(S("dt_done"), 1)
            f(exd[:, 0:8], dtr[1][:, TP:T], ACT.Exp)
            f(exd[:, 8:16], dtr[0][:, TP:T], ACT.Copy).then_inc(S("dt_ready"), 1)
            for c in range(DC):
                b = tile(n_of("v", c))
                f(V[:, c, :], b[:, 0:T], ACT.Gelu_apprx_tanh).then_inc(empty["a"], 1)
            for c in range(CC):
                act.wait_ge(S("conv_ready"), 1 + c // 4)
                f(XBC[:, c, :], XBC[:, c, :], ACT.Silu, bias=par[:, CB + c:CB + c + 1]).then_inc(S("xbc_ready"), 1)
            copies("tr0", [conv_o[:, i * 512:(i + 1) * 512] for i in range(3)], lambda b: b[0:11, :])
            for i in range(4):
                b = tile(n_of("tr0", 3 + i))
                f(x_tm[:, i // 2, (i % 2) * 512:(i % 2 + 1) * 512], b, ACT.Copy).then_inc(empty["a"], 1)
            b = tile(n_of("tr0", 7))
            f(b_tm.rearrange("p j n -> p (j n)"), b, ACT.Copy).then_inc(empty["a"], 1)
            b = tile(n_of("tr0", 8))
            f(bc_s, b[0:NB, :], ACT.Copy).then_inc(empty["a"], 1)
            copies("cb", [CBT.rearrange("p k n -> p (k n)")])
            act.wait_ge(S("conv_stored"), 32)
            for c in range(DC):
                b = tile(n_of("z", c))
                f(Z[:, c, :], b[:, 0:T], ACT.Silu).then_inc(empty["a"], 1)
            act.wait_ge(S("dec_in"), 1)
            f(small[:, 160:224], small[:, 160:224], ACT.Exp).then_inc(S("dec_ready"), 1)

            def lmat(i):
                if i >= 4:
                    b = tile(n_csb(i))
                    if i >= 5:
                        act.wait_ge(S("ce_ready"), i - 4)
                    f(ecs, b, ACT.Exp).then_inc(S("ecs_ready"), 1)
                act.wait_ge(S("ldiff_ready"), i + 1)
                f(Lm[i % 2], Lm[i % 2], ACT.Exp).then_inc(S("lexp_ready"), 1)

            for i in range(8):
                lmat(i)
            copies("sfT", [ssm_o[:, 4 * i:4 * i + 4, :].rearrange("p c n -> p (c n)") for i in range(2)])
            for c in range(DC):
                f(v_sq[:, c, :], V[:, c, :], ACT.Square).then_inc(S("v_squares"), 1)
            for c in range(DC):
                b = tile(n_of("u", c))
                f(U[:, c, :], b[:, 0:T], ACT.Gelu_apprx_tanh).then_inc(empty["a"], 1)
            act.wait_ge(S("variance_done"), 1)
            f(rs, ps[:, 5, 0:T], ACT.Sqrt, bias=eps_c, scale=1.0 / D).then_inc(S("v_root"), 1)
            for c in range(DC):
                act.wait_ge(S("v_scaled"), c + 1)
                f(V[:, c, :], V[:, c, :], ACT.Identity, bias=par[:, LNB + c:LNB + c + 1]).then_inc(S("v_normed"), 1)
            for i in range(4):
                b = tile(n_of("vtm", i))
                f(v_tm[:, i // 2, (i % 2) * 512:(i % 2 + 1) * 512], b, ACT.Copy).then_inc(empty["a"], 1)
            copies("avT", [av_o[:, i * 512:(i + 1) * 512] for i in range(2)], lambda b: b[0:NB, :])
            for c in range(DC):
                act.wait_ge(S("yz_ready"), 1)
                f(HT[:, c, :], Z[:, c, :], ACT.Square).then_inc(S("yz_squares"), 1)
            act.wait_ge(S("gate_done"), 1)
            for g in range(2):
                f(rsg[:, g, :], ps[:, 4 + 2 * g, 0:T], ACT.Sqrt, bias=eps_c, scale=2.0 / D).then_inc(S("gate_root"), 1)
            act.wait_ge(S("mem_loaded"), 16)
            for m in range(2):
                f(KT.rearrange("p c t -> p (c t)")[:, m * D:(m + 1) * D], mem_in[:, m, :], ACT.Square,
                  accum_out=mrs[:, m:m + 1]).then_inc(S("mem_step"), 1)
            act.wait_ge(S("mem_step"), 2)
            f(mrs[:, 2:4], mrs[:, 0:2], ACT.Sqrt, bias=eps_c, scale=1.0 / D).then_inc(S("mem_root"), 1)
            act.wait_ge(S("mem_rs_ready"), 1)
            for m in range(2):
                last = f(mem_in[:, m, :], mem_in[:, m, :], ACT.Copy, scale=mrs[:, m:m + 1])
            last.then_inc(S("mem_scaled"), 1)
            act.wait_ge(S("mem_turned"), 1)
            for i in range(4):
                last = f(memh[:, 2 * i:2 * i + 2, :].rearrange("p c t -> p (c t)"), ps[:, 4 + i, :], ACT.Copy)
            last.then_inc(S("memh_ready"), 1)
            block_out("out0")

            def attention(l, k_post, k_pre):
                root(k_post)
                squares_of_x(k_pre)
                for i in range(4):
                    b = tile(n_of(f"k{l}", i))
                    f(k_tm[:, i % 2, (i // 2) * 512:(i // 2 + 1) * 512], b, ACT.Copy).then_inc(empty["a"], 1)
                first_hi(f"q{l}")
                root(k_pre)
                input_hi(k_pre)
                for c in range(DC):
                    b = tile(n_of(f"q{l}", c))
                    f(QT[:, c, :], b[:, 0:T], ACT.Copy, scale=(D // XH) ** -0.5).then_inc(empty["a"], 1)
                copies(f"qs{l}", [q_s[:, i * 512:(i + 1) * 512] for i in range(2)], lambda b: b[0:NB, :])
                copies(f"kT{l}", [KT[:, c, :] for c in range(DC)], lambda b: b[:, 0:MEM])
                for i in range(4):
                    b = tile(n_of(f"vm{l}", i))
                    f(vm_tm[:, i % 2, (i // 2) * 512:(i // 2 + 1) * 512], b, ACT.Copy).then_inc(empty["a"], 1)
                b = tile(n_of(f"sT{l}"))
                act.wait_ge(S("sample_max"), l + 1)
                f(p_s, b[0:32, 0:256], ACT.Exp, bias=smx, accum_out=ssm).then_inc(empty["a"], 1)
                for i in range(4):
                    b = tile(n_sc(l, i))
                    act.wait_ge(S("max_ready"), 4 * l + i + 1)
                    g, hp = i // 2, i % 2
                    for h in range(2):
                        last = f(PR[:, g, 2 * hp + h, :], b[:, h * 256:(h + 1) * 256], ACT.Exp,
                                 bias=mx[:, 2 * i + h:2 * i + h + 1], accum_out=sm[:, 2 * i + h:2 * i + h + 1])
                    last.then_inc(empty["a"], 1)
                copies(f"pT{l}", [PT[:, h].rearrange("p m t -> p (m t)") for h in range(XH)])
                copies(f"pv{l}", [OT[:, c, 0:TP] for c in range(DC)], lambda b: b[:, 0:TP])
                block_out(f"xo{l}")
                root(k_pre + 1)
                if l == 0:
                    first_hi("gate0")
                squares_of_x(k_pre + 2)
                root(k_pre + 2)
                if l == 0:
                    input_hi(k_pre + 2)

            attention(0, 1, 2)
            for i in range(FC):
                b = tile(n_of(f"gate{i // 4}", i % 4))
                if i >= 4:
                    act.wait_ge(empty["v"], emptied(n_of(f"up{i // 4 - 1}", i % 4))[1])
                f(gtmp[i % 4], b[:, 0:T], ACT.Silu).then_inc(empty["a"], 1)
            block_out("down")
            root(5)
            first_hi("f")
            squares_of_x(6)
            root(6)
            input_hi(6)
            for name, dst, fn in (("f", Fg, ACT.Sigmoid), ("q", Q, ACT.Silu)):
                for c in range(DC):
                    b = tile(n_of(name, c))
                    f(dst[:, c, :], b[:, 0:T], fn).then_inc(empty["a"], 1)
            act.wait_ge(S("fg_ready"), 1)
            f(Fg, Fg, ACT.Ln).then_inc(S("logf_ready"), 1)
            for c in range(DC):
                b = tile(n_of("i", c))
                f(I[:, c, :], b[:, 0:T], ACT.Copy).then_inc(empty["a"], 1)
            act.wait_ge(S("bc_ready"), 1)
            f(etot[:, :, 0:4], BC[:, :, 63:TP:64], ACT.Exp)
            f(es, BC[:, :, TP:T], ACT.Exp).then_inc(S("es_ready"), 1)
            f(E[:, :, 0:TP], BC[:, :, 0:TP], ACT.Exp).then_inc(S("e_ready"), 1)
            make_hi([hi_count[0]])
            act.wait_ge(S("e_used"), 1)
            f(E[:, :, 0:TP], BC[:, :, 0:TP], ACT.Exp, scale=-1.0).then_inc(S("e_ready"), 1)
            make_hi([hi_count[0]])
            act.wait_ge(S("e_used"), 2)
            f(E[:, :, 0:TP], E[:, :, 0:TP], ACT.Exp).then_inc(S("e_ready"), 1)
            for c in range(DC):
                b = tile(n_of("g", c))
                f(G[:, c, :], b[:, 0:T], ACT.Silu).then_inc(empty["a"], 1)
            for i in range(4):
                b = tile(n_of("iT", i))
                f(i_tm[:, i // 2, (i % 2) * 512:(i % 2 + 1) * 512], b, ACT.Copy).then_inc(empty["a"], 1)
            copies("isT", [i_s[:, i * 512:(i + 1) * 512] for i in range(2)], lambda b: b[0:NB, :])
            for i in range(4):
                b = tile(n_of("kT", i))
                f(kp_tm[:, i // 2, (i % 2) * 512:(i % 2 + 1) * 512], b, ACT.Copy).then_inc(empty["a"], 1)
            copies("ho", [E[:, h, 0:TP] for h in range(8)], lambda b: b[:, 0:TP])
            act.wait_ge(empty["a"], emptied(n_of("ho", 7))[1])
            for h in range(8):
                f(HT[:, h, 0:TP], E[:, h, 0:TP], ACT.Square).then_inc(S("ho_squares"), 1)
            for h in range(8):
                b = tile(n_of("hn", h))
                f(BC[:, h, 0:TP], b[:, 0:TP], ACT.Sqrt, bias=eps_c, scale=1.0 / P).then_inc(empty["a"], 1)
            act.wait_ge(S("ho_samples"), 1)
            f(HT[:, :, TP:T], E[:, :, TP:T], ACT.Square).then_inc(S("ho_squares"), 1)
            b = tile(n_of("hns"))
            f(BC[:, :, TP:T], split(b[:, 0:64], DC), ACT.Sqrt, bias=eps_c, scale=1.0 / P).then_inc(empty["a"], 1)
            block_out("out1")
            attention(1, 7, 8)
            act.wait_ge(S("experts_may_start"), 1)
            for i in range(6):
                g, half = i // 2, i % 2
                nt = GROUPS[g][1]
                b = tile(n_of("htok", i))
                f(h_tok[0:nt, g, half * 512:(half + 1) * 512], b[0:nt, :], ACT.Copy).then_inc(empty["a"], 1)
            act.wait_ge(S("top_diff"), 1)
            f(tw[:, :, 1], tw[:, :, 0], ACT.Exp).then_inc(S("top_exp"), 1)
            act.wait_ge(S("rounds_ready"), 1)

            def tokens_hi():
                for half in range(2):
                    f(xe_hi[:, half * 512:(half + 1) * 512], ps[:, 2 + half, :], ACT.Copy).then_inc(S("xe_hi_made"), 1)

            def copy_oe():
                f(oe[:, 0:512], ps[:, 4, :], ACT.Copy)
                f(oe[:, 512:D], ps[:, 5, :], ACT.Copy).then_inc(S("oe_ready"), 1)

            act.wait_ge(S("gather_done"), 1)
            tokens_hi()
            steps_v = nc.values_load(steps_i[0:1, 0:1], engines=[mybir.EngineType.Activation], min_val=NE, max_val=3 * NE)
            with act.Fori(0, steps_v) as it_:
                it = act.snap(it_)

                def expert_hi(q):
                    if q % 2 == 0:
                        slot_ = q // 2 % MRING
                        act.wait_ge(mloaded[slot_], it * (16 * NBLK // MRING) + mloaded_before[slot_]
                                    + 16 * (q // 2 // MRING + 1))
                    act.wait_ge(S("quarter_used"), it * NQ + q + 1)
                    f(wr_[:, q % QRING, 0, :], quarter(q), ACT.Copy).then_inc(S("hi_made"), 1)

                for q in range(NQ):
                    expert_hi(q)
                    if q == QRING - 1:
                        copy_oe()
                    if q - QRING == TURN_PLACES:
                        act.wait_ge(S("pickT_done"), it + 1)
                        f(pickT, ps[:, 7, 0:T], ACT.Copy)
                    if q - QRING == GATHER:
                        act.wait_ge(S("gather_done"), it + 2)
                        tokens_hi()
                    kind, s, i = QUARTERS[q - QRING] if q >= QRING else ("", 0, 0)
                    if kind == "gate" and i == 3:
                        act.wait_ge(S("quarter_used"), it * NQ + q + 1)
                        f(sg[s % 2], ps[:, 2 * (s % 2), :], ACT.Silu).then_inc(S("silu_done"), 1)
                    if q - QRING in TURN:
                        s = TURN[q - QRING]
                        act.wait_ge(S("h_transposed"), it * NSL + s + 1)
                        f(hT_hi[s % 2], ps[:, 6, :], ACT.Copy).then_inc(S("hT_hi_made"), 1)
            act.wait_ge(S("quarter_used"), steps_v * NQ + QRING)
            copy_oe()
            act.wait_ge(S("experts_done"), 1)
            act.wait_ge(S("x_tok_done"), 1)
            for g, (t0, nt) in enumerate(GROUPS):
                f(x_tok[0:nt, g, 0:512], ps[0:nt, 2 * g, :], ACT.Copy)
                f(x_tok[0:nt, g, 512:D], ps[0:nt, 2 * g + 1, :], ACT.Copy).then_inc(S("x_tok_ready"), 1)
                f(ysq[0:nt, :], acc[0:nt, g, :], ACT.Square, accum_out=frs[0:nt, g:g + 1]).then_inc(S("y_squares"), 1)
                act.wait_ge(S("y_squares"), g + 1)
                f(frs[0:nt, 3 + g:4 + g], frs[0:nt, g:g + 1], ACT.Sqrt, bias=eps_c[0:nt], scale=1.0 / D) \
                    .then_inc(S("y_root"), 1)

        @block.vector
        def _(dve):
            v = nc.vector
            TT, TS, STT = v.tensor_tensor, v.tensor_scalar, v.scalar_tensor_tensor
            steps = [0]

            def link(ins):
                steps[0] += 1
                ins.then_inc(S("dve_step"), 1)
                dve.wait_ge(S("dve_step"), steps[0])

            lo_count = [0]

            def make_lo(qs):
                for q in qs:
                    raw_q, hi, lo = quarter_of(q)
                    dve.wait_ge(S("dense_hi_made"), q + 1)
                    TT(lo, raw_q, hi.bitcast(F32), ALU.subtract).then_inc(lo_made, 1)
                    lo_count[0] = q + 1

            def first_lo(name):
                make_lo(range(lo_count[0], needed(n_of(name) - 1) + 2))

            def lo_through(name, i, lead=0):
                make_lo(ahead_of(n_of(name, i), lo_count[0], lead))

            def tile(n):
                make_lo(ahead_of(n, lo_count[0], 2))
                dve.wait_ge(tile_done, n + 1)
                return bank(n)

            def copied(n):
                make_lo(ahead_of(n, lo_count[0], 2))
                dve.wait_ge(empty["a"], emptied(n)[1])

            def finish_norm(k):
                kind, layer, pre = NORMS[k]
                dve.wait_ge(S("root_ready"), k + 1)
                link(v.reciprocal(rs, rs))
                if pre:
                    for c in range(DC + 2):
                        if c < DC:
                            STT(out=HT[:, c, :], in0=XT[:, c, :], scalar=gain(kind, layer, c), in1=rs,
                                op0=ALU.mult, op1=ALU.mult).then_inc(S("normed"), 1)
                        if c >= 2 and k in SPLIT_NORMS:
                            dve.wait_ge(S("x_hi_made"), DC * SPLIT_NORMS.index(k) + c - 1)
                            TT(x_lo[:, c - 2, :], HT[:, c - 2, :], x_hi[:, c - 2, :].bitcast(F32), ALU.subtract) \
                                .then_inc(S("x_lo_made"), 1)
                else:
                    for c in range(DC + 1):
                        if c < DC:
                            STT(out=MT[:, c, :], in0=MT[:, c, :], scalar=gain(kind, layer, c), in1=rs,
                                op0=ALU.mult, op1=ALU.mult).then_inc(S("out_scaled"), 1)
                        if c:
                            dve.wait_ge(S("out_scaled"), DC * posts.index(k) + c)
                            TT(XT[:, c - 1, :], XT[:, c - 1, :], MT[:, c - 1, :], ALU.add).then_inc(S("x_updated"), 1)

            v.memset(eps_c, EPS).then_inc(S("eps_ready"), 1)
            b = tile(n_of("par"))
            v.tensor_copy(par, b[:, 0:220]).then_inc(empty["v"], 1)
            dve.wait_ge(empty["v"], 1)
            TT(omlb, par[:, LB + 8:LB + 16], par[:, LB:LB + 8], ALU.subtract).then_inc(S("lb_diff"), 1)
            b = tile(n_of("st"))
            v.tensor_copy(raws[:, :, 0:3, :], b[:, 0:288].rearrange("p (c b k) -> p c k b", c=CC, b=NB)) \
                .then_inc(empty["v"], 1)
            finish_norm(0)
            dve.wait_ge(S("lb_ready"), 1)
            link(TS(omlb, lb1, -1.0, 1.0, ALU.mult, ALU.add))
            for c4 in range(3):
                dve.wait_ge(empty["a"], emptied(n_of("xbc", 4 * c4 + 3))[1])
                cc = range(4 * c4, 4 * c4 + 4)
                for c in cc:
                    last = TS(XBC[:, c, 0:TP], raw[:, c, 3:259], par[:, CW + 36 + c:CW + 37 + c], None, ALU.mult)
                link(last)
                for k in range(3):
                    for c in cc:
                        last = STT(out=XBC[:, c, 0:TP], in0=raw[:, c, k:k + TP], scalar=par[:, CW + 12 * k + c:CW + 12 * k + c + 1],
                                   in1=XBC[:, c, 0:TP], op0=ALU.mult, op1=ALU.add)
                    link(last)
                xs = XBC[:, 4 * c4:4 * c4 + 4, TP:T]
                tmp = t2[:, 0, 0:32].rearrange("p (c b) -> p c b", c=4)
                for k in range(4):
                    w = par[:, CW + 12 * k + 4 * c4:CW + 12 * k + 4 * c4 + 4].unsqueeze(2).broadcast_to([P, 4, NB])
                    link(TT(tmp if k else xs, raws[:, 4 * c4:4 * c4 + 4, k, :], w, ALU.mult))
                    if k:
                        ins = TT(xs, xs, tmp, ALU.add)
                        if k < 3:
                            link(ins)
                        else:
                            ins.then_inc(S("conv_ready"), 1)
            tail = conv_tail.rearrange("p (c t) -> p c t", c=CC)
            v.tensor_copy(tail[:, :, 0:3], raw[:, :, TP:TP + 3])
            v.tensor_copy(tail[:, :, 3:11], raws[:, :, 3, :]).then_inc(S("tail_ready"), 1)
            b = tile(n_of("dt"))
            x_, p_, e_, z_, z2_ = dtr[2], dtr[4], dtr[3], dtr[5], dtr[6]
            v.tensor_scalar(x_, b[0:16, 0:T], dtb, None, ALU.add).then_inc(empty["v"], 1)
            dve.wait_ge(empty["v"], emptied(n_of("dt"))[1])
            link(TS(e_, x_, -1.0, None, ALU.mult))
            TT(e_, e_, x_, ALU.max).then_inc(S("dt_abs_ready"), 1)
            dve.wait_ge(S("dt_exp_ready"), 1)
            link(TS(z_, e_, 2.0, None, ALU.add))
            link(v.reciprocal(z_, z_))
            link(TT(z_, z_, e_, ALU.mult))
            link(TT(z2_, z_, z_, ALU.mult))
            link(TS(p_, z2_, 1.0 / 17, None, ALU.mult))
            for k in range(7, 0, -1):
                link(STT(out=p_, in0=p_, scalar=1.0 / (2 * k + 1), in1=z2_, op0=ALU.add, op1=ALU.mult))
            link(STT(out=p_, in0=p_, scalar=1.0, in1=z_, op0=ALU.add, op1=ALU.mult))
            link(TS(x_, x_, 0.0, None, ALU.max))
            link(STT(out=dtr[0], in0=p_, scalar=2.0, in1=x_, op0=ALU.mult, op1=ALU.add))
            dve.wait_ge(S("aexp_ready"), 1)
            TS(dtr[1], dtr[0], aexp, -1.0, ALU.mult, ALU.mult).then_inc(S("dt_done"), 1)
            dve.wait_ge(S("dt_tm_done"), 1)
            v.tensor_copy(small[:, 64:128], ps[:, 5, 0:64]).then_inc(S("dt_tm_ready"), 1)
            link(v.tensor_copy(exc.rearrange("p c k -> p (c k)"), ps[:, 5, 128:256]))
            dve.wait_ge(S("xbc_ready"), CC)
            TT(exc[:, :, 8:16], exc[:, :, 8:16], XBC[:, 0:DC, TP:T], ALU.mult).then_inc(S("exc_ready"), 1)
            b = tile(n_of("vmean"))
            for c in range(DC):
                last = STT(out=V[:, c, :], in0=b[:, 0:T], scalar=-1.0 / D, in1=V[:, c, :], op0=ALU.mult, op1=ALU.add)
            last.then_inc(empty["v"], 1)
            dve.wait_ge(S("cs_done"), 1)
            v.tensor_copy(small[:, 128:160], ps[:, 6, 0:32])
            link(v.tensor_copy(small[:, 192:224], ps[:, 6, 32:64]))
            TT(small[:, 160:192], small[:, 192:224], small[:, 128:160], ALU.subtract).then_inc(S("dec_in"), 1)
            dve.wait_ge(S("dec_ready"), 1)
            link(TT(wdec, wdec, dd[:, :, 0, :], ALU.mult))

            def weigh(j):
                TT(xw.rearrange("p (h n) -> p h n", h=16), x_tm[:, j, :].rearrange("p (h n) -> p h n", h=16),
                   wdec[:, j, :].unsqueeze(2).broadcast_to([P, 16, 64]), ALU.mult).then_inc(S("xw_ready"), 1)

            def lmat(i):
                j, hq = i // 4, i % 4
                b = tile(n_csb(i))
                if i >= 2:
                    dve.wait_ge(S("y_ssd_done"), i - 1)
                if i >= 4:
                    dve.wait_ge(S("ecs_ready"), i - 3)
                for h in range(4):
                    last = STT(out=Lm[i % 2][:, h * P:(h + 1) * P], in0=b[:, h * P:(h + 1) * P],
                               scalar=cs[:, j, 4 * hq + h:4 * hq + h + 1], in1=mneg, op0=ALU.subtract, op1=ALU.add)
                last.then_inc(empty["v"], 1)
                dve.wait_ge(empty["v"], emptied(n_csb(i))[1])
                v.sem_inc(S("ldiff_ready"), 1)
                if i >= 4:
                    TT(split(Ce[i % 2], 4), split(ecs, 4), XBC[:, 10 + hq // 2, j * P:(j + 1) * P].unsqueeze(1).broadcast_to([P, 4, P]),
                       ALU.mult).then_inc(S("ce_ready"), 1)
                dve.wait_ge(S("lexp_ready"), i + 1)
                for h in range(4):
                    last = STT(out=Lm[i % 2][:, h * P:(h + 1) * P], in0=Lm[i % 2][:, h * P:(h + 1) * P],
                               scalar=dd[:, j, 0, 4 * hq + h:4 * hq + h + 1], in1=CBT[:, 2 * j + hq // 2, :],
                               op0=ALU.mult, op1=ALU.mult)
                last.then_inc(S("lmat_ready"), 1)

            def y_out(i):
                j, hq = i // 4, i % 4
                dve.wait_ge(S("y_ssd_done"), i + 1)
                for c2 in range(2):
                    c = 2 * hq + c2
                    last = STT(out=XBC[:, c, j * P:(j + 1) * P], in0=XBC[:, c, j * P:(j + 1) * P], scalar=dcol[:, c:c + 1],
                               in1=ps[:, 5 + 2 * (i % 2), c2 * P:(c2 + 1) * P], op0=ALU.mult, op1=ALU.add)
                last.then_inc(S("y_ssd_used"), 1)

            dve.wait_ge(empty["a"], emptied(n_of("cb"))[1])
            weigh(0)
            lmat(0), lmat(1)
            for i in range(4):
                y_out(i)
                lmat(i + 2)
            for g in range(2):
                b = tile(n_of("stA", g))
                v.tensor_copy(prev[:, g * 512:(g + 1) * 512], b).then_inc(empty["v"], 1)
            weigh(1)
            dve.wait_ge(empty["v"], emptied(n_of("stA", 1))[1])
            link(TT(sfin.rearrange("p (h n) -> p h n", h=16), prev.rearrange("p (h n) -> p h n", h=16),
                    cdec[:, 1, :].unsqueeze(2).broadcast_to([P, 16, 64]), ALU.mult))
            for g in range(2):
                b = tile(n_of("stA", 2 + g))
                TT(sfin[:, g * 512:(g + 1) * 512], sfin[:, g * 512:(g + 1) * 512], b, ALU.add).then_inc(empty["v"], 1)
            for i in range(4, 8):
                y_out(i)
                if i < 6:
                    lmat(i + 2)
            def sample_state(b_):
                dve.wait_ge(S("bc_spread"), b_ + 1)
                b = ps[:, 4 + 2 * (b_ % 2), :]
                if b_:
                    dve.wait_ge(S("s0_used"), b_)
                for g in range(2):
                    last = TT(t2[:, 4 * g:4 * g + 4, :], b[:, g * P:(g + 1) * P].unsqueeze(1).broadcast_to([P, 4, P]),
                              exc[:, 4 * g:4 * g + 4, 8 + b_:9 + b_].broadcast_to([P, 4, P]), ALU.mult)
                link(last)
                dve.wait_ge(S("s0_decayed"), b_ + 1)
                TT(s0[b_ % 4], s0[b_ % 4], t2, ALU.add).then_inc(S("s0_summed"), 1)
                dve.wait_ge(S("s0_summed"), b_ + 1)
                for g in range(2):
                    last = TT(t2[:, 4 * g:4 * g + 4, :], s0[b_ % 4][:, 4 * g:4 * g + 4, :],
                              b[:, 256 + g * P:256 + (g + 1) * P].unsqueeze(1).broadcast_to([P, 4, P]), ALU.mult)
                last.then_inc(S("bc_used"), 1)
                dve.wait_ge(S("bc_used"), b_ + 1)
                v.tensor_reduce(ysum[:, :, b_], t2, X, ALU.add).then_inc(S("s0_used"), 1)

            for b_ in range(6):
                sample_state(b_)
            dve.wait_ge(S("v_root"), 1)
            link(v.reciprocal(rs, rs))
            for c in range(DC):
                STT(out=V[:, c, :], in0=V[:, c, :], scalar=par[:, LNG + c:LNG + c + 1], in1=rs, op0=ALU.mult, op1=ALU.mult) \
                    .then_inc(S("v_scaled"), 1)
            for i in range(2):
                b = tile(n_of("wsT", i))
                TT(wsT[:, 4 * i:4 * i + 4, :], split(b, 4), triu.unsqueeze(1).broadcast_to([P, 4, P]), ALU.mult) \
                    .then_inc(empty["v"], 1)
            for b_ in range(6, NB):
                sample_state(b_)
            dve.wait_ge(S("wb_done"), 1)
            v.tensor_copy(wb[:, 0:8], ps[:, 7, 128:136])
            link(v.tensor_copy(wb[:, 8:16], ps[:, 5, 136:144]))
            dve.wait_ge(S("v_normed"), DC)
            tmp = t2[:, 0, 0:64].rearrange("p (c b) -> p c b", c=DC)
            dve.wait_ge(S("s0_used"), NB)
            link(TT(tmp, V[:, :, TP:T], wb[:, 0:8].unsqueeze(2).broadcast_to([P, DC, NB]), ALU.mult))
            link(TT(tmp, tmp, wb[:, 8:16].unsqueeze(2).broadcast_to([P, DC, NB]), ALU.add))
            dve.wait_ge(empty["a"], emptied(n_of("u", 7))[1])
            TT(U[:, :, TP:T], U[:, :, TP:T], tmp, ALU.mult)
            for h in range(8):
                b = tile(n_of("mixA", h))
                TT(U[:, h, 0:TP], U[:, h, 0:TP], b[:, 0:TP], ALU.mult).then_inc(empty["v"], 1)
            dve.wait_ge(empty["v"], emptied(n_of("mixA", 7))[1])
            v.sem_inc(S("ya_ready"), 1)
            dve.wait_ge(S("s0_used"), NB)
            xs = XBC[:, 0:DC, TP:T]
            link(TT(xs, xs, dcol.unsqueeze(2).broadcast_to([P, DC, NB]), ALU.mult))
            link(TT(xs, xs, ysum, ALU.add))
            TT(Z, Z, XBC[:, 0:DC, :], ALU.mult).then_inc(S("yz_ready"), 1)
            dve.wait_ge(S("gate_root"), 2)
            link(v.reciprocal(rsg, rsg))
            for c in range(DC):
                STT(out=Z[:, c, :], in0=Z[:, c, :], scalar=par[:, BN + c:BN + c + 1], in1=rsg[:, c // 4, :],
                    op0=ALU.mult, op1=ALU.mult).then_inc(S("yb_ready"), 1)

            dve.wait_ge(S("mem_root"), 1)
            v.reciprocal(mrs[:, 0:2], mrs[:, 2:4]).then_inc(S("mem_rs_ready"), 1)

            def attention(l, k_post, k_pre):
                finish_norm(k_post)
                first_lo(f"q{l}")
                finish_norm(k_pre)
                lo_through(f"q{l}", 7)
                for i in range(16):
                    b_, half = i // 2, i % 2
                    dve.wait_ge(S("q_spread"), 16 * l + i + 1)
                    b = ps[:, 5 + i % 2, :]
                    if half == 0:
                        dve.wait_ge(S(f"k_cache_loaded{b_ % 2}"), 16 * (4 * l + b_ // 2 + 1))
                    for m in range(2):
                        for h in range(2):
                            col = (2 * half + h) * NB + b_
                            ins = v.tensor_tensor_reduce(out=junk, in0=kc[b_ % 2][:, m, (2 * half + h) * 256:(2 * half + h + 1) * 256],
                                                         in1=b[:, h * 256:(h + 1) * 256], scale=1.0, scalar=0.0, op0=ALU.mult,
                                                         op1=ALU.add, accum_out=scs[:, m, col:col + 1])
                            link(ins) if not (m and h) else None
                    ins.then_inc(S("q_spread_used"), 1)
                    dve.wait_ge(S("q_spread_used"), 16 * l + i + 1)
                    if half:
                        v.sem_inc(S("k_cache_used"), 1)
                b = tile(n_of(f"sT{l}"))
                link(v.tensor_reduce(smx, b[0:32, 0:256], X, ALU.max))
                TS(smx, smx, -1.0, None, ALU.mult).then_inc(S("sample_max"), 1)
                dve.wait_ge(empty["a"], emptied(n_of(f"sT{l}"))[1])
                link(v.reciprocal(ssm, ssm))
                TS(p_s, p_s, ssm, None, ALU.mult).then_inc(S("sample_probs"), 1)
                for i in range(5):
                    if i == 2:
                        b = tile(n_of(f"pTs{l}"))
                        dve.wait_ge(S("pts_zeroed"), l + 1)
                        v.tensor_copy(pts.rearrange("p k b n -> p k (b n)")[:, :, 0:64:9], split(b[:, 0:64], 2 * XH)) \
                            .then_inc(empty["v"], 1)
                    if i < 4:
                        b = tile(n_sc(l, i))
                        link(v.tensor_reduce(mx[:, 2 * i:2 * i + 2], b.rearrange("p (h m) -> p h m", h=2), X, ALU.max))
                        TS(mx[:, 2 * i:2 * i + 2], mx[:, 2 * i:2 * i + 2], -1.0, None, ALU.mult).then_inc(S("max_ready"), 1)
                    if i:
                        g, hp = (i - 1) // 2, (i - 1) % 2
                        dve.wait_ge(empty["a"], emptied(n_sc(l, i - 1))[1])
                        link(v.reciprocal(sm[:, 2 * i - 2:2 * i], sm[:, 2 * i - 2:2 * i]))
                        TT(PR[:, g, 2 * hp:2 * hp + 2, :], PR[:, g, 2 * hp:2 * hp + 2, :],
                           sm[:, 2 * i - 2:2 * i].unsqueeze(2).broadcast_to([P, 2, MEM]), ALU.mult).then_inc(S("probs_ready"), 1)
                dve.wait_ge(S("v_cache_used"), NB * (l + 1))
                v.tensor_copy(o_tm, ps[0:NB, 4:8, 0:256]).then_inc(S("o_rows"), 1)
                dve.wait_ge(S("o_turned"), 2 * l + 1)
                v.tensor_copy(OT[:, :, TP:T], split(ps[:, 7, 0:64], DC)).then_inc(S("o_samples"), 1)
                finish_norm(k_pre + 1)
                if l == 0:
                    first_lo("gate0")
                finish_norm(k_pre + 2)

            attention(0, 1, 2)
            for i in range(FC):
                copied(n_of(f"gate{i // 4}", i % 4))
                b = tile(n_of(f"up{i // 4}", i % 4))
                TT(hid[:, i, :], b[:, 0:T], gtmp[i % 4], ALU.mult).then_inc(empty["v"], 1)
            finish_norm(5)
            first_lo("f")
            finish_norm(6)
            copied(n_of("f", 7))
            for c in range(DC):
                last = TS(Fg[:, c, :], Fg[:, c, :], omlb[:, c:c + 1], lb1[:, c:c + 1], ALU.mult, ALU.add)
            link(last)
            TS(K, Fg, -1.0, 1.0, ALU.mult, ALU.add).then_inc(S("fg_ready"), 1)
            lo_through("q", 7, 2)
            dve.wait_ge(S("logf_ready"), 1)
            dve.wait_ge(S("hgrn_consts"), 1)
            v.tensor_copy(q_one.rearrange("p h b n -> p h (b n)")[:, :, 0:64:9], Q[:, :, TP:T])
            flat = "p c t -> p (c t)"
            v.tensor_tensor_scan(BC.rearrange(flat), cmask.rearrange(flat), Fg.rearrange(flat), 0.0, ALU.mult, ALU.add) \
                .then_inc(S("bc_ready"), 1)
            pr = (slice(None), slice(None), slice(0, TP))
            lo_through("i", 7, 3)
            dve.wait_ge(S("e_ready"), 1)
            TT(Q[pr], Q[pr], E[pr], ALU.mult).then_inc(S("e_used"), 1)
            make_lo([lo_count[0]])
            dve.wait_ge(S("e_ready"), 2)
            link(TT(Fg[pr], K[pr], E[pr], ALU.mult))
            make_lo([lo_count[0]])
            for c in range(DC):
                last = TT(E[:, c, 0:TP].rearrange("p (k t) -> p k t", k=4),
                          BC[:, c, 63:TP:64].unsqueeze(2).broadcast_to([P, 4, 64]),
                          BC[:, c, 0:TP].rearrange("p (k t) -> p k t", k=4), ALU.subtract)
            last.then_inc(S("e_used"), 1)
            dve.wait_ge(S("e_ready"), 3)
            TT(K[pr], K[pr], E[pr], ALU.mult).then_inc(S("k_decayed"), 1)
            lo_through("g", 7)
            for hq in range(2):
                b = tile(n_of("att", hq)).rearrange("p (h j t) -> p h j t", h=4, j=2)
                for q in range(2):
                    rows = slice(64 * q, 64 * q + 64)
                    last = v.copy_predicated(att[rows, 4 * hq:4 * hq + 4, :, 64 * q:64 * q + 64],
                                             triu[rows, 64 * q:64 * q + 64].bitcast(U32).unsqueeze(1).unsqueeze(1)
                                             .broadcast_to([64, 4, 2, 64]), b[rows, :, :, :])
                last.then_inc(empty["v"], 1)
            for ch in range(4):
                for half in range(2):
                    b = tile(n_of("upd", 2 * ch + half))
                    if ch:
                        dve.wait_ge(empty["v"], emptied(n_of("upd", 2 * ch - 2 + half))[1])
                    for c in range(4):
                        h = 4 * half + c
                        if ch:
                            last = STT(out=st[ch][:, h, :], in0=st[ch - 1][:, h, :], scalar=etot[:, h, ch:ch + 1],
                                       in1=b[:, c * P:(c + 1) * P], op0=ALU.mult, op1=ALU.add)
                        else:
                            last = v.tensor_copy(st[0][:, h, :], b[:, c * P:(c + 1) * P])
                    last.then_inc(empty["v"], 1)
            dve.wait_ge(empty["v"], emptied(n_of("upd", 7))[1])
            v.sem_inc(S("s4_ready"), 1)
            for b_ in range(NB):
                for half in range(2):
                    b = tile(n_of("vB", 2 * b_ + half))
                    dve.wait_ge(S("h0_decayed"), b_ + 1)
                    for c in range(4):
                        h = 4 * half + c
                        last = STT(out=st[b_ % 4][:, h, :], in0=b[:, c * P:(c + 1) * P], scalar=K[:, h, TP + b_:TP + b_ + 1],
                                   in1=st[b_ % 4][:, h, :], op0=ALU.mult, op1=ALU.add)
                    last.then_inc(empty["v"], 1)
                dve.wait_ge(empty["v"], emptied(n_of("vB", 2 * b_ + 1))[1])
                v.sem_inc(S("h_updated"), 1)
                h = b_
                dve.wait_ge(empty["a"], emptied(n_of("hn", h))[1])
                link(v.reciprocal(BC[:, h, 0:TP], BC[:, h, 0:TP]))
                link(STT(out=E[:, h, 0:TP], in0=E[:, h, 0:TP], scalar=par[:, CN + h:CN + h + 1], in1=BC[:, h, 0:TP],
                         op0=ALU.mult, op1=ALU.mult))
                TT(E[:, h, 0:TP], E[:, h, 0:TP], G[:, h, 0:TP], ALU.mult)
            dve.wait_ge(S("hgrn_read"), NB)
            v.tensor_copy(i_s, ps[0:NB, 5:7, :].rearrange("p k n -> p (k n)")).then_inc(S("o_rows"), 1)
            dve.wait_ge(S("o_turned"), 2)
            es_, gs_ = E[:, :, TP:T], G[:, :, TP:T]
            v.tensor_copy(es_, split(ps[:, 7, 64:128], DC)).then_inc(S("ho_samples"), 1)
            dve.wait_ge(S("ho_samples"), 1)
            link(TT(gs_, gs_, par[:, CN:CN + DC].unsqueeze(2).broadcast_to([P, DC, NB]), ALU.mult))
            TT(gs_, gs_, es_, ALU.mult).then_inc(S("gated_samples"), 1)
            dve.wait_ge(empty["a"], emptied(n_of("hns"))[1])
            link(v.reciprocal(BC[:, :, TP:T], BC[:, :, TP:T]))
            dve.wait_ge(S("gated_samples"), 1)
            TT(es_, gs_, BC[:, :, TP:T], ALU.mult).then_inc(S("ho_ready"), 1)
            attention(1, 7, 8)
            b = tile(n_of("logit"))
            dve.wait_ge(empty["a"], emptied(n_of("htok", 5))[1])
            link(v.memset(rtf[:, 0:640], 0.0))
            for g, (t0, nt) in enumerate(GROUPS):
                last = v.tensor_copy(lg[0:nt, g, :], b[0:nt, 8 * g:8 * g + 8])
            last.then_inc(empty["v"], 1)
            dve.wait_ge(empty["v"], emptied(n_of("logit"))[1])
            for g in range(3):
                last = v.max(top[:, g, :], lg[:, g, :])
            link(last)
            for g in range(3):
                v.max_index(topi[:, g, :], top[:, g, :], lg[:, g, :])
            link(TT(tw[:, :, 0], top[:, :, 1], top[:, :, 0], ALU.subtract))
            v.tensor_copy(topf, topi).then_inc(S("top_diff"), 1)
            dve.wait_ge(S("top_diff"), 1)
            for g in range(3):
                for q in range(2):
                    last = TS(oh[:, 2 * g + q, :], iota[:, 0:8], topf[:, g, q:q + 1], None, ALU.is_equal)
            link(last)
            TT(msk, oh[:, 0:6:2, :], oh[:, 1:6:2, :], ALU.add).then_inc(S("mask_ready"), 1)
            dve.wait_ge(S("top_exp"), 1)
            link(TS(tw[:, :, 2], tw[:, :, 1], 1.0, None, ALU.add))
            link(v.reciprocal(tw[:, :, 3], tw[:, :, 2]))
            link(TT(tw[:, :, 0], tw[:, :, 3], tw[:, :, 1], ALU.mult))
            for g in range(3):
                last = TS(gat[:, g, :], oh[:, 2 * g, :], tw[:, g, 3:4], None, ALU.mult)
            link(last)
            for g in range(3):
                last = STT(out=gat[:, g, :], in0=oh[:, 2 * g + 1, :], scalar=tw[:, g, 0:1], in1=gat[:, g, :],
                           op0=ALU.mult, op1=ALU.add)
            link(last)
            b = tile(n_of("posn"))
            v.tensor_copy(table[:, 0:NE, 0:3], split(b[:, 0:24], 3).rearrange("p g e -> p e g"))
            v.tensor_copy(table[:, 0:NE, 3:6], msk.rearrange("p g e -> p e g"))
            v.tensor_copy(table[:, 0:NE, 6:9], gat.rearrange("p g e -> p e g"))
            v.tensor_reduce(cmx[:, 0:1], b[:, 24:32], X, ALU.max).then_inc(empty["v"], 1)
            dve.wait_ge(empty["v"], emptied(n_of("posn"))[1])
            link(TS(cmx[:, 1:2], cmx[:, 0:1], float(P), 1.0, ALU.is_gt, ALU.add))
            link(TS(cmx[:, 2:3], cmx[:, 0:1], float(2 * P), None, ALU.is_gt))
            link(TT(rounds, cmx[:, 1:2], cmx[:, 2:3], ALU.add))
            link(TS(cmx[:, 0:1], rounds, float(NE), None, ALU.mult))
            v.tensor_copy(steps_i, cmx[:, 0:1])
            v.tensor_copy(rounds_i, rounds).then_inc(S("rounds_ready"), 1)
            for r in (1, 2):
                TS(table[:, r * NE:(r + 1) * NE, 0:3], table[:, 0:NE, 0:3], -float(r * P), None, ALU.add)
                last = v.tensor_copy(table[:, r * NE:(r + 1) * NE, 3:9], table[:, 0:NE, 3:9])
            link(last)
            v.sem_inc(S("hs_ready"), NSL)
            v.sem_inc(S("lo_made"), 2 * MRING)
            dve.wait_ge(S("rounds_ready"), 1)
            dve.wait_ge(S("experts_may_start"), 1)

            def picks(step, count):
                v.tensor_copy(cur.unsqueeze(1), table[:, bass.ds(step, 1), :]).then_inc(S("cur_ready"), 1)
                dve.wait_ge(S("cur_ready"), count)
                for g in range(3):
                    TS(pickg[:, g, :], iota, cur[:, g:g + 1], cur[:, 6 + g:7 + g], ALU.is_equal, ALU.mult)
                    last = TS(pick[:, g, :], iota, cur[:, g:g + 1], cur[:, 3 + g:4 + g], ALU.is_equal, ALU.mult)
                last.then_inc(S("pick_ready"), 1)

            def tokens_lo(made_hi):
                for half in range(2):
                    cols = slice(half * 512, (half + 1) * 512)
                    dve.wait_ge(S("xe_hi_made"), made_hi + half + 1)
                    last = TT(xe_lo[:, cols], ps[:, 2 + half, :], xe_hi[:, cols].bitcast(F32), ALU.subtract)
                last.then_inc(S("xe_ready"), 1)

            def add_rows(i, before):
                g, half = i // 2, i % 2
                nt = GROUPS[g][1]
                dve.wait_ge(S("scatter_done"), before + i + 1)
                sl = acc[0:nt, g, half * 512:(half + 1) * 512]
                TT(sl, sl, ps[0:nt, 7 - i % 2, :], ALU.add).then_inc(S("acc_added"), 1)

            picks(0, 1)
            tokens_lo(0)
            steps_v = nc.values_load(steps_i[0:1, 0:1], engines=[mybir.EngineType.DVE], min_val=NE, max_val=3 * NE)
            with dve.Fori(0, steps_v) as it_:
                it = dve.snap(it_)
                nxt = dve.snap(it + 1)
                for q in range(NQ):
                    dve.wait_ge(S("hi_made"), it * NQ + q + 1)
                    TT(wr_[:, q % QRING, 1, :], quarter(q), wr_[:, q % QRING, 0, :].bitcast(F32), ALU.subtract) \
                        .then_inc(S("lo_made"), 1)
                    if q - QRING in SCATTER:
                        add_rows(SCATTER.index(q - QRING), it * 6)
                    if q - QRING == TURN_PLACES + 1:
                        dve.wait_ge(S("pickT_done"), it + 1)
                        picks(nxt, it + 2)
                    kind, s, i = QUARTERS[q - QRING] if q >= QRING else ("", 0, 0)
                    if kind == "up" and i == 3:
                        dve.wait_ge(S("quarter_used"), it * NQ + q + 1)
                        dve.wait_ge(S("silu_done"), it * NSL + s + 1)
                        TT(hs[s % 2], sg[s % 2], ps[:, 2 * (s % 2) + 1, :], ALU.mult).then_inc(S("hs_ready"), 1)
                    if q - QRING == GATHER:
                        tokens_lo(it * 2 + 2)
                    if q - QRING in TURN:
                        s = TURN[q - QRING]
                        dve.wait_ge(S("hT_hi_made"), it * NSL + s + 1)
                        TT(hT_lo[s % 2], ps[:, 6, :], hT_hi[s % 2].bitcast(F32), ALU.subtract).then_inc(S("hT_ready"), 1)
            for i in range(6):
                add_rows(i, steps_v * 6)
            dve.wait_ge(S("acc_added"), steps_v * 6 + 6)
            v.sem_inc(S("experts_done"), 1)
            dve.wait_ge(S("gb_loaded"), 16)
            for g, (t0, nt) in enumerate(GROUPS):
                dve.wait_ge(S("y_root"), g + 1)
                link(v.reciprocal(frs[0:nt, g:g + 1], frs[0:nt, 3 + g:4 + g]))
                link(STT(out=acc[0:nt, g, :], in0=acc[0:nt, g, :], scalar=frs[0:nt, g:g + 1], in1=gb[0:nt, :],
                         op0=ALU.mult, op1=ALU.mult))
                dve.wait_ge(S("x_tok_ready"), g + 1)
                TT(acc[0:nt, g, :], acc[0:nt, g, :], x_tok[0:nt, g, :], ALU.add).then_inc(S("y_ready"), 1)


INPUTS = ["x_prompt", "x_sample", "mem_prompt", "cache_mem_k", "cache_mem_v", "state_conv", "state_ssm", "state_hgrn",
          "norm_mix_pre", "norm_mix_post", "norm_x_pre", "norm_x_post", "norm_ffn_pre", "norm_ffn_post", "norm_mem",
          "xa_wq", "xa_wk", "xa_wv", "xa_wo", "ev_w_in", "a_ws", "a_bs", "a_ln_g", "a_ln_b", "b_conv_w", "b_conv_b",
          "b_dt_bias", "b_a_log", "b_d", "b_norm", "ev_w_out", "ffn_w_gate", "ffn_w_up", "ffn_w_down", "od_w_in",
          "hgrn_lb_logits", "c_norm", "od_w_out", "moe_router", "moe_w_gate", "moe_w_up", "moe_w_down"]
OUTPUTS = [("y_prompt", (1, 256, 1024)), ("y_sample", (8, 1, 1024)), ("mem_k", (2, 1, 256, 4, 256)),
           ("mem_v", (2, 1, 256, 4, 256)), ("conv_prompt", (1, 1, 3, 1536)), ("ssm_prompt", (1, 1, 2, 8, 64, 128)),
           ("hgrn_prompt", (1, 1, 8, 128, 128)), ("conv_sample", (1, 8, 3, 1536)),
           ("ssm_sample", (1, 8, 2, 8, 64, 128)), ("hgrn_sample", (1, 8, 8, 128, 128)), ("av_sample", (1, 8, 1, 1024))]


def kernel(**inputs):
    import numpy as np
    import concourse.bacc as bacc
    from concourse.bass_utils import run_bass_kernel_spmd

    nc = bacc.Bacc("TRN2", target_bir_lowering=False, num_devices=1)
    arrays, a, o = {}, {}, {}
    for name in INPUTS:
        x = np.ascontiguousarray(inputs[name])
        arrays[f"in_{name}"] = x
        a[name] = nc.dram_tensor(f"in_{name}", x.shape, mybir.dt.from_np(x.dtype), kind="ExternalInput").ap()
    for name, shape in OUTPUTS:
        o[name] = nc.dram_tensor(f"out_{name}", shape, F32, kind="ExternalOutput").ap()
    program(nc, a, o)
    r = run_bass_kernel_spmd(nc, [arrays], core_ids=[0])
    return tuple(r.results[0][f"out_{name}"] for name, _ in OUTPUTS)
```
